# Optimizing a Trainium2 kernel written in Bass

```python
import jax, jax.numpy as jnp
from jax import lax
import numpy as np
import math

D_MODEL = 1024
BATCH = 1
SEQ = 512
DEPTH = 1

EPS = 1e-6
CONV_WIDTH = D_MODEL
CONV_K = 3
GDN_HEADS = 8
GDN_DK = 128
GDN_DV = 128
GDN_CONV_K = 4
GDN_CHUNK = 64
GDN_QK = GDN_HEADS * GDN_DK
GDN_VW = GDN_HEADS * GDN_DV
D_FF = 256 * ((8 * D_MODEL // 3 + 255) // 256)
FFN_CONV_K = 3
IN_SPLITS = (CONV_WIDTH, CONV_WIDTH, CONV_WIDTH, GDN_QK, GDN_QK, GDN_VW, GDN_VW, GDN_HEADS, GDN_HEADS, D_MODEL, D_MODEL)
IN_WIDTH = sum(IN_SPLITS)


def _split_points():
    pts, acc = [], 0
    for w in IN_SPLITS[:-1]:
        acc += w
        pts.append(acc)
    return pts

def rmsnorm(x, g):
    xf = x.astype(jnp.float32)
    y = xf * lax.rsqrt(jnp.mean(xf * xf, axis=-1, keepdims=True) + EPS)
    return (y * g.astype(jnp.float32)).astype(x.dtype)

def l2norm(x):
    return x * lax.rsqrt(jnp.sum(x * x, axis=-1, keepdims=True) + EPS)

def causal_dwconv(x, w):
    K = w.shape[0]
    S = x.shape[1]
    xp = jnp.pad(x, ((0, 0), (K - 1, 0), (0, 0)))
    return sum(xp[:, j:j + S] * w[j] for j in range(K))

def short_conv_branch(bg, cg, xv, conv_w):
    return bg * causal_dwconv(cg * xv, conv_w)

def gated_delta_rule_chunked(q, k, v, g, beta):
    Bsz, S, H, dk = q.shape
    dv = v.shape[-1]
    C = GDN_CHUNK
    N = S // C

    def chunks(t):
        return t.reshape(Bsz, N, C, H, *t.shape[3:]).swapaxes(2, 3)

    q, k, v, g, beta = (chunks(t) for t in (q, k, v, g, beta))
    G = jnp.cumsum(g, axis=-1)
    tril = jnp.tril(jnp.ones((C, C), dtype=bool))
    strict = jnp.tril(jnp.ones((C, C), dtype=bool), -1)
    decay = jnp.exp(jnp.where(tril, G[..., :, None] - G[..., None, :], -jnp.inf))
    k_beta = k * beta[..., None]
    v_beta = v * beta[..., None]
    L = jnp.where(strict, jnp.einsum('bnhid,bnhjd->bnhij', k_beta, k) * decay, 0.0)
    eye = jnp.eye(C, dtype=q.dtype)
    rhs = jnp.concatenate([v_beta, k_beta * jnp.exp(G)[..., None]], axis=-1)
    sol = lax.linalg.triangular_solve(eye + L, rhs, left_side=True, lower=True)
    u, w = sol[..., :dv], sol[..., dv:]
    A_qk = jnp.einsum('bnhid,bnhjd->bnhij', q, k) * decay
    q_dec = q * jnp.exp(G)[..., None]
    G_last = G[..., -1:]
    k_dec = k * jnp.exp(G_last - G)[..., None]

    def step(state, inp):
        q_c, k_c, u_c, w_c, A_c, gl = inp
        v_new = u_c - jnp.einsum('bhcd,bhde->bhce', w_c, state)
        o = jnp.einsum('bhcd,bhde->bhce', q_c, state) + jnp.einsum('bhij,bhje->bhie', A_c, v_new)
        state = state * jnp.exp(gl)[..., None] + jnp.einsum('bhcd,bhce->bhde', k_c, v_new)
        return state, o

    xs = tuple(jnp.moveaxis(t, 1, 0) for t in (q_dec, k_dec, u, w, A_qk, G_last))
    state0 = jnp.zeros((Bsz, H, dk, dv), dtype=q.dtype)
    _, o = lax.scan(step, state0, xs)
    return o.transpose(1, 0, 3, 2, 4).reshape(Bsz, S, H, dv)

def gdn_branch(q, k, v, z, a, b, conv_w, A_log, dt_bias, norm_g):
    Bsz, S, _ = q.shape
    dtype = q.dtype
    f32 = jnp.float32
    qkv = jax.nn.silu(causal_dwconv(jnp.concatenate([q, k, v], axis=-1), conv_w))
    q, k, v = jnp.split(qkv, [GDN_QK, 2 * GDN_QK], axis=-1)
    q = l2norm(q.reshape(Bsz, S, GDN_HEADS, GDN_DK).astype(f32)) * (GDN_DK ** -0.5)
    k = l2norm(k.reshape(Bsz, S, GDN_HEADS, GDN_DK).astype(f32))
    v = v.reshape(Bsz, S, GDN_HEADS, GDN_DV).astype(f32)
    beta = jax.nn.sigmoid(b.astype(f32))
    g = -jnp.exp(A_log.astype(f32)) * jax.nn.softplus(a.astype(f32) + dt_bias.astype(f32))
    o = gated_delta_rule_chunked(q, k, v, g, beta)
    o = o * lax.rsqrt(jnp.mean(o * o, axis=-1, keepdims=True) + EPS) * norm_g.astype(f32)
    o = o * jax.nn.silu(z.reshape(Bsz, S, GDN_HEADS, GDN_DV).astype(f32))
    return o.reshape(Bsz, S, GDN_VW).astype(dtype)

def conv_ffn(h, w_up, conv_w, w_down):
    up = causal_dwconv(h @ w_up, conv_w)
    gate, val = jnp.split(up, [D_FF], axis=-1)
    return (jax.nn.silu(gate) * val) @ w_down

def first_inputs(seed: int = 0) -> dict:
    key = jax.random.key(seed)
    ks = jax.random.split(key, 16)
    f32 = jnp.float32
    nrm = lambda k, shape, scale: jax.random.normal(k, shape, f32) * scale
    x = jax.random.normal(ks[0], (BATCH, SEQ, D_MODEL), f32)
    norm_mix_g = 1.0 + nrm(ks[1], (DEPTH, D_MODEL), 0.02)
    w_in = nrm(ks[2], (DEPTH, D_MODEL, IN_WIDTH), D_MODEL ** -0.5)
    conv_a_w = nrm(ks[3], (DEPTH, CONV_K, CONV_WIDTH), CONV_K ** -0.5)
    gdn_conv_w = nrm(ks[4], (DEPTH, GDN_CONV_K, 2 * GDN_QK + GDN_VW), GDN_CONV_K ** -0.5)
    gdn_A_log = jnp.log(jax.random.uniform(ks[5], (DEPTH, GDN_HEADS), f32, 1.0, 16.0))
    dt = jnp.exp(jax.random.uniform(ks[6], (DEPTH, GDN_HEADS), f32, np.log(1e-3), np.log(1e-1)))
    gdn_dt_bias = dt + jnp.log(-jnp.expm1(-dt))
    gdn_norm_g = 1.0 + nrm(ks[7], (DEPTH, GDN_DV), 0.02)
    w_a_out = nrm(ks[8], (DEPTH, CONV_WIDTH, D_MODEL), CONV_WIDTH ** -0.5)
    w_b_out = nrm(ks[9], (DEPTH, GDN_VW, D_MODEL), GDN_VW ** -0.5)
    w_o = nrm(ks[10], (DEPTH, D_MODEL, D_MODEL), D_MODEL ** -0.5)
    norm_ffn_g = 1.0 + nrm(ks[11], (DEPTH, D_MODEL), 0.02)
    w_up = nrm(ks[12], (DEPTH, D_MODEL, 2 * D_FF), D_MODEL ** -0.5)
    ffn_conv_w = nrm(ks[13], (DEPTH, FFN_CONV_K, 2 * D_FF), FFN_CONV_K ** -0.5)
    w_down = nrm(ks[14], (DEPTH, D_FF, D_MODEL), D_FF ** -0.5)
    norm_final_g = 1.0 + nrm(ks[15], (D_MODEL,), 0.02)
    return {"x": x, "norm_mix_g": norm_mix_g, "w_in": w_in, "conv_a_w": conv_a_w,
            "gdn_conv_w": gdn_conv_w, "gdn_A_log": gdn_A_log, "gdn_dt_bias": gdn_dt_bias,
            "gdn_norm_g": gdn_norm_g, "w_a_out": w_a_out, "w_b_out": w_b_out, "w_o": w_o,
            "norm_ffn_g": norm_ffn_g, "w_up": w_up, "ffn_conv_w": ffn_conv_w, "w_down": w_down,
            "norm_final_g": norm_final_g}

def first_block(x, norm_mix_g, w_in, conv_a_w, gdn_conv_w, gdn_A_log, gdn_dt_bias, gdn_norm_g,
              w_a_out, w_b_out, w_o, norm_ffn_g, w_up, ffn_conv_w, w_down, norm_final_g):
    pts = _split_points()
    for l in range(DEPTH):
        h = rmsnorm(x, norm_mix_g[l])
        proj = h @ w_in[l]
        bg, cg, xv, q, k, v, z, a, b, ga, gb = jnp.split(proj, pts, axis=-1)
        y_a = short_conv_branch(bg, cg, xv, conv_a_w[l]) @ w_a_out[l]
        y_b = gdn_branch(q, k, v, z, a, b, gdn_conv_w[l], gdn_A_log[l], gdn_dt_bias[l],
                         gdn_norm_g[l]) @ w_b_out[l]
        mix = jax.nn.sigmoid(ga) * y_a + jax.nn.sigmoid(gb) * y_b
        x = x + mix @ w_o[l]
        h = rmsnorm(x, norm_ffn_g[l])
        x = x + conv_ffn(h, w_up[l], ffn_conv_w[l], w_down[l])
    return rmsnorm(x, norm_final_g)


CHUNK = 64
HEAD_DIM = 64
POOL_WINDOWS = (2, 4, 8, 16)
POOL_WIDTH = D_MODEL // 4
POOL_GROUP = POOL_WIDTH // len(POOL_WINDOWS)
DSA_WIDTH = 3 * D_MODEL // 8
DSA_HEADS = DSA_WIDTH // HEAD_DIM
FOX_WIDTH = 3 * D_MODEL // 8
FOX_HEADS = FOX_WIDTH // HEAD_DIM
MIX_WIDTH = POOL_WIDTH + DSA_WIDTH + FOX_WIDTH
IDX_HEADS = 8
IDX_DIM = 32
DSA_TOPK_MAX = 256
DSA_QBLOCK = 32
FOX_QBLOCK = 128
RMS_EPS = 1e-6
IN_SIZES = (
    POOL_WIDTH, POOL_WIDTH,
    DSA_WIDTH, DSA_WIDTH, DSA_WIDTH, DSA_WIDTH,
    IDX_HEADS * IDX_DIM, IDX_DIM, IDX_HEADS,
    FOX_WIDTH, FOX_WIDTH, FOX_WIDTH, FOX_WIDTH,
    FOX_HEADS,
)
IN_COLS = 2 * POOL_WIDTH + 4 * DSA_WIDTH + IDX_HEADS * IDX_DIM + IDX_DIM + IDX_HEADS + 4 * FOX_WIDTH + FOX_HEADS


def rmsnorm_2(x, g):
    xf = x.astype(jnp.float32)
    y = xf * lax.rsqrt(jnp.mean(xf * xf, axis=-1, keepdims=True) + RMS_EPS)
    return (y * g.astype(jnp.float32)).astype(x.dtype)

def split_columns(z):
    parts = []
    off = 0
    for n in IN_SIZES:
        parts.append(z[..., off:off + n])
        off += n
    return parts

def pool_mixer(v, w_grp, scale):
    B, L, _ = v.shape
    vf = v.astype(jnp.float32)
    cs = jnp.pad(jnp.cumsum(vf, axis=1), ((0, 0), (1, 0), (0, 0)))
    t = jnp.arange(L)
    outs = []
    for gi, w in enumerate(POOL_WINDOWS):
        sl = slice(gi * POOL_GROUP, (gi + 1) * POOL_GROUP)
        c = cs[:, :, sl]
        lo = jnp.maximum(t + 1 - w, 0)
        win_sum = c[:, t + 1] - c[:, lo]
        cnt = (t + 1 - lo).astype(jnp.float32)[None, :, None]
        outs.append(win_sum / cnt - vf[:, :, sl])
    p = jnp.stack(outs, axis=2).astype(v.dtype)
    y = jnp.einsum('blgc,gcd->blgd', p, w_grp).reshape(B, L, POOL_WIDTH)
    return y * scale

def dsa_mixer(q, k, v, iq, ik, iw, topk):
    B, L, H, dh = q.shape
    n_blocks = L // DSA_QBLOCK
    key_pos = jnp.arange(L)
    sm_scale = 1.0 / math.sqrt(dh)
    gather = jax.vmap(lambda arr, idx: arr[idx])

    def block(bi):
        start = bi * DSA_QBLOCK
        qb = lax.dynamic_slice_in_dim(q, start, DSA_QBLOCK, axis=1)
        iqb = lax.dynamic_slice_in_dim(iq, start, DSA_QBLOCK, axis=1)
        iwb = lax.dynamic_slice_in_dim(iw, start, DSA_QBLOCK, axis=1)
        qpos = start + jnp.arange(DSA_QBLOCK)
        limit = (qpos // CHUNK + 1) * CHUNK
        dots = jnp.einsum('bqhd,bsd->bqhs', iqb, ik).astype(jnp.float32)
        score = jnp.einsum('bqh,bqhs->bqs', iwb.astype(jnp.float32), jax.nn.relu(dots))
        admissible = key_pos[None, None, :] < limit[None, :, None]
        score = jnp.where(admissible, score, -jnp.inf)
        _, sel = lax.top_k(score, topk)
        valid = sel < limit[None, :, None]
        kg = gather(k, sel)
        vg = gather(v, sel)
        s = jnp.einsum('bqhd,bqkhd->bqhk', qb, kg).astype(jnp.float32) * sm_scale
        s = jnp.where(valid[:, :, None, :], s, -jnp.inf)
        p = jax.nn.softmax(s, axis=-1).astype(v.dtype)
        return jnp.einsum('bqhk,bqkhd->bqhd', p, vg)

    o = lax.map(block, jnp.arange(n_blocks))
    return jnp.transpose(o, (1, 0, 2, 3, 4)).reshape(B, L, H, dh)

def fox_mixer(q, k, v, log_f):
    B, L, H, dh = q.shape
    sm_scale = 1.0 / math.sqrt(dh)
    F = jnp.transpose(jnp.cumsum(log_f, axis=1), (0, 2, 1))
    outs = []
    for bi in range(L // FOX_QBLOCK):
        s0 = bi * FOX_QBLOCK
        e = s0 + FOX_QBLOCK
        s = jnp.einsum('bqhd,bkhd->bhqk', q[:, s0:e], k[:, :e]).astype(jnp.float32) * sm_scale
        s = s + F[:, :, s0:e, None] - F[:, :, None, :e]
        mask = jnp.arange(s0, e)[:, None] >= jnp.arange(e)[None, :]
        s = jnp.where(mask[None, None], s, -jnp.inf)
        p = jax.nn.softmax(s, axis=-1).astype(v.dtype)
        outs.append(jnp.einsum('bhqk,bkhd->bqhd', p, v[:, :e]))
    return jnp.concatenate(outs, axis=1)

def second_inputs(seed: int = 0) -> dict:
    key = jax.random.key(seed)
    ks = jax.random.split(key, 9)
    x = jax.random.normal(ks[0], (BATCH, SEQ, D_MODEL), jnp.float32)
    w_in = jax.random.normal(ks[1], (DEPTH, D_MODEL, IN_COLS), jnp.float32) * D_MODEL ** -0.5
    norm_g = 1.0 + 0.02 * jax.random.normal(ks[2], (DEPTH, D_MODEL), jnp.float32)
    pool_w = jax.random.normal(ks[3], (DEPTH, len(POOL_WINDOWS), POOL_GROUP, POOL_GROUP), jnp.float32) * POOL_GROUP ** -0.5
    pool_scale = 1.0 + 0.1 * jax.random.normal(ks[4], (DEPTH, POOL_WIDTH), jnp.float32)
    fox_bf = 3.0 + 0.5 * jax.random.normal(ks[5], (DEPTH, FOX_HEADS), jnp.float32)
    w_out = jax.random.normal(ks[6], (DEPTH, MIX_WIDTH, D_MODEL), jnp.float32) * MIX_WIDTH ** -0.5
    final_g = 1.0 + 0.02 * jax.random.normal(ks[7], (D_MODEL,), jnp.float32)
    return {'x': x, 'w_in': w_in, 'norm_g': norm_g, 'pool_w': pool_w, 'pool_scale': pool_scale,
            'fox_bf': fox_bf, 'w_out': w_out, 'final_g': final_g}

def second_block(x, w_in, norm_g, pool_w, pool_scale, fox_bf, w_out, final_g):
    B, L, _ = x.shape
    topk = min(DSA_TOPK_MAX, L // 4)
    idx_w_scale = IDX_HEADS ** -0.5
    for layer in range(DEPTH):
        h = rmsnorm_2(x, norm_g[layer])
        z = jnp.einsum('bld,dc->blc', h, w_in[layer])
        (pv, pg, dq, dk, dv, dg, iq, ik, iw, fq, fk, fv, fg, ff) = split_columns(z)
        a_out = pool_mixer(pv, pool_w[layer], pool_scale[layer]) * jax.nn.silu(pg)
        b_o = dsa_mixer(dq.reshape(B, L, DSA_HEADS, HEAD_DIM), dk.reshape(B, L, DSA_HEADS, HEAD_DIM),
                        dv.reshape(B, L, DSA_HEADS, HEAD_DIM), iq.reshape(B, L, IDX_HEADS, IDX_DIM),
                        ik, iw * idx_w_scale, topk)
        b_out = b_o.reshape(B, L, DSA_WIDTH) * jax.nn.silu(dg)
        log_f = jax.nn.log_sigmoid(ff.astype(jnp.float32) + fox_bf[layer].astype(jnp.float32))
        c_o = fox_mixer(fq.reshape(B, L, FOX_HEADS, HEAD_DIM), fk.reshape(B, L, FOX_HEADS, HEAD_DIM),
                        fv.reshape(B, L, FOX_HEADS, HEAD_DIM), log_f)
        c_out = c_o.reshape(B, L, FOX_WIDTH) * jax.nn.silu(fg)
        mixed = jnp.concatenate([a_out, b_out, c_out], axis=-1)
        x = x + jnp.einsum('blc,cd->bld', mixed, w_out[layer])
    return rmsnorm_2(x, final_g)


def setup_inputs(seed=0):
    out = dict(first_inputs(seed))
    for name, value in second_inputs(seed + 1).items():
        if name != "x":
            out[name + "_2"] = value
    return out


def reference(
    x, norm_mix_g, w_in, conv_a_w, gdn_conv_w, gdn_A_log, gdn_dt_bias, gdn_norm_g, w_a_out,
    w_b_out, w_o, norm_ffn_g, w_up, ffn_conv_w, w_down, norm_final_g, w_in_2, norm_g_2,
    pool_w_2, pool_scale_2, fox_bf_2, w_out_2, final_g_2,
):
    x = first_block(
        x, norm_mix_g, w_in, conv_a_w, gdn_conv_w, gdn_A_log, gdn_dt_bias, gdn_norm_g, w_a_out,
        w_b_out, w_o, norm_ffn_g, w_up, ffn_conv_w, w_down, norm_final_g,
    )
    return second_block(
        x, w_in_2, norm_g_2, pool_w_2, pool_scale_2, fox_bf_2, w_out_2, final_g_2,
    )


_drawn_inputs = setup_inputs


def setup_inputs(seed=0):
    import zlib

    import numpy as np

    out = dict(_drawn_inputs(seed))
    spreads = {}
    factors = {'gdn_norm_g': 7.622, 'norm_ffn_g': 3.721, 'norm_g_2': 5.373, 'final_g_2': 2.808}
    for name, (base, spread) in spreads.items():
        noise = np.random.default_rng([zlib.crc32(name.encode()), seed]).standard_normal(out[name].shape)
        drawn = base * np.exp(spread * noise) if base else spread * noise
        out[name] = __import__('jax').numpy.asarray(drawn.astype(out[name].dtype))
    for name, factor in factors.items():
        out[name] = (out[name] * factor).astype(out[name].dtype)
    return out
```

```python
from contextlib import ExitStack

import concourse.bass as bass
from concourse import mybir

P = 128
F32 = mybir.dt.float32
F32R = mybir.dt.float32r
ALU = mybir.AluOpType
ACT = mybir.ActivationFunctionType
AX_X = mybir.AxisListType.X
ds = bass.ds

T = 512
TC = T // P
D = 1024
KD = D // P
HEADS = 8
FF = 2816
FB = FF // P
EPS = 1e-6
NEG = -1.0e30

A_BG, A_CG, A_XV, A_Q, A_K, A_V, A_Z = (i * D for i in range(7))
A_AB = 7 * D
A_GA = A_AB + 2 * HEADS
A_GB = A_GA + D

H_HI, H_LO = 0, KD
YA_HI, YA_LO = 2 * KD, 3 * KD
YB_HI, YB_LO = 4 * KD, 5 * KD
MIX_HI, MIX_LO = 2 * KD, 3 * KD
FF_CUT = (12, 10)
FF_HI, FF_LO = 2 * KD, 4 * KD
SLOTS_A = 4 * KD

C_G, C_NEGE, C_E, C_BETA, C_BKD, C_EL = (TC * i for i in range(6))
N_COL = 6 * TC
N_TAP = 3 * 4 + 3

R_MIX_G = 0
R_CONV_A = 8
R_CONV_G = 32
R_FFN_G = 128
R_CONV_F = 136
R_FIN_G = R_CONV_F + 3 * 2 * FB
R_G2 = R_FIN_G + 8
R_PSC = R_G2 + 8
R_GDN_G = R_PSC + 2
R_END = R_GDN_G + 1

PAR_DMAS = 13

HX = 6
GROUPS = HX
IDX_HEADS = 8
TOPK = 128
FILL, TAKEN = -3.0e38, -3.3e38
B_PV, B_PG, B_DQ, B_DK, B_DV, B_DG, B_IQ = 0, 256, 512, 896, 1280, 1664, 2048
B_IK, B_IW, B_FQ, B_FK, B_FV, B_FG, B_FF = 2304, 2336, 2344, 2728, 3112, 3496, 3880
B_END = B_FF + HX
SEL_AT = [P * c * (c + 1) // 2 for c in range(TC + 1)]
Z_UNITS = ([("iwff", 0, 0), ("ik", 0, B_IK), ("iq", 0, B_IQ), ("iq", 1, B_IQ + P)]
           + [(w, g, c + g * P) for g in range(3) for w, c in (("q", B_FQ), ("k", B_FK), ("v", B_FV), ("g", B_FG))]
           + [(w, g + 3, c + g * P) for g in range(3) for w, c in (("q", B_DQ), ("k", B_DK), ("v", B_DV), ("g", B_DG))]
           + [("pv", b, B_PV + b * P) for b in range(2)] + [("pg", b, B_PG + b * P) for b in range(2)])
W_ORDER = (5, 6, 7, 2, 3, 4, 0, 1)


MASKED = -3.0e38


def readers():
    n = {"act": 0, "dve": 0}
    out = []
    for what, _, _ in Z_UNITS:
        who = "dve" if what == "k" else "act"
        n[who] += 1
        out.append((who, n[who]))
    return out


Z_READER = readers()


def reads_of(what):
    return [count for (name, _, _), (_, count) in zip(Z_UNITS, Z_READER) if name == what]


Q_READ, V_READ, G_READ, PV_READ, PG_READ = (reads_of(w) for w in ("q", "v", "g", "pv", "pg"))


def schedule():
    at = {}
    put = lambda u, m, e: at.setdefault((u, m), []).append(e)
    put(1, 1, ("turn_iw",))
    put(2, 1, ("cum_f",))
    put(3, 1, ("turn_f",))
    todo = [(c, h) for c in range(1, TC) for h in range(IDX_HEADS)]
    for n, (c, h) in enumerate(todo):
        put((18 + n // 2) // 4, (18 + n // 2) % 4, ("score", n, c, h))
    rounds = [(r, c) for c in range(1, TC) for r in range(TOPK // 8)]
    for n, (r, c) in enumerate(rounds):
        put((24 + n) // 4, (24 + n) % 4, ("round", r, c))
    todo = {}
    for t in range(2 * GROUPS):
        start = 4 * 7 + 1 + 8 * t
        for c in range(TC):
            todo.setdefault(start + 2 * c + 2, []).append((5, ("weigh", c, t)))
            todo.setdefault(start + 2 * c + 4, []).append((0, ("t", c, t)))
            todo.setdefault(start + 2 * c, []).append((3, ("s", c, t)))
        todo.setdefault(start + 11, []).append((1, ("pv", 0, t)))
        if t % 2 == 0:
            todo.setdefault(start + 2, []).append((2, ("turn_v", t // 2)))
    last = len(Z_UNITS)
    todo.setdefault(4 * last - 4, []).append((4, ("pool", 0)))
    todo.setdefault(4 * last, []).append((4, ("pool", 1)))
    for slot in sorted(todo):
        for _, e in sorted(todo[slot], key=lambda x: x[0]):
            put(slot // 4, slot % 4, e)
    assert max(todo) == 4 * last
    return at


class Steps:

    def __init__(self, eng, sem):
        self.eng, self.sem, self.base, self.n = eng, sem, 0, 0

    def link(self, ins):
        ins.then_inc(self.sem, 1)
        self.n += 1
        self.eng.wait_ge(self.sem, self.base + self.n)

    def enter(self, i, per):
        self.at, self.base, self.n, self.per = self.base + self.n, self.base + self.n + i * per, 0, per

    def leave(self, turns):
        assert self.n == self.per, (self.n, self.per)
        self.base, self.n = self.at + turns * self.per, 0


def hybrid_block_kernel(nc, x, norm_mix_g, w_in, conv_a_w, gdn_conv_w, gdn_A_log, gdn_dt_bias, gdn_norm_g,
                        w_a_out, w_b_out, w_o, norm_ffn_g, w_up, ffn_conv_w, w_down, norm_final_g,
                        w_in_2, norm_g_2, pool_w_2, pool_scale_2, fox_bf_2, w_out_2, final_g_2, out):
    with ExitStack() as ctx:
        def sb(name, shape, dt=F32):
            return ctx.enter_context(nc.sbuf_tensor(name, shape, dt))

        def sem(name):
            return ctx.enter_context(nc.semaphore(name))

        raw = sb("raw", [P, 4, KD * P])
        whi = sb("whi", [P, 2, KD * P], F32R)
        wlo = sb("wlo", [P, 2, KD * P], F32R)
        act_a = sb("act_a", [P, SLOTS_A, T], F32R)
        xT = sb("xT", [P, KD, T])
        gate = sb("gate", [P, KD, T])
        qc = sb("qc", [P, T])
        kc = sb("kc", [P, T])
        vc = sb("vc", [P, T])
        cx = sb("cx", [P, T])
        ca = sb("ca", [P, T])
        zs = sb("zs", [P, T])
        Kt = sb("Kt", [P, TC, P])
        Vt = sb("Vt", [P, TC, P])
        KT = sb("KT", [P, TC, P])
        QT = sb("QT", [P, TC, P])
        dec = sb("dec", [P, TC, P])
        LT = sb("LT", [P, TC, P])
        AT = sb("AT", [P, TC, P])
        Ti = sb("Ti", [P, TC, P])
        Ui = sb("Ui", [P, TC, P])
        Yb = sb("Yb", [P, TC, P])
        S = sb("S", [P, P])
        vn = sb("vn", [P, P])
        vd = sb("vd", [P, P])
        Rr = sb("Rr", [P, P])
        qs = sb("qs", [P, P])
        ident = sb("ident", [P, P])
        ones = sb("ones", [P, P])
        triu = sb("triu", [P, P])
        tril = sb("tril", [P, P])
        negT = sb("negT", [P, P])
        lev = sb("lev", [P, 7, P])
        negm1 = sb("negm1", [P, P])
        par = sb("par", [P, R_END])
        hcols = sb("hcols", [P, HEADS, N_COL])
        htaps = sb("htaps", [P, HEADS, N_TAP])
        hc = sb("hc", [P, N_COL])
        hw = sb("hw", [P, N_TAP])
        sm = sb("sm", [P, 12, 2 * HEADS * TC])
        rows8 = sb("rows8", [P, 2 * HEADS + 6])
        ss = sb("ss", [P, 4, TC])
        rr = sb("rr", [P, 8, TC])
        mhalf = sb("mhalf", [P, 2 * TC])
        eps_one = sb("eps_one", [P, TC])
        eps_head = sb("eps_head", [P, TC])

        small = sb("small", [P, 80])
        guard = nc.sbuf_tensor("act_b", [P, 2 * KD, T], F32R)
        act_b = guard.__enter__()
        guard.__exit__(None, None, None)
        selb = sb("selb", [P, SEL_AT[TC]])
        pT = sb("pT", [P, TC, T])
        cbias = sb("cbias", [P, T])
        vraw = sb("vraw", [P, T])
        pw = sb("pw", [P, 2, P])
        gfin = sb("gfin", [P, D])
        frow = sb("frow", [HX, 2, T])

        wk = sb("wk", [P, D])
        outs = gate[:, 0:4, :].rearrange("p (c a) t -> p c (a t)", c=2)

        def slot(n):
            return act_a[:, n, :] if n < SLOTS_A else act_b[:, n - SLOTS_A, :]

        def flat(t):
            return t[:].rearrange("p c j -> p (c j)")

        def ring(g, what):
            return gate[:, 4 * (g % 2) + what, :]

        vt = (Kt, Vt)
        iq = (flat(KT), flat(QT))
        ikz = (flat(dec), flat(LT), flat(AT), flat(Ti))
        iwff = Ui
        relu = (flat(Yb), zs[:])
        prob = (qc[:], kc[:], flat(Yb), zs[:])
        sg = (vc, cx)
        ot = ca
        pvb = flat(KT)
        wins = ((flat(QT), flat(dec)), (flat(LT), flat(AT)))

        gb = ctx.enter_context(nc.psum_tensor("gb", [P, 4, T], F32))
        gd = ctx.enter_context(nc.psum_tensor("gd", [P, 4, T], F32))

        xin = gate[:].rearrange("p (c a) t -> p c (a t)", c=TC)
        prow = Kt[:].rearrange("p c j -> p (c j)")

        def wide(ap):
            return ap.unsqueeze(2).to_broadcast([P, TC, P])

        def over(ap):
            return ap.unsqueeze(1).to_broadcast([P, TC, P])

        def bank(t):
            return t.rearrange("p (c j) -> p c j", c=TC)

        raw_landed = [sem(f"raw_landed{i}") for i in range(4)]
        hi_ready = sem("hi_ready")
        split_ready = sem("split_ready")
        unit_done = sem("unit_done")
        out_read = sem("out_read")
        x_landed = sem("x_landed")
        par_landed = sem("par_landed")
        prow_clear = sem("prow_clear")
        pool_order = sem("pool_order")
        act_order = sem("act_order")
        dve_order = sem("dve_order")
        masks_ready = sem("masks_ready")
        x_turned = sem("x_turned")
        xT_ready = sem("xT_ready")
        par_turned = sem("par_turned")
        par_ready = sem("par_ready")
        xsq_ready = sem("xsq_ready")
        xsq_used = sem("xsq_used")
        xss_ready = sem("xss_ready")
        xr_ready = sem("xr_ready")
        xrb_ready = sem("xrb_ready")
        xrb_kept = sem("xrb_kept")
        hn_ready = sem("hn_ready")
        hn_hi = sem("hn_hi")
        h_ready = sem("h_ready")
        ab_ready = sem("ab_ready")
        ab_turned = sem("ab_turned")
        abt_ready = sem("abt_ready")
        ab_exp = sem("ab_exp")
        ab_g = sem("ab_g")
        gcum_done = sem("gcum_done")
        gcum_sb = sem("gcum_sb")
        cols_exp = sem("cols_exp")
        taps_ready = sem("taps_ready")
        tap_first = sem("tap_first")
        conv_done = sem("conv_done")
        conv_silu = sem("conv_silu")
        z_ready = sem("z_ready")
        ga_ready = sem("ga_ready")
        cg_ready = sem("cg_ready")
        cg_copied = sem("cg_copied")
        ya_ready = sem("ya_ready")
        ya_hi = sem("ya_hi")
        ya_lo = sem("ya_lo")
        hc_ready = sem("hc_ready")
        kq_turned = sem("kq_turned")
        sq_ready = sem("sq_ready")
        ss_ready = sem("ss_ready")
        r_ready = sem("r_ready")
        gb_done = sem("gb_done")
        arg_ready = sem("arg_ready")
        dec_ready = sem("dec_ready")
        decb_ready = sem("decb_ready")
        tok_ready = sem("tok_ready")
        back_done = sem("back_done")
        kt_ready = sem("kt_ready")
        kk_done = sem("kk_done")
        lt_ready = sem("lt_ready")
        u_ready = sem("u_ready")
        u_turned = sem("u_turned")
        t_first = sem("t_first")
        t_ready = sem("t_ready")
        v_turned = sem("v_turned")
        vtok_ready = sem("vtok_ready")
        y_done = sem("y_done")
        ym_ready = sem("ym_ready")
        z_done = sem("z_done")
        vn_done = sem("vn_done")
        vn_ready = sem("vn_ready")
        vd_ready = sem("vd_ready")
        av_done = sem("av_done")
        su_done = sem("su_done")
        s_ready = sem("s_ready")
        ks_done = sem("ks_done")
        rhs_ready = sem("rhs_ready")
        qs_ready = sem("qs_ready")
        o_ready = sem("o_ready")
        osq_ready = sem("osq_ready")
        oss_ready = sem("oss_ready")
        or_ready = sem("or_ready")
        on_ready = sem("on_ready")
        o_turned = sem("o_turned")
        yb_ready = sem("yb_ready")
        yb_hi = sem("yb_hi")
        yb_lo = sem("yb_lo")
        gb_tanh = sem("gb_tanh")
        mix_ready = sem("mix_ready")
        mix_hi = sem("mix_hi")
        mix_lo = sem("mix_lo")
        xT_norm = sem("xT_norm")
        up_first = sem("up_first")
        up_conv = sem("up_conv")
        up_silu = sem("up_silu")
        up_ready = sem("up_ready")
        up_hi = sem("up_hi")
        up_lo = sem("up_lo")
        iw_extra = sem("iw_extra")
        ik_extra = sem("ik_extra")
        late_landed = sem("late_landed")
        late_clear = sem("late_clear")
        pads_ready = sem("pads_ready")
        z_read = sem("z_read")
        z_read_v = sem("z_read_v")
        iw_turned = sem("iw_turned")
        iw_split = sem("iw_split")
        f_exp = sem("f_exp")
        f_ready = sem("f_ready")
        f_cum = sem("f_cum")
        f_tok = sem("f_tok")
        f_turned = sem("f_turned")
        f_rows = sem("f_rows")
        f_put = [sem(f"f_put{g}") for g in range(3)]
        score_done = sem("score_done")
        relu_ready = sem("relu_ready")
        relu_used = sem("relu_used")
        sel_ready = sem("sel_ready")
        v_turn_done = sem("v_turn_done")
        v_ready = sem("v_ready")
        s_done = sem("s_done")
        max_ready = sem("max_ready")
        exp_ready = sem("exp_ready")
        p_ready = sem("p_ready")
        p_turned = sem("p_turned")
        pT_ready = sem("pT_ready")
        pv_done = sem("pv_done")
        ot_ready = sem("ot_ready")
        m_hi = sem("m_hi")
        m_lo = sem("m_lo")
        win_ready = sem("win_ready")
        pool_done = sem("pool_done")
        tile_done = sem("tile_done")
        osq = sem("osq")
        orr = sem("orr")
        outs_ready = sem("outs_ready")
        out_sent = [sem(f"out_sent{i}") for i in range(2)]

        def blocks(w):
            return w[0].rearrange("(k p) n -> p k n", p=P)

        w_in_v, w_a_v, w_b_v, w_o_v = blocks(w_in), blocks(w_a_out), blocks(w_b_out), blocks(w_o)
        w_up_v, w_dn_v = blocks(w_up), blocks(w_down)

        N_AB = 0
        N_B = 1
        N_C1 = N_B + 8 * HEADS
        N_C2 = N_C1 + KD
        N_D = N_C2 + 2 * KD
        N_UP = [N_D + KD, 0]
        N_DN = [N_UP[0] + 2 * FF_CUT[0], 0]
        N_UP[1] = N_DN[0] + 2 * KD
        N_DN[1] = N_UP[1] + 2 * FF_CUT[1]
        N_Z = N_DN[1] + 2 * KD
        N_W = N_Z + len(Z_UNITS)
        plan = schedule()
        R_C2 = KD
        R_D = R_C2 + KD
        R_UP = [R_D + KD, R_D + KD + FF_CUT[0] + KD]
        R_DN = [R_UP[0] + FF_CUT[0], R_UP[1] + FF_CUT[1]]
        B_COLS = (A_Q, A_K, A_V, A_CG, A_XV, A_BG, A_GA, A_Z)

        block = ctx.enter_context(nc.Block())

        @block.sync
        def _(sp):
            def load(n, i, src, k=KD):
                if not isinstance(n, int) or n >= 4:
                    sp.wait_ge(split_ready, n - 3)
                dst = raw[:, i % 4, 0:k * P].rearrange("p (k n) -> p k n", k=k)
                sp.dma_start(dst, src).then_inc(raw_landed[i % 4], 16)

            xv = x[0].rearrange("(c p) d -> p c d", p=P)
            for c in range(TC):
                sp.dma_start(xin[:, c, :], xv[:, c, :]).then_inc(x_landed, 16)
            sp.wait_ge(prow_clear, 1)
            r = 0
            for src, n in ((norm_mix_g[0], 8), (conv_a_w[0].rearrange("k c -> (k c)"), 24),
                           (gdn_conv_w[0].rearrange("k c -> (k c)"), 96), (norm_ffn_g[0], 8),
                           (ffn_conv_w[0].rearrange("k c -> (k c)"), 3 * 2 * FB), (norm_final_g, 8), (norm_g_2[0], 8),
                           (pool_scale_2[0], 2), (gdn_norm_g[0], 1)):
                v = src.rearrange("(r p) -> r p", p=P)
                done = 0
                while done < n:
                    m = min(n - done, P - r % P)
                    sp.dma_start(prow[r % P:r % P + m, r // P * P:r // P * P + P],
                                 v[done:done + m, :]).then_inc(par_landed, 16)
                    r, done = r + m, done + m
            assert r == R_END
            for src, at, n in ((gdn_A_log, 0, 8), (gdn_dt_bias, 8, 8), (fox_bf_2, 16, 6)):
                sp.dma_start(rows8[:, at:at + n], src.to_broadcast([P, n])).then_inc(par_landed, 16)
            load(N_AB, N_AB, w_in_v[:, :, A_AB:A_AB + P])

            past = sp.alloc_register("column")
            sp.reg_mov(past, 3 * P)

            def column(less):
                return ds(sp.snap(past) + less, P)

            def head_loads(h):
                for s in range(8):
                    load(N_B + 8 * h + s, N_B + s, w_in_v[:, :, column(B_COLS[s] - 3 * P)])
                sp.reg_add(past, past, P)

            head_loads(0)
            with sp.Fori(1, HEADS) as h:
                head_loads(h)
            for j in range(KD):
                load(N_C1 + j, N_C1 + j, w_a_v[:, :, j * P:j * P + P])
            sp.reg_mov(past, 3 * P)
            with sp.Fori(0, KD // 2) as i:
                for q in range(2):
                    for s, w, c in ((0, w_in_v, A_GB), (1, w_b_v, 0)):
                        load(N_C2 + 4 * i + 2 * q + s, N_C2 + 2 * q + s, w[:, :, column(c + q * P - 3 * P)])
                sp.reg_add(past, past, 2 * P)
            with sp.Fori(0, KD // 4) as i:
                for s in range(4):
                    load(N_D + 4 * i + s, N_D + s, w_o_v[:, :, ds(i * (4 * P) + s * P, P)])
            for f in range(2):
                with sp.Fori(0, FF_CUT[f] // 2) as i:
                    for q in range(2):
                        for s in range(2):
                            c = s * FF + (f * FF_CUT[0] + q) * P
                            load(N_UP[f] + 4 * i + 2 * q + s, N_UP[f] + 2 * q + s,
                                 w_up_v[:, :, ds(i * (2 * P) + c, P)])
                kh = FF_CUT[f] // 2
                with sp.Fori(0, KD // 2) as i:
                    for q in range(2):
                        for s in range(2):
                            k0 = f * FF_CUT[0] + s * kh
                            load(N_DN[f] + 4 * i + 2 * q + s, N_DN[f] + 2 * q + s,
                                 w_dn_v[:, k0:k0 + kh, ds(i * (2 * P) + q * P, P)], kh)

            w2 = w_in_2[0].rearrange("(k p) n -> p k n", p=P)
            for u, (what, g, c) in enumerate(Z_UNITS):
                n = N_Z + u
                if what == "iwff":
                    sp.wait_ge(split_ready, n - 3)
                    dst = raw[:, n % 4, :].rearrange("p (k n) -> p k n", k=KD)
                    sp.dma_start(dst[:, :, 64:P], w2[:, :, B_END - 64:B_END]).then_inc(iw_extra, 16)
                    sp.wait_ge(iw_extra, 16)
                    sp.dma_start(dst[:, :, 0:64], w2[:, :, B_IW:B_IW + 64]).then_inc(raw_landed[n % 4], 16)
                elif what == "ik":
                    sp.wait_ge(split_ready, n - 3)
                    dst = raw[:, n % 4, :].rearrange("p (k n) -> p k n", k=KD)
                    for i in range(3):
                        sp.dma_start(dst[:, :, 32 * i:32 * i + 32], w2[:, :, B_IK:B_IK + 32]).then_inc(ik_extra, 16)
                    sp.wait_ge(ik_extra, 48)
                    sp.dma_start(dst[:, :, 96:P], w2[:, :, B_IK:B_IK + 32]).then_inc(raw_landed[n % 4], 16)
                else:
                    load(n, n, w2[:, :, c:c + P])
                if u == 6:
                    sp.wait_ge(late_clear, 1)
                    for i in range(4):
                        r = 64 * (i % 2)
                        sp.dma_start(pw[r:r + 64, i // 2, r:r + 64], pool_w_2[0, i]).then_inc(late_landed, 16)
                    sp.dma_start(gfin[:], final_g_2.rearrange("(a n) -> a n", a=1).to_broadcast([P, D])).then_inc(
                        late_landed, 16)
            for i, k in enumerate(W_ORDER):
                n = N_W + i
                sp.wait_ge(split_ready, n - 3)
                sp.dma_start(raw[:, n % 4, :], w_out_2[0, k * P:k * P + P, :]).then_inc(raw_landed[n % 4], 16)
            for c in range(TC):
                sp.wait_ge(outs_ready, c + 1)
                sp.dma_start(out[0, c * P:c * P + P, :], outs[:, c % 2, :]).then_inc(out_sent[c % 2], 16)
            for i in range(2):
                sp.wait_ge(out_sent[i], 16 * TC // 2)
        @block.tensor
        def _(pe):
            def unit(n, i, b, k0, rhs_hi, rhs_lo, kn=KD, first=True, last=True, parts=1, ready=None):
                pe.wait_ge(split_ready, n + 1)
                todo = []
                for k in range(kn):
                    hi = whi[:, i % 2, k * P:k * P + P]
                    lo = wlo[:, i % 2, k * P:k * P + P]
                    a, c = slot(rhs_hi + k0 + k), slot(rhs_lo + k0 + k)
                    todo += [(hi, a), (hi, c), (lo, a)]
                each = len(todo) // parts
                for m, (l, r) in enumerate(todo):
                    if ready and m % 3 == 0:
                        pe.wait_ge(ready[0], ready[1] + m // 3 + 1)
                    ins = pe.matmul(gb[:, b, :], l, r, start=(first and m == 0), stop=(last and m == len(todo) - 1))
                    if m == len(todo) - 1:
                        ins.then_inc(unit_done, 1)
                    if (m + 1) % each == 0:
                        yield

            def whole(*a, **k):
                for _ in unit(*a, **k):
                    pass

            def norm_sum(n, ring, start, stop, bank=0):
                pe.wait_ge(xsq_ready, n + 1)
                pe.matmul(gd[:, bank, :], ones[:], (cx, ca)[ring][:], start=start, stop=stop).then_inc(xsq_used, 1)

            def norm_spread(norm, banks=(1,)):
                pe.wait_ge(xr_ready, norm + 1)
                for i, b in enumerate(banks):
                    for c in range(TC):
                        ins = pe.matmul(gd[:, b, c * P:c * P + P], rr[:, 4 + i, c:c + 1].to_broadcast([P, P]), ident[:],
                                        start=True, stop=True)
                ins.then_inc(xrb_ready, 1)

            pe.wait_ge(masks_ready, 1)
            pe.wait_ge(x_landed, 16 * TC)
            for k in range(KD):
                if k >= 2:
                    pe.wait_ge(xT_ready, k - 1)
                for c in range(TC):
                    ins = pe.transpose(gd[:, 2 + k % 2, c * P:c * P + P], xin[:, c, k * P:k * P + P], ident[:])
                ins.then_inc(x_turned, 1)
                if k:
                    norm_sum(k - 1, (k - 1) % 2, k == 1, False)
            pe.wait_ge(par_landed, 16 * PAR_DMAS)
            for r in range((R_END + P - 1) // P):
                m = min(P, R_END - r * P)
                ins = pe.transpose(gd[:, 1, r * P:r * P + m], prow[0:m, r * P:r * P + P], ident[0:m, 0:m])
            ins.then_inc(par_turned, 1)
            norm_sum(KD - 1, 1, False, True)
            pe.wait_ge(par_ready, 1)
            norm_spread(0)

            whole(N_AB, N_AB, 3, 0, H_HI, H_LO, ready=(h_ready, 0))
            whole(N_B, N_B, 0, 0, H_HI, H_LO)
            pe.wait_ge(ab_ready, 1)
            for c in range(TC):
                ins = pe.transpose(gd[:, 0, c * P:c * P + P], Yb[:, c, :], ident[:])
            ins.then_inc(ab_turned, 1)

            def step(g, h):
                if g == 0:
                    pe.wait_ge(conv_silu, 3 * h + 2)
                    for c in range(TC):
                        ins = pe.transpose(gd[:, 0, c * P:c * P + P], kc[:, c * P:c * P + P], ident[:])
                    ins.then_inc(kq_turned, 1)
                    for c in range(TC):
                        ins = pe.transpose(gd[:, 1, c * P:c * P + P], qc[:, c * P:c * P + P], ident[:])
                    ins.then_inc(kq_turned, 1)
                elif g == 1:
                    pe.wait_ge(hc_ready, h + 1)
                    for c in range(TC):
                        ins = pe.matmul(gd[:, 3, c * P:c * P + P], hc[:, C_G + c:C_G + c + 1].to_broadcast([P, P]),
                                        ident[:], start=True, stop=True)
                    ins.then_inc(gb_done, 1)
                elif g == 3:
                    for i, src in ((0, Kt), (1, Yb)):
                        pe.wait_ge(tok_ready, 2 * h + 1 + i)
                        for c in range(TC):
                            ins = pe.transpose(gd[:, i, c * P:c * P + P], src[:, c, :], ident[:])
                        ins.then_inc(back_done, 1)
                elif g == 4:
                    pe.wait_ge(kt_ready, 2 * h + 1)
                    if not (isinstance(h, int) and h == 0):
                        pe.wait_ge(yb_ready, h)
                    for c in range(TC):
                        ins = pe.matmul(gd[:, 2, c * P:c * P + P], KT[:, c, :], KT[:, c, :], start=True, stop=True)
                    ins.then_inc(kk_done, 1)
                    pe.wait_ge(kt_ready, 2 * h + 2)
                    pe.wait_ge(arg_ready, h + 1)
                    for c in range(TC):
                        ins = pe.matmul(gd[:, 3, c * P:c * P + P], KT[:, c, :], QT[:, c, :], start=True, stop=True)
                    ins.then_inc(kk_done, 1)
                elif g == 5:
                    pe.wait_ge(conv_silu, 3 * h + 3)
                    for c in range(TC):
                        ins = pe.transpose(gd[:, 1, c * P:c * P + P], vc[:, c * P:c * P + P], ident[:])
                    ins.then_inc(v_turned, 1)
                elif g == 6:
                    pe.wait_ge(u_ready, 7 * h + 1)
                    pe.wait_ge(lt_ready, 2 * h + 2)
                    for c in range(TC):
                        ins = pe.transpose(gd[:, 3, c * P:c * P + P], Ui[:, c, :], ident[:])
                    ins.then_inc(u_turned, 1)
                elif 7 <= g <= 18 and g % 2:
                    l = (g - 7) // 2
                    if l == 0:
                        pe.wait_ge(t_first, h + 1)
                    else:
                        pe.wait_ge(t_ready, 5 * h + l)
                    for c in range(TC):
                        ins = pe.matmul(gd[:, 0, c * P:c * P + P], LT[:, c, :], Ti[:, c, :], start=True, stop=True)
                    ins.then_inc(y_done, 1)
                elif 7 <= g <= 18:
                    l = (g - 8) // 2
                    pe.wait_ge(ym_ready, 6 * h + l + 1)
                    if l == 0:
                        pe.wait_ge(vtok_ready, h + 1)
                    if l < 5:
                        for c in range(TC):
                            pe.matmul(gd[:, 1, c * P:c * P + P], Ui[:, c, :], Yb[:, c, :], start=True, stop=True)
                    for c in range(TC):
                        ins = pe.matmul(gd[:, 2, c * P:c * P + P], Yb[:, c, :], Ui[:, c, :], start=True, stop=True)
                    ins.then_inc(z_done, 1)
                elif 19 <= g <= 29:
                    c = (g - 18) // 3
                    what = (g - 18) % 3
                    if what == 0:
                        pe.wait_ge(s_ready, 3 * h + c)
                        pe.matmul(gd[:, 0, 0:P], KT[:, c, :], S[:], start=True, stop=True)
                        pe.matmul(gd[:, 0, P:2 * P], QT[:, c, :], S[:], start=True, stop=True).then_inc(ks_done, 1)
                    elif what == 1:
                        if c == 0:
                            pe.wait_ge(u_ready, 7 * h + 7)
                            rhs = Vt[:, 0, :]
                        else:
                            pe.wait_ge(rhs_ready, 3 * h + c)
                            rhs = Rr[:]
                        pe.matmul(gd[:, 3, 0:P], Ui[:, c, :], rhs, start=True, stop=True).then_inc(vn_done, 1)
                    else:
                        if c < TC - 1:
                            pe.wait_ge(vd_ready, 3 * h + c + 1)
                            pe.matmul(gd[:, 2, 0:P], Kt[:, c, :], vd[:], start=True, stop=True).then_inc(su_done, 1)
                        pe.wait_ge(vn_ready, 4 * h + c + 1)
                        if c >= 1:
                            pe.wait_ge(o_ready, 4 * h + c)
                        pe.matmul(gd[:, 1, 0:P], AT[:, c, :], vn[:], start=True, stop=True).then_inc(av_done, 1)
                elif g == 31:
                    pe.wait_ge(on_ready, h + 1)
                    for c in range(TC):
                        ins = pe.transpose(gd[:, 2, c * P:c * P + P], LT[:, c, :], ident[:])
                    ins.then_inc(o_turned, 1)

            def head(h, peeled):
                for s in range(8):
                    if peeled and s == 0:
                        pe.wait_ge(ab_g, 1)
                        pe.matmul(gd[:, 0, 0:HEADS * TC], triu[:], sm[:, 0, 0:HEADS * TC], start=True, stop=True)
                        pe.matmul(gd[:, 0, P:P + HEADS * TC], ones[:], sm[:, 0, 0:HEADS * TC],
                                  start=True, stop=True).then_inc(gcum_done, 1)
                        continue
                    if s >= 4:
                        free, count = ((conv_done, 3 * h + 1), (conv_done, 3 * h + 2), (conv_done, 3 * h + 3),
                                       (cg_copied, h + 1))[s - 4]
                        pe.wait_ge(free, count)
                    elif not peeled:
                        pe.wait_ge((cg_ready, ya_ready, ga_ready, z_ready)[s], h)
                    elif s == 3:
                        pe.wait_ge(ab_ready, 1)
                    u = unit(N_B + 8 * h + s, N_B + s, s % 4, 0, H_HI, H_LO, parts=4)
                    for m in range(4):
                        next(u)
                        if s >= 3:
                            step((s - 3) * 4 + m, h)
                        elif not peeled:
                            step(20 + s * 4 + m, h - 1)
                    for _ in u:
                        pass

            head(0, True)
            with pe.Fori(1, HEADS) as h:
                head(h, False)

            pe.wait_ge(ya_lo, HEADS)
            for j in range(KD):
                if j < 4:
                    pe.wait_ge((cg_ready, ya_ready, ga_ready, z_ready)[j], HEADS)
                else:
                    pe.wait_ge(out_read, j - 3)
                u = unit(N_C1 + j, N_C1 + j, j % 4, 0, YA_HI, YA_LO, parts=4)
                for m in range(4):
                    next(u)
                    if j < 3:
                        step(20 + j * 4 + m, HEADS - 1)
                for _ in u:
                    pass
            with pe.Fori(0, KD // 2) as i:
                for q in range(2):
                    pe.wait_ge(out_read, 2 * i + (R_C2 + q - 1))
                    whole(N_C2 + 4 * i + 2 * q, N_C2 + 2 * q, 2 * q, 0, H_HI, H_LO)
                    pe.wait_ge(yb_lo, HEADS)
                    whole(N_C2 + 4 * i + 2 * q + 1, N_C2 + 2 * q + 1, 2 * q + 1, 0, YB_HI, YB_LO)
            for j in range(KD):
                pe.wait_ge(out_read, R_D + (j - 3 if j >= 4 else -1 if j < 2 else 0))
                u = unit(N_D + j, N_D + j, j % 4, 0, MIX_HI, MIX_LO, parts=2, ready=(mix_lo, 0) if j == 0 else None)
                next(u)
                if j:
                    norm_sum(KD + j - 1, (j - 1) % 2, j == 1, False)
                for _ in u:
                    pass
            norm_sum(2 * KD - 1, 1, False, True)
            norm_spread(1)

            def down(f, i, sums=False):
                kh = FF_CUT[f] // 2
                for q in range(2):
                    pe.wait_ge(out_read, 2 * i + (R_DN[f] + q - 1))
                    for s in range(2):
                        pe.wait_ge(up_lo, f * FF_CUT[0] + kh * (s + 1))
                        whole(N_DN[f] + 4 * i + 2 * q + s, N_DN[f] + 2 * q + s, q,
                              s * kh, FF_HI, FF_LO, kn=kh, first=(s == 0), last=(s == 1))
                        if sums and s == 0 and not (isinstance(i, int) and i == 0 and q == 0):
                            stream_sums(2 * i + q - 1)

            def stream_sums(j):
                peeled = isinstance(j, int)
                for i, b in ((0, 0), (1, 2)):
                    norm_sum(2 * j + (2 * KD + i), i, peeled and j == 0, peeled and j == KD - 1, b)

            for f in range(2):
                with pe.Fori(0, FF_CUT[f] // 2) as i:
                    for q in range(2):
                        pe.wait_ge(out_read, 2 * i + (R_UP[f] + q - 1))
                        for s in range(2):
                            if s:
                                pe.wait_ge(out_read, R_UP[f])
                            whole(N_UP[f] + 4 * i + 2 * q + s, N_UP[f] + 2 * q + s, 2 * q + s, 0, H_HI, H_LO,
                                  ready=(h_ready, KD) if f == q == s == 0 else None)
                if f == 0:
                    with pe.Fori(0, KD // 2) as i:
                        down(f, i)
                else:
                    down(f, 0, sums=True)
                    with pe.Fori(1, KD // 2) as i:
                        down(f, i, sums=True)
            stream_sums(KD - 1)
            norm_spread(2, (1, 3))


            def beside(e):
                what = e[0]
                if what == "turn_iw":
                    pe.wait_ge(z_read, 1)
                    for c in range(TC):
                        ins = pe.transpose(gd[:, 2, c * P:c * P + P], flat(iwff)[:, c * P:c * P + P], ident[:])
                    ins.then_inc(iw_turned, 1)
                elif what == "cum_f":
                    pe.wait_ge(f_ready, 1)
                    pe.matmul(gd[:, 3, 0:HX * TC], triu[:], sm[:, 0, 0:HX * TC], start=True, stop=False)
                    pe.matmul(gd[:, 3, 0:HX * TC], ones[:], sm[:, 1, 0:HX * TC], start=False, stop=True).then_inc(f_cum, 1)
                elif what == "turn_f":
                    pe.wait_ge(f_tok, 1)
                    for c in range(TC):
                        ins = pe.transpose(gd[0:HX, 2, c * P:c * P + P], sm[:, 2, c * HX:c * HX + HX], ident[:])
                    ins.then_inc(f_turned, 1)
                elif what == "score":
                    _, n, c, h = e
                    pe.wait_ge(z_read, 4)
                    if n >= 2:
                        pe.wait_ge(relu_ready, n - 1)
                    pe.matmul(gd[:, n % 2, 0:(c + 1) * P], iq[h // 4][:, c * P:c * P + P], ikz[h % 4][:, 0:(c + 1) * P],
                              start=True, stop=True).then_inc(score_done, 1)
                elif what == "turn_v":
                    g = e[1]
                    pe.wait_ge(z_read, V_READ[g])
                    if g == 0:
                        pe.wait_ge(f_rows, 1)
                    else:
                        pe.wait_ge(pT_ready, TC * 2 * g)
                    for c in range(TC):
                        ins = pe.transpose(gd[:, 2, c * P:c * P + P], vraw[:, c * P:c * P + P], ident[:])
                    ins.then_inc(v_turn_done, 1)
                elif what == "s":
                    _, c, t = e
                    g, i = t // 2, t % 2
                    if c == 0:
                        pe.wait_ge(z_read, Q_READ[g])
                        pe.wait_ge(z_read_v, g + 1)
                        if g < 3:
                            pe.wait_ge(f_put[g], 64)
                        if t == 0:
                            pe.wait_ge(relu_ready, (TC - 1) * IDX_HEADS)
                    n = TC * t + c
                    if n >= 2:
                        pe.wait_ge(exp_ready, n - 1)
                    q = ring(g, i if g < 3 else 0)
                    pe.matmul(gd[:, c % 2, 0:(c + 1) * P], q[:, c * P:c * P + P], ring(g, 2 + i)[:, 0:(c + 1) * P],
                              start=True, stop=True).then_inc(s_done, 1)
                elif what == "t":
                    _, c, t = e
                    n = TC * t + c
                    pe.wait_ge(p_ready, n + 1)
                    if n >= 1:
                        pe.wait_ge(pT_ready, n)
                    pe.wait_ge(v_ready, t // 2 + 1)
                    for j in range(c + 1):
                        ins = pe.transpose(gd[:, 2, j * P:j * P + P], prob[c][:, j * P:j * P + P], ident[:])
                    ins.then_inc(p_turned, 1)
                elif what == "pv":
                    t = e[2]
                    g, i = t // 2, t % 2
                    pe.wait_ge(pT_ready, TC * (t + 1))
                    if g and i == 0:
                        pe.wait_ge(ot_ready, g)
                    for j in range(TC):
                        ins = pe.matmul(gd[64 * i:64 * i + 64, 3, j * P:T], vt[g % 2][:, j, 64 * i:64 * i + 64],
                                        pT[:, j, j * P:T], start=(j == 0), stop=(j == TC - 1))
                    ins.then_inc(pv_done, 1)
                elif what == "pool":
                    b = e[1]
                    pe.wait_ge(win_ready, b + 1)
                    pe.wait_ge(late_landed, 16 * 5)
                    pe.matmul(gb[:, (len(Z_UNITS) - 4 + b) % 4, :], pw[:, b, :], wins[b][0], start=True, stop=True).then_inc(pool_done, 1)

            for u in range(len(Z_UNITS)):
                if u >= 4:
                    reader, count = Z_READER[u - 4]
                    pe.wait_ge({"act": z_read, "dve": z_read_v}[reader], count)
                if u == 1:
                    pe.wait_ge(pads_ready, 1)
                p = unit(N_Z + u, N_Z + u, u % 4, 0, H_HI, H_LO, parts=4, ready=(h_ready, 2 * KD) if u == 0 else None)
                for m in range(4):
                    next(p)
                    for e in plan.get((u, m), ()):
                        beside(e)
                for _ in p:
                    pass
            for e in plan[(len(Z_UNITS), 0)]:
                beside(e)
            def place(c, half):
                b = 2 * c + half
                return gb[:, b, :] if b < 4 else gd[:, b - 4, :]

            pe.wait_ge(xT_norm, KD)
            for c in (1, 2, 3, 0):
                pe.wait_ge(*((ot_ready, GROUPS + 2), (z_read, Z_READER[-1][1]), (exp_ready, TC * 2 * GROUPS),
                             (ot_ready, GROUPS))[c])
                for half in range(2):
                    for j in range(4):
                        pe.matmul(place(c, half)[:, j * P:j * P + P], xT[:, 4 * half + j, c * P:c * P + P], ident[:],
                                  start=(j == 0), stop=False, skip_group_check=True)
            for i, k in enumerate(W_ORDER):
                n = N_W + i
                pe.wait_ge(split_ready, n + 1)
                pe.wait_ge(m_lo, i + 1)
                for c in range(TC):
                    hi = act_a[:, MIX_HI + k, c * P:c * P + P]
                    lo = act_a[:, MIX_LO + k, c * P:c * P + P]
                    for half in range(2):
                        wh = whi[:, n % 2, half * T:half * T + T]
                        wl = wlo[:, n % 2, half * T:half * T + T]
                        for m, (l, r) in enumerate(((hi, wh), (lo, wh), (hi, wl))):
                            ins = pe.matmul(place(c, half), l, r, start=False, stop=(i == KD - 1 and m == 2),
                                            skip_group_check=True)
                    if i == KD - 1:
                        ins.then_inc(tile_done, 1)
                    elif c == TC - 1:
                        ins.then_inc(unit_done, 1)

        @block.scalar
        def _(sc):
            own = Steps(sc, act_order)

            def split(n, i, k=KD):
                sc.wait_ge(raw_landed[i % 4], (n + 4 - i % 4) * 4)
                if not isinstance(n, int) or n >= 2:
                    sc.wait_ge(unit_done, n - 1)
                sc.activation(whi[:, i % 2, 0:k * P], raw[:, i % 4, 0:k * P], ACT.Copy).then_inc(hi_ready, 1)

            def norm_square(n, ring, src, gain=1.0):
                if not isinstance(n, int) or n >= 2:
                    sc.wait_ge(xsq_used, n - 1)
                sc.activation((cx, ca)[ring][:], src, ACT.Square, scale=gain).then_inc(xsq_ready, 1)

            def norm_split(norm):
                for k in range(KD):
                    sc.wait_ge(hn_ready, KD * norm + k + 1)
                    sc.activation(act_a[:, H_HI + k, :], (qc, kc, vc)[k % 3][:], ACT.Copy).then_inc(hn_hi, 1)

            for k in range(KD):
                sc.wait_ge(x_turned, k + 1)
                sc.activation(xT[:, k, :], gd[:, 2 + k % 2, :], ACT.Copy).then_inc(xT_ready, 1)
                sc.wait_ge(xT_ready, k + 1)
                norm_square(k, k % 2, xT[:, k, :])
            split(N_AB, N_AB)
            norm_split(0)
            split(N_B, N_B)
            sc.wait_ge(unit_done, 1)
            sc.activation(Yb[:].rearrange("p c j -> p (c j)"), gb[:, 3, :], ACT.Copy).then_inc(ab_ready, 1)
            sc.wait_ge(abt_ready, 1)
            sc.activation(sm[:, 3, 0:32], sm[:, 2, 0:32], ACT.Exp, scale=-1.0)
            sc.activation(sm[:, 3, 32:64], sm[:, 2, 32:64], ACT.Exp, scale=-1.0)
            sc.activation(sm[:, 4, 0:HEADS], rows8[:, 0:HEADS], ACT.Exp).then_inc(ab_exp, 1)
            split(N_B + 1, N_B + 1)
            sc.wait_ge(gcum_sb, 1)
            sc.activation(sm[:, 8, 0:32], sm[:, 5, 0:32], ACT.Exp)
            sc.activation(sm[:, 9, 0:32], sm[:, 6, 0:32], ACT.Exp)
            sc.activation(sm[:, 10, 0:32], sm[:, 7, 0:32], ACT.Exp).then_inc(cols_exp, 1)

            def step(g, h):
                if g == 0:
                    for i, dst in ((0, Ti), (1, Ui)):
                        sc.wait_ge(kq_turned, 2 * h + 1 + i)
                        sc.activation(dst[:], bank(gd[:, i, :]), ACT.Square).then_inc(sq_ready, 1)
                elif g == 2:
                    sc.wait_ge(arg_ready, h + 1)
                    sc.activation(dec[:], dec[:], ACT.Exp).then_inc(dec_ready, 1)
                elif g == 3:
                    for i, dst in ((0, KT), (1, QT)):
                        sc.wait_ge(back_done, 2 * h + 1 + i)
                        sc.activation(dst[:], bank(gd[:, i, :]), ACT.Copy,
                                      scale=(1.0, float(P) ** -0.5)[i]).then_inc(kt_ready, 1)
                elif g == 5:
                    sc.wait_ge(v_turned, h + 1)
                    sc.activation(Vt[:], bank(gd[:, 1, :]), ACT.Copy).then_inc(vtok_ready, 1)
                elif g == 6:
                    sc.wait_ge(u_turned, h + 1)
                    sc.activation(Ti[:], bank(gd[:, 3, :]), ACT.Copy).then_inc(t_first, 1)
                elif 19 <= g <= 29:
                    c = (g - 18) // 3
                    what = (g - 18) % 3
                    if what == 0:
                        sc.wait_ge(rhs_ready, 3 * h + c)
                        sc.activation(qs[:], gd[:, 0, P:2 * P], ACT.Copy, scale=hc[:, C_E + c:C_E + c + 1]).then_inc(qs_ready, 1)
                    elif what == 1:
                        sc.wait_ge(vn_done, 4 * h + c + 1)
                        if c < TC - 1:
                            sc.activation(vd[:], gd[:, 3, 0:P], ACT.Copy,
                                          scale=hc[:, C_BKD + c:C_BKD + c + 1]).then_inc(vd_ready, 1)
                        sc.activation(vn[:], gd[:, 3, 0:P], ACT.Copy, scale=hc[:, C_BETA + c:C_BETA + c + 1]).then_inc(vn_ready, 1)
                elif g == 30:
                    sc.wait_ge(o_ready, 4 * h + 4)
                    sc.activation(Ti[:], LT[:], ACT.Square).then_inc(osq_ready, 1)
                elif g == 31:
                    sc.wait_ge(yb_ready, h + 1)
                    sc.activation(act_b[:, ds(h + (YB_HI - SLOTS_A), 1), :].rearrange("p a t -> p (a t)"),
                                  Yb[:].rearrange("p c j -> p (c j)"), ACT.Copy).then_inc(yb_hi, 1)

            def first_half(h, s):
                sc.wait_ge(unit_done, N_B + 8 * h + s + 1)
                if s < 3:
                    if s == 0:
                        sc.wait_ge(taps_ready, h + 1)
                    sc.activation((qc, kc, vc)[s][:], gb[:, s, :], ACT.Copy,
                                  scale=hw[:, 4 * s + 3:4 * s + 4]).then_inc(tap_first, 1)
                elif s == 3:
                    if not (isinstance(h, int) and h == 0):
                        sc.wait_ge(ya_lo, h)
                    sc.activation(cx[:], gb[:, 3, :], ACT.Copy).then_inc(cg_copied, 1)
                elif s == 6:
                    sc.activation(gate[:, ds(h, 1), :].rearrange("p a t -> p (a t)"), gb[:, 2, :], ACT.Tanh,
                                  scale=0.5).then_inc(ga_ready, 1)
                elif s == 7:
                    if not (isinstance(h, int) and h == 0):
                        sc.wait_ge(yb_ready, h)
                    sc.activation(zs[:], gb[:, 3, :], ACT.Silu).then_inc(z_ready, 1)

            def second_half(h, s):
                if s < 3:
                    sc.wait_ge(conv_done, 3 * h + s + 1)
                    dst = (qc, kc, vc)[s]
                    sc.activation(dst[:], dst[:], ACT.Silu).then_inc(conv_silu, 1)
                elif s == 5:
                    sc.wait_ge(ya_ready, h + 1)
                    sc.activation(act_a[:, ds(h + YA_HI, 1), :].rearrange("p a t -> p (a t)"), ca[:],
                                  ACT.Copy).then_inc(ya_hi, 1)

            def head(h, peeled):
                for s in range(8):
                    if not (peeled and s == 0):
                        split(N_B + 8 * h + s + 1, N_B + s + 1)
                    for m in range(4):
                        if m == 1:
                            if s > 0:
                                first_half(h, s - 1)
                            elif not peeled:
                                first_half(h - 1, 7)
                        if m == 3 and s > 0:
                            second_half(h, s - 1)
                        if s >= 3:
                            step((s - 3) * 4 + m, h)
                        elif not peeled:
                            step(20 + s * 4 + m, h - 1)

            head(0, True)
            with sc.Fori(1, HEADS) as h:
                head(h, False)
            for j in range(KD):
                split(N_C1 + j + 1, N_C1 + j + 1)
                for m in range(4):
                    if j == 0 and m == 1:
                        first_half(HEADS - 1, 7)
                    if j < 3:
                        step(20 + j * 4 + m, HEADS - 1)
            split(N_C2 + 1, N_C2 + 1)
            with sc.Fori(0, KD // 2) as i:
                for q in range(2):
                    sc.wait_ge(unit_done, N_C2 + 4 * i + 2 * q + 1)
                    sc.activation((qc, kc)[q][:], gb[:, 2 * q, :], ACT.Tanh, scale=0.5).then_inc(gb_tanh, 1)
                    split(N_C2 + 4 * i + 2 * q + 2, N_C2 + 2 * q + 2)
                    sc.wait_ge(mix_ready, 2 * i + q + 1)
                    sc.activation(act_a[:, ds(2 * i + (MIX_HI + q), 1), :].rearrange("p a t -> p (a t)"), (qc, kc)[q][:],
                                  ACT.Copy, scale=0.5).then_inc(mix_hi, 1)
                    split(N_C2 + 4 * i + 2 * q + 3, N_C2 + 2 * q + 3)
            for j in range(KD):
                if j < KD - 1:
                    split(N_D + j + 2, N_D + j + 2)
                sc.wait_ge(out_read, R_D + j + 1)
                norm_square(KD + j, j % 2, xT[:, j, :])
            split(N_D + KD + 1, N_D + KD + 1)
            norm_split(1)
            for f in range(2):
                with sc.Fori(0, FF_CUT[f] // 2) as i:
                    for q in range(2):
                        for s in range(2):
                            j = 2 * i + (f * FF_CUT[0] + q)
                            sc.wait_ge(unit_done, N_UP[f] + 4 * i + 2 * q + s + 1)
                            dst = ((qc, kc), (vc, cx))[q][s]
                            sc.activation(dst[:], gb[:, 2 * q + s, :], ACT.Copy,
                                          scale=par[:, ds(2 * i + (R_CONV_F + 2 * 2 * FB + s * FB + f * FF_CUT[0] + q), 1)]
                                          ).then_inc(up_first, 1)
                            split(N_UP[f] + 4 * i + 2 * q + s + 2, N_UP[f] + 2 * q + s + 2)
                            if s == 0:
                                sc.wait_ge(up_conv, j + 1)
                                sc.activation(dst[:], dst[:], ACT.Silu).then_inc(up_silu, 1)
                            else:
                                sc.wait_ge(up_ready, j + 1)
                                sc.activation(act_a[:, ds(2 * i + (FF_HI + q), 1), :].rearrange("p a t -> p (a t)"),
                                              (qc, vc)[q][:], ACT.Copy).then_inc(up_hi, 1)
                with sc.Fori(0, KD // 2) as i:
                    for s in range(4):
                        split(N_DN[f] + 4 * i + s + 2, N_DN[f] + s + 2)
                        if f and s % 2:
                            q = s // 2
                            sc.wait_ge(out_read, 2 * i + (R_DN[1] + q + 1))
                            xj = xT[:, ds(2 * i + q, 1), :].rearrange("p a t -> p (a t)")
                            norm_square(4 * i + (2 * KD + 2 * q), 0, xj)
                            norm_square(4 * i + (2 * KD + 2 * q + 1), 1, xj, par[:, ds(2 * i + (R_FIN_G + q), 1)])
            sc.wait_ge(xrb_ready, 3)
            sc.activation(flat(Vt), gd[:, 1, :], ACT.Copy).then_inc(xrb_kept, 1)
            norm_split(2)

            sc.wait_ge(pads_ready, 1)

            def z_out(u):
                what, g, _ = Z_UNITS[u]
                src = gb[:, u % 4, :]
                sc.wait_ge(unit_done, N_Z + u + 1)
                if what == "iwff":
                    sc.activation(flat(iwff), src, ACT.Copy).then_inc(z_read, 1)
                elif what == "ik":
                    for i in range(4):
                        ins = sc.activation(ikz[i][32 * i:32 * i + 32, :], src[32 * i:32 * i + 32, :], ACT.Copy)
                    ins.then_inc(z_read, 1)
                elif what == "iq":
                    sc.activation(iq[g], src, ACT.Copy).then_inc(z_read, 1)
                elif what == "q" and g < 3:
                    if g == 2:
                        sc.wait_ge(s_done, TC * 2)
                    for i in range(2):
                        r = slice(64 * i, 64 * i + 64)
                        ins = sc.activation(ring(g, i)[r, :], src[r, :], ACT.Copy, scale=0.125)
                    ins.then_inc(z_read, 1)
                elif what == "q":
                    sc.wait_ge(s_done, TC * 2 * (g - 1))
                    sc.activation(ring(g, 0), src, ACT.Copy, scale=0.125).then_inc(z_read, 1)
                elif what == "v":
                    if g:
                        sc.wait_ge(v_turn_done, g)
                    sc.activation(vraw[:], src, ACT.Copy).then_inc(z_read, 1)
                elif what == "g":
                    if g >= 2:
                        sc.wait_ge(ot_ready, g - 1)
                    sc.activation(sg[g % 2][:], src, ACT.Silu).then_inc(z_read, 1)
                elif what == "pv":
                    if g:
                        sc.wait_ge(win_ready, 1)
                    sc.activation(pvb, src, ACT.Copy).then_inc(z_read, 1)
                elif what == "pg":
                    if g == 0:
                        sc.wait_ge(ot_ready, GROUPS - 1)
                    else:
                        sc.wait_ge(ot_ready, GROUPS)
                    sc.activation(sg[g][:], src, ACT.Silu).then_inc(z_read, 1)

            def mixed(i, k):
                sc.wait_ge(ot_ready, i + 1)
                sc.activation(act_a[:, MIX_HI + k, :], ot[:], ACT.Copy).then_inc(m_hi, 1)

            def beside(e):
                what = e[0]
                if what == "turn_iw":
                    sc.wait_ge(iw_split, 1)
                    sc.activation(sm[:, 3, 0:HX * TC], sm[:, 2, 0:HX * TC], ACT.Exp, scale=-1.0).then_inc(f_exp, 1)
                elif what == "turn_f":
                    sc.wait_ge(f_turned, 1)
                    sc.activation(frow[:, 0, :], gd[0:HX, 2, :], ACT.Copy)
                    sc.activation(frow[:, 1, :], gd[0:HX, 2, :], ACT.Copy, scale=-1.0).then_inc(f_rows, 1)
                elif what == "score":
                    _, n, c, h = e
                    if n >= 2:
                        sc.wait_ge(relu_used, n - 1)
                    sc.wait_ge(score_done, n + 1)
                    sc.activation(relu[n % 2][:, 0:(c + 1) * P], gd[:, n % 2, 0:(c + 1) * P], ACT.Relu).then_inc(relu_ready, 1)
                elif what == "turn_v":
                    g = e[1]
                    sc.wait_ge(v_turn_done, g + 1)
                    if g == 1:
                        sc.wait_ge(xT_norm, KD)
                    if g >= 2:
                        sc.wait_ge(pv_done, 2 * (g - 1))
                    sc.activation(flat(vt[g % 2]), gd[:, 2, :], ACT.Copy).then_inc(v_ready, 1)
                elif what == "s":
                    _, c, t = e
                    n = TC * t + c
                    sc.wait_ge(max_ready, n + 1)
                    if n >= TC:
                        sc.wait_ge(p_turned, n - TC + 1)
                    elif n == 2:
                        sc.wait_ge(relu_used, (TC - 1) * IDX_HEADS)
                    w = (c + 1) * P
                    sc.activation(prob[c][:, 0:w], gd[:, c % 2, 0:w], ACT.Exp, bias=small[:, 8 + c:9 + c], scale=-1.0,
                                  accum_out=small[:, 12 + c:13 + c]).then_inc(exp_ready, 1)
                elif what == "t":
                    _, c, t = e
                    n = TC * t + c
                    sc.wait_ge(p_turned, n + 1)
                    if t and c == 0:
                        sc.wait_ge(pv_done, t)
                    sc.activation(pT[:, 0:c + 1, c * P:c * P + P],
                                  gd[:, 2, 0:(c + 1) * P].rearrange("p (j q) -> p j q", q=P), ACT.Copy).then_inc(pT_ready, 1)
                elif what == "pv":
                    t = e[2]
                    if t % 2:
                        mixed(t // 2, (5, 6, 7, 2, 3, 4)[t // 2])

            for u in range(len(Z_UNITS)):
                n = N_Z + u + 1
                if u:
                    split(n, n)
                for m in range(4):
                    if m == 1 and u:
                        z_out(u - 1)
                    for e in plan.get((u, m), ()):
                        beside(e)
            z_out(len(Z_UNITS) - 1)
            for e in plan[(len(Z_UNITS), 0)]:
                beside(e)
            for b in range(2):
                mixed(GROUPS + b, b)
            for i in range(1, KD):
                split(N_W + i, N_W + i)
            for c in range(TC):
                sc.wait_ge(tile_done, c + 1)
                if c:
                    sc.wait_ge(osq, c)
                src = gb[:, 2 * c:2 * c + 2, :] if c < 2 else gd[:, 2 * c - 4:2 * c - 2, :]
                sc.activation(wk[:].rearrange("p (a n) -> p a n", a=2), src, ACT.Square,
                              accum_out=small[:, 16 + c:17 + c]).then_inc(osq, 1)

        @block.vector
        def _(dve):
            own = Steps(dve, dve_order)
            link = own.link

            def split(n, i, k=KD):
                dve.wait_ge(hi_ready, n + 1)
                dve.tensor_tensor(wlo[:, i % 2, 0:k * P], raw[:, i % 4, 0:k * P],
                                  whi[:, i % 2, 0:k * P].bitcast(F32), ALU.subtract).then_inc(split_ready, 1)

            def log1p(e, s, t, out_):
                link(dve.tensor_scalar(s, e, 2.0, None, ALU.add))
                link(dve.reciprocal(s, s))
                link(dve.tensor_tensor(s, s, e, ALU.mult))
                link(dve.tensor_tensor(t, s, s, ALU.mult))
                link(dve.tensor_scalar(out_, t, 1.0 / 17, None, ALU.mult))
                for c in range(15, 1, -2):
                    link(dve.scalar_tensor_tensor(out_, out_, 1.0 / c, t, ALU.add, ALU.mult))
                link(dve.scalar_tensor_tensor(out_, out_, 1.0, s, ALU.add, ALU.mult))
                link(dve.tensor_scalar(out_, out_, 2.0, None, ALU.mult))

            def sum_positions(b=0, tmp=Yb):
                link(dve.tensor_tensor(tmp[:], bank(gd[:, b, :]), over(ident[:]), ALU.mult))
                return dve.tensor_reduce(ss[:, b // 2, :], tmp[:], AX_X, ALU.add)

            def normalise(norm, g0, b=1):
                dve.wait_ge(xrb_ready, norm + 1)

                def low_part(k):
                    dve.wait_ge(hn_hi, KD * norm + k + 1)
                    dve.tensor_tensor(act_a[:, H_LO + k, :], (qc, kc, vc)[k % 3][:], act_a[:, H_HI + k, :].bitcast(F32),
                                      ALU.subtract).then_inc(h_ready, 1)

                for k in range(KD):
                    if k >= 3:
                        dve.wait_ge(h_ready, KD * norm + k - 2)
                    dve.scalar_tensor_tensor((qc, kc, vc)[k % 3][:], xT[:, k, :], par[:, g0 + k:g0 + k + 1], gd[:, b, :],
                                             ALU.mult, ALU.mult).then_inc(hn_ready, 1)
                    if k:
                        low_part(k - 1)
                low_part(KD - 1)

            dve.memset(prow[:, :], 0.0).then_inc(prow_clear, 1)
            dve.wait_ge(par_turned, 1)
            dve.tensor_copy(par[:], gd[:, 1, 0:R_END]).then_inc(par_ready, 1)
            dve.wait_ge(par_ready, 1)
            link(dve.tensor_tensor(par[:, R_G2:R_G2 + KD], par[:, R_G2:R_G2 + KD], par[:, R_FIN_G:R_FIN_G + KD], ALU.mult))
            dve.tensor_scalar(par[:, R_G2:R_G2 + KD], par[:, R_G2:R_G2 + KD], float(D) ** 0.5, None, ALU.mult)
            dve.tensor_scalar(par[:, R_GDN_G:R_GDN_G + 1], par[:, R_GDN_G:R_GDN_G + 1], float(P) ** 0.5, None, ALU.mult)
            for b in range(3):
                dve.tensor_copy(htaps[:, :, 4 * b:4 * b + 4],
                                par[:, R_CONV_G:R_CONV_G + 96].rearrange("p (k b h) -> p h b k", k=4, b=3)[:, :, b, :])
            link(dve.tensor_copy(htaps[:, :, 12:15],
                                 par[:, R_CONV_A:R_CONV_A + 24].rearrange("p (k h) -> p h k", k=3)))
            dve.wait_ge(xsq_used, KD)
            sum_positions().then_inc(xss_ready, 1)
            normalise(0, R_MIX_G)
            split(N_AB, N_AB)
            split(N_B, N_B)

            dve.wait_ge(ab_turned, 1)
            abt = bank(gd[:, 0, :])
            hct = lambda ap: ap.rearrange("p (h c) -> p h c", c=TC)
            link(dve.tensor_tensor(hct(sm[:, 1, 0:32]), abt[:, :, 0:HEADS].rearrange("p c h -> p h c"),
                                   rows8[:, HEADS:2 * HEADS].unsqueeze(2).to_broadcast([P, HEADS, TC]), ALU.add))
            link(dve.tensor_copy(hct(sm[:, 2, 32:64]), abt[:, :, HEADS:2 * HEADS].rearrange("p c h -> p h c")))
            link(dve.tensor_scalar(sm[:, 2, 0:32], sm[:, 1, 0:32], -1.0, None, ALU.mult))
            dve.tensor_tensor(sm[:, 2, 0:32], sm[:, 2, 0:32], sm[:, 1, 0:32], ALU.max).then_inc(abt_ready, 1)
            dve.wait_ge(ab_exp, 1)
            link(dve.tensor_scalar(sm[:, 3, 32:64], sm[:, 3, 32:64], 1.0, None, ALU.add))
            link(dve.reciprocal(sm[:, 11, 0:32], sm[:, 3, 32:64]))
            log1p(sm[:, 3, 0:32], sm[:, 5, 0:32], sm[:, 6, 0:32], sm[:, 7, 0:32])
            link(dve.tensor_scalar(sm[:, 1, 0:32], sm[:, 1, 0:32], 0.0, None, ALU.max))
            link(dve.tensor_tensor(sm[:, 1, 0:32], sm[:, 1, 0:32], sm[:, 7, 0:32], ALU.add))
            dve.scalar_tensor_tensor(hct(sm[:, 0, 0:32]), hct(sm[:, 1, 0:32]), -1.0,
                                     sm[:, 4, 0:HEADS].unsqueeze(2).to_broadcast([P, HEADS, TC]),
                                     ALU.mult, ALU.mult).then_inc(ab_g, 1)
            split(N_B + 1, N_B + 1)
            dve.wait_ge(gcum_done, 1)
            link(dve.tensor_copy(sm[:, 5, 0:32], gd[:, 0, 0:32]))
            link(dve.tensor_copy(sm[:, 6, 0:32], gd[:, 0, P:P + 32]))
            dve.tensor_tensor(sm[:, 7, 0:32], sm[:, 6, 0:32], sm[:, 5, 0:32], ALU.subtract).then_inc(gcum_sb, 1)
            dve.wait_ge(cols_exp, 1)
            cols = lambda at: hcols[:, :, at:at + TC]
            dve.tensor_copy(cols(C_G), hct(sm[:, 5, 0:32]))
            dve.tensor_scalar(cols(C_NEGE), hct(sm[:, 8, 0:32]), -1.0, None, ALU.mult)
            dve.tensor_copy(cols(C_E), hct(sm[:, 8, 0:32]))
            dve.tensor_copy(cols(C_BETA), hct(sm[:, 11, 0:32]))
            dve.tensor_tensor(cols(C_BKD), hct(sm[:, 11, 0:32]), hct(sm[:, 10, 0:32]), ALU.mult)
            link(dve.tensor_copy(cols(C_EL), hct(sm[:, 9, 0:32])))

            def step(g, h):
                if g == 0:
                    if not (isinstance(h, int) and h == 0):
                        dve.wait_ge(o_turned, h)
                    dve.tensor_copy(hc[:], hcols[:, ds(h, 1), :].rearrange("p a n -> p (a n)")).then_inc(hc_ready, 1)
                    for i, src in ((0, Ti), (1, Ui)):
                        dve.wait_ge(sq_ready, 2 * h + 1 + i)
                        dve.tensor_reduce(ss[:, i, :], src[:], AX_X, ALU.add).then_inc(ss_ready, 1)
                elif g == 1:
                    dve.wait_ge(gb_done, h + 1)
                    link(dve.tensor_tensor(dec[:], bank(gd[:, 3, :]), wide(hc[:, C_G:C_G + TC]), ALU.subtract))
                    dve.tensor_tensor(dec[:], dec[:], over(negT[:]), ALU.add).then_inc(arg_ready, 1)
                elif g == 2:
                    for i, dst in ((0, Kt), (1, Yb)):
                        dve.wait_ge(r_ready, 2 * h + 1 + i)
                        dve.tensor_tensor(dst[:], bank(gd[:, i, :]), wide(rr[:, 2 + i, :]), ALU.mult).then_inc(tok_ready, 1)
                elif g == 4:
                    dve.wait_ge(kk_done, 2 * h + 1)
                    dve.wait_ge(decb_ready, h + 1)
                    dve.tensor_tensor(LT[:], bank(gd[:, 2, :]), LT[:], ALU.mult).then_inc(lt_ready, 1)
                    dve.wait_ge(lt_ready, 2 * h + 1)
                    link(dve.tensor_tensor(Ui[:], LT[:], over(negm1[:]), ALU.mult))
                    dve.tensor_tensor(Ui[:], Ui[:], over(ident[:]), ALU.add).then_inc(u_ready, 1)
                    dve.wait_ge(kk_done, 2 * h + 2)
                    dve.tensor_tensor(AT[:], bank(gd[:, 3, :]), dec[:], ALU.mult).then_inc(lt_ready, 1)
                elif 7 <= g <= 18 and g % 2:
                    l = (g - 7) // 2
                    dve.wait_ge(y_done, 6 * h + l + 1)
                    dve.tensor_tensor(Yb[:], bank(gd[:, 0, :]), over(lev[:, l, :]), ALU.mult).then_inc(ym_ready, 1)
                elif 7 <= g <= 18:
                    l = (g - 8) // 2
                    dve.wait_ge(z_done, 6 * h + l + 1)
                    if l < 5:
                        dve.tensor_tensor(Ti[:], Ti[:], bank(gd[:, 1, :]), ALU.subtract).then_inc(t_ready, 1)
                    dve.tensor_tensor(Ui[:], Ui[:], bank(gd[:, 2, :]), ALU.subtract).then_inc(u_ready, 1)
                elif 19 <= g <= 29:
                    c = (g - 18) // 3
                    what = (g - 18) % 3
                    if what == 0:
                        dve.wait_ge(ks_done, 3 * h + c)
                        dve.scalar_tensor_tensor(Rr[:], gd[:, 0, 0:P], hc[:, C_NEGE + c:C_NEGE + c + 1], Vt[:, c, :],
                                                 ALU.mult, ALU.add).then_inc(rhs_ready, 1)
                    elif what == 2:
                        if c < TC - 1:
                            dve.wait_ge(su_done, 3 * h + c + 1)
                        if c == 0:
                            dve.tensor_copy(S[:], gd[:, 2, 0:P]).then_inc(s_ready, 1)
                            dve.wait_ge(av_done, 4 * h + c + 1)
                            dve.tensor_copy(LT[:, 0, :], gd[:, 1, 0:P]).then_inc(o_ready, 1)
                        else:
                            if c < TC - 1:
                                dve.scalar_tensor_tensor(S[:], S[:], hc[:, C_EL + c:C_EL + c + 1], gd[:, 2, 0:P],
                                                         ALU.mult, ALU.add).then_inc(s_ready, 1)
                            dve.wait_ge(av_done, 4 * h + c + 1)
                            dve.wait_ge(qs_ready, 3 * h + c)
                            dve.tensor_tensor(LT[:, c, :], gd[:, 1, 0:P], qs[:], ALU.add).then_inc(o_ready, 1)
                elif g == 30:
                    dve.wait_ge(osq_ready, h + 1)
                    dve.tensor_reduce(ss[:, 2, :], Ti[:], AX_X, ALU.add).then_inc(oss_ready, 1)
                    dve.wait_ge(or_ready, h + 1)
                    dve.tensor_tensor(LT[:], LT[:], wide(rr[:, 5, :]), ALU.mult).then_inc(on_ready, 1)
                elif g == 31:
                    dve.wait_ge(o_turned, h + 1)
                    yb = Yb[:].rearrange("p c j -> p (c j)")
                    dve.wait_ge(z_ready, h + 1)
                    dve.scalar_tensor_tensor(yb, gd[:, 2, :], par[:, R_GDN_G:R_GDN_G + 1], zs[:],
                                             ALU.mult, ALU.mult).then_inc(yb_ready, 1)
                    dve.wait_ge(yb_hi, h + 1)
                    dve.tensor_tensor(act_b[:, ds(h + (YB_LO - SLOTS_A), 1), :].rearrange("p a t -> p (a t)"), yb,
                                      act_b[:, ds(h + (YB_HI - SLOTS_A), 1), :].rearrange("p a t -> p (a t)").bitcast(F32),
                                      ALU.subtract).then_inc(yb_lo, 1)

            def after(h, s):
                if s < 3:
                    dve.wait_ge(tap_first, 3 * h + s + 1)
                    dst = (qc, kc, vc)[s]
                    for a in range(1, 4):
                        ins = dve.scalar_tensor_tensor(dst[:, a:T], gb[:, s, 0:T - a], hw[:, 4 * s + 3 - a:4 * s + 4 - a],
                                                       dst[:, a:T], ALU.mult, ALU.add)
                        if a < 3:
                            link(ins)
                    ins.then_inc(conv_done, 1)
                elif s == 4:
                    dve.wait_ge(unit_done, N_B + 8 * h + s + 1)
                    dve.wait_ge(cg_copied, h + 1)
                    dve.tensor_tensor(cx[:], gb[:, 0, :], cx[:], ALU.mult).then_inc(cg_ready, 1)
                    dve.wait_ge(cg_ready, h + 1)
                    link(dve.tensor_scalar(ca[:], cx[:], hw[:, 14:15], None, ALU.mult))
                    for a in range(1, 3):
                        link(dve.scalar_tensor_tensor(ca[:, a:T], cx[:, 0:T - a], hw[:, 14 - a:15 - a], ca[:, a:T],
                                                      ALU.mult, ALU.add))
                elif s == 5:
                    dve.wait_ge(unit_done, N_B + 8 * h + s + 1)
                    dve.tensor_tensor(ca[:], ca[:], gb[:, 1, :], ALU.mult).then_inc(ya_ready, 1)
                    dve.wait_ge(ya_hi, h + 1)
                    dve.tensor_tensor(act_a[:, ds(h + YA_LO, 1), :].rearrange("p a t -> p (a t)"), ca[:],
                                      act_a[:, ds(h + YA_HI, 1), :].rearrange("p a t -> p (a t)").bitcast(F32),
                                      ALU.subtract).then_inc(ya_lo, 1)

            def head(h, peeled):
                dve.tensor_copy(hw[:], htaps[:, ds(h, 1), :].rearrange("p a n -> p (a n)")).then_inc(taps_ready, 1)
                for s in range(8):
                    if not (peeled and s == 0):
                        split(N_B + 8 * h + s + 1, N_B + s + 1)
                    for m in range(4):
                        if s > 0 and m == (3 if s == 6 else 1):
                            after(h, s - 1)
                        if s >= 3:
                            step((s - 3) * 4 + m, h)
                        elif not peeled:
                            step(20 + s * 4 + m, h - 1)

            head(0, True)
            with dve.Fori(1, HEADS) as h:
                own.enter(h - 1, 11)
                head(h, False)
            own.leave(HEADS - 1)
            for j in range(KD):
                split(N_C1 + j + 1, N_C1 + j + 1)
                if j < 3:
                    for m in range(4):
                        step(20 + j * 4 + m, HEADS - 1)
                dve.wait_ge(ga_ready, HEADS)
                dve.wait_ge(unit_done, N_C1 + j + 1)
                dve.scalar_tensor_tensor(gate[:, j, :], gate[:, j, :], 1.0, gb[:, j % 4, :],
                                         ALU.add, ALU.mult).then_inc(out_read, 1)
            dve.wait_ge(out_read, KD)
            split(N_C2 + 1, N_C2 + 1)
            with dve.Fori(0, KD // 2) as i:
                for q in range(2):
                    split(N_C2 + 4 * i + 2 * q + 2, N_C2 + 2 * q + 2)
                    m = (qc, kc)[q]
                    dve.wait_ge(unit_done, N_C2 + 4 * i + 2 * q + 2)
                    dve.wait_ge(gb_tanh, 2 * i + q + 1)
                    dve.scalar_tensor_tensor(m[:], m[:], 1.0, gb[:, 2 * q + 1, :], ALU.add, ALU.mult).then_inc(out_read, 1)
                    dve.wait_ge(out_read, 2 * i + (R_C2 + q + 1))
                    dve.tensor_tensor(m[:], m[:], gate[:, ds(2 * i + q, 1), :].rearrange("p a t -> p (a t)"),
                                      ALU.add).then_inc(mix_ready, 1)
                    dve.wait_ge(mix_hi, 2 * i + q + 1)
                    dve.scalar_tensor_tensor(act_a[:, ds(2 * i + (MIX_LO + q), 1), :].rearrange("p a t -> p (a t)"), m[:], 0.5,
                                             act_a[:, ds(2 * i + (MIX_HI + q), 1), :].rearrange("p a t -> p (a t)").bitcast(F32),
                                             ALU.mult, ALU.subtract).then_inc(mix_lo, 1)
                    split(N_C2 + 4 * i + 2 * q + 3, N_C2 + 2 * q + 3)
            for j in range(KD):
                dve.wait_ge(unit_done, N_D + j + 1)
                dve.tensor_tensor(xT[:, j, :], xT[:, j, :], gb[:, j % 4, :], ALU.add).then_inc(out_read, 1)
                split(N_D + j + 2, N_D + j + 2)
            dve.wait_ge(xsq_used, 2 * KD)
            sum_positions().then_inc(xss_ready, 1)
            normalise(1, R_FFN_G)
            for f in range(2):
                with dve.Fori(0, FF_CUT[f] // 2) as i:
                    own.enter(i, 4)
                    for q in range(2):
                        for s in range(2):
                            j = 2 * i + (f * FF_CUT[0] + q)
                            dst = ((qc, kc), (vc, cx))[q][s]
                            dve.wait_ge(up_first, 2 * j + s + 1)
                            for a in range(1, 3):
                                at = R_CONV_F + (2 - a) * 2 * FB + s * FB + f * FF_CUT[0] + q
                                ins = dve.scalar_tensor_tensor(dst[:, a:T], gb[:, 2 * q + s, 0:T - a],
                                                               par[:, ds(2 * i + at, 1)],
                                                               dst[:, a:T], ALU.mult, ALU.add)
                                if a == 1:
                                    link(ins)
                            ins.then_inc((up_conv, out_read)[s], 1)
                            split(N_UP[f] + 4 * i + 2 * q + s + 2, N_UP[f] + 2 * q + s + 2)
                            if s == 1:
                                g = (qc, vc)[q]
                                dve.wait_ge(up_silu, j + 1)
                                dve.wait_ge(out_read, 2 * i + (R_UP[f] + q + 1))
                                dve.tensor_tensor(g[:], g[:], dst[:], ALU.mult).then_inc(up_ready, 1)
                                dve.wait_ge(up_hi, j + 1)
                                dve.tensor_tensor(act_b[:, ds(2 * i + (FF_LO - SLOTS_A + q), 1), :].rearrange("p a t -> p (a t)"), g[:],
                                                  act_a[:, ds(2 * i + (FF_HI + q), 1), :].rearrange("p a t -> p (a t)").bitcast(F32),
                                                  ALU.subtract).then_inc(up_lo, 1)
                own.leave(FF_CUT[f] // 2)
                with dve.Fori(0, KD // 2) as i:
                    for q in range(2):
                        split(N_DN[f] + 4 * i + 2 * q + 2, N_DN[f] + 2 * q + 2)
                        dve.wait_ge(unit_done, N_DN[f] + 4 * i + 2 * q + 2)
                        xj = xT[:, ds(2 * i + q, 1), :].rearrange("p a t -> p (a t)")
                        dve.tensor_tensor(xj, xj, gb[:, q, :], ALU.add).then_inc(out_read, 1)
                        split(N_DN[f] + 4 * i + 2 * q + 3, N_DN[f] + 2 * q + 3)
            dve.wait_ge(xsq_used, 4 * KD)
            sum_positions(0, Yb)
            sum_positions(2, Kt).then_inc(xss_ready, 1)
            normalise(2, R_G2, 3)

            dve.wait_ge(pads_ready, 1)

            def beside(e):
                what = e[0]
                if what == "turn_iw":
                    dve.wait_ge(iw_turned, 1)
                    t = bank(gd[:, 2, :])
                    col = lambda i, k: sm[:, i, 0:TC * k].rearrange("p (c h) -> p c h", h=k)
                    dve.tensor_scalar(col(8, IDX_HEADS), t[:, :, 0:IDX_HEADS], float(IDX_HEADS) ** -0.5, None, ALU.mult)
                    link(dve.tensor_tensor(col(4, HX), t[:, :, P - HX:P],
                                           rows8[:, 16:16 + HX].unsqueeze(1).to_broadcast([P, TC, HX]), ALU.add))
                    n = HX * TC
                    link(dve.tensor_scalar(sm[:, 5, 0:n], sm[:, 4, 0:n], -1.0, None, ALU.mult))
                    dve.tensor_tensor(sm[:, 2, 0:n], sm[:, 4, 0:n], sm[:, 5, 0:n], ALU.max).then_inc(iw_split, 1)
                    dve.wait_ge(f_exp, 1)
                    log1p(sm[:, 3, 0:n], sm[:, 6, 0:n], sm[:, 7, 0:n], sm[:, 9, 0:n])
                    link(dve.tensor_scalar(sm[:, 5, 0:n], sm[:, 5, 0:n], 0.0, None, ALU.max))
                    link(dve.tensor_tensor(sm[:, 5, 0:n], sm[:, 5, 0:n], sm[:, 9, 0:n], ALU.add))
                    link(dve.tensor_scalar(sm[:, 0, 0:n], sm[:, 5, 0:n], -1.0, None, ALU.mult))
                    link(dve.memset(sm[:, 1, 0:HX], 0.0))
                    for c in range(1, TC):
                        ins = dve.tensor_tensor(sm[:, 1, c * HX:c * HX + HX], sm[:, 1, (c - 1) * HX:c * HX],
                                                sm[:, 0, (c - 1) * HX:c * HX], ALU.add)
                        if c < TC - 1:
                            link(ins)
                    ins.then_inc(f_ready, 1)
                elif what == "cum_f":
                    dve.wait_ge(f_cum, 1)
                    dve.tensor_copy(sm[:, 2, 0:HX * TC], gd[:, 3, 0:HX * TC]).then_inc(f_tok, 1)
                elif what == "score":
                    _, n, c, h = e
                    dve.wait_ge(relu_ready, n + 1)
                    w = (c + 1) * P
                    acc = selb[:, SEL_AT[c]:SEL_AT[c] + w]
                    f = sm[:, 8, c * IDX_HEADS + h:c * IDX_HEADS + h + 1]
                    if h == 0:
                        ins = dve.tensor_scalar(acc, relu[n % 2][:, 0:w], f, 0.0, ALU.mult, ALU.add)
                    else:
                        dve.wait_ge(relu_used, n)
                        ins = dve.scalar_tensor_tensor(acc, relu[n % 2][:, 0:w], f, acc, ALU.mult, ALU.add)
                    ins.then_inc(relu_used, 1)
                    if h == IDX_HEADS - 1:
                        dve.wait_ge(relu_used, n + 1)
                        link(dve.memset(selb[0:64, SEL_AT[c] + w - 64:SEL_AT[c] + w], FILL))
                elif what == "round":
                    _, r, c = e
                    v = selb[:, SEL_AT[c]:SEL_AT[c + 1]]
                    link(dve.max(small[:, 0:8], v))
                    link(dve.match_replace(v, small[:, 0:8], v, TAKEN))
                    if r == TOPK // 8 - 1:
                        dve.tensor_scalar(v, v, 0.5 * (FILL + TAKEN), NEG, ALU.is_gt, ALU.mult).then_inc(sel_ready, 1)
                elif what == "s":
                    _, c, t = e
                    n = TC * t + c
                    w = (c + 1) * P
                    if t < HX:
                        bias = cbias[:, T - w:T]
                    else:
                        bias = selb[:, SEL_AT[c]:SEL_AT[c + 1]]
                        if t == HX and c == 0:
                            dve.wait_ge(sel_ready, TC - 1)
                    dve.wait_ge(s_done, n + 1)
                    dve.tensor_tensor_reduce(gd[:, c % 2, 0:w], gd[:, c % 2, 0:w], bias, -1.0, -MASKED, ALU.add,
                                             ALU.min, small[:, 8 + c:9 + c]).then_inc(max_ready, 1)
                elif what == "weigh":
                    _, c, t = e
                    n = TC * t + c
                    dve.wait_ge(exp_ready, n + 1)
                    link(dve.reciprocal(small[:, 24 + c:25 + c], small[:, 12 + c:13 + c]))
                    p = prob[c][:, 0:(c + 1) * P]
                    dve.tensor_scalar(p, p, small[:, 24 + c:25 + c], None, ALU.mult).then_inc(p_ready, 1)
                elif what == "pv":
                    t = e[2]
                    if t % 2:
                        g = t // 2
                        dve.wait_ge(pv_done, t + 1)
                        dve.wait_ge(z_read, G_READ[g])
                        if g:
                            dve.wait_ge(m_lo, g)
                        dve.tensor_tensor(ot[:], gd[:, 3, :], sg[g % 2][:], ALU.mult).then_inc(ot_ready, 1)
                        low(g, (5, 6, 7, 2, 3, 4)[g])

            def low(i, k):
                dve.wait_ge(m_hi, i + 1)
                dve.tensor_tensor(act_a[:, MIX_LO + k, :], ot[:], act_a[:, MIX_HI + k, :].bitcast(F32),
                                  ALU.subtract).then_inc(m_lo, 1)

            def z_out(u):
                what, g, _ = Z_UNITS[u]
                if what == "k":
                    dve.wait_ge(unit_done, N_Z + u + 1)
                    if g >= 2:
                        dve.wait_ge(s_done, TC * 2 * (g - 1))
                    for i in range(2):
                        r = slice(64 * i, 64 * i + 64)
                        if g in (3, 4):
                            for row in (64 - 64 * i, 96 - 64 * i):
                                dve.memset(ring(g, 2 + i)[row:row + 1, :], 0.0)
                        ins = dve.tensor_copy(ring(g, 2 + i)[r, :], gb[r, u % 4, :])
                    ins.then_inc(z_read_v, 1)
                elif what == "pv":
                    dve.wait_ge(z_read, PV_READ[g])
                    src, have = pvb, 1
                    for dst in wins[g] * (1 + g):
                        link(dve.tensor_copy(dst[:, 0:have], src[:, 0:have]))
                        link(dve.tensor_tensor(dst[:, have:T], src[:, have:T], src[:, 0:T - have], ALU.add))
                        src, have = dst, 2 * have
                    res = wins[g][0]
                    for rows, win in zip((slice(0, 64), slice(64, P)), wins[g]):
                        link(dve.scalar_tensor_tensor(res[rows, 16:T], win[rows, 16:T], small[rows, 32 + g:33 + g],
                                                      pvb[rows, 16:T], ALU.mult, ALU.subtract))
                        link(dve.tensor_tensor(res[rows, 0:16], win[rows, 0:16], small[rows, 48 + 16 * g:64 + 16 * g], ALU.mult))
                        ins = dve.tensor_tensor(res[rows, 0:16], res[rows, 0:16], pvb[rows, 0:16], ALU.subtract)
                        if rows.start == 0:
                            link(ins)
                    ins.then_inc(win_ready, 1)

            def pool_out(b):
                dve.wait_ge(pool_done, b + 1)
                dve.wait_ge(z_read, PG_READ[b])
                dve.wait_ge(m_lo, GROUPS + b)
                dve.scalar_tensor_tensor(ot[:], gb[:, (len(Z_UNITS) - 4 + b) % 4, :], par[:, R_PSC + b:R_PSC + b + 1], sg[b][:],
                                         ALU.mult, ALU.mult).then_inc(ot_ready, 1)
                low(GROUPS + b, b)

            for u in range(len(Z_UNITS)):
                if u:
                    split(N_Z + u + 1, N_Z + u + 1)
                for m in range(4):
                    if m == 1 and u:
                        z_out(u - 1)
                    for e in plan.get((u, m), ()):
                        beside(e)
            for e in plan[(len(Z_UNITS), 0)]:
                beside(e)
            for b in range(2):
                pool_out(b)
            for i in range(1, KD):
                split(N_W + i, N_W + i)
            dve.wait_ge(late_landed, 16 * 5)
            for c in range(TC):
                dve.wait_ge(orr, c + 1)
                if c >= 2:
                    dve.wait_ge(out_sent[c % 2], 16)
                src = gb[:, 2 * c:2 * c + 2, :] if c < 2 else gd[:, 2 * c - 4:2 * c - 2, :]
                dve.scalar_tensor_tensor(outs[:, c % 2, :].rearrange("p (a n) -> p a n", a=2), src, small[:, 36 + c:37 + c],
                                         gfin[:].rearrange("p (a n) -> p a n", a=2), ALU.mult, ALU.mult).then_inc(outs_ready, 1)

        @block.gpsimd
        def _(pool):
            own = Steps(pool, pool_order)
            link = own.link

            def keep(out_, in_, pattern, base, mult, op=ALU.is_ge, fill=0.0):
                link(pool.affine_select(out=out_, in_=in_, pattern=pattern, compare_op=op, fill=fill,
                                        base=base, channel_multiplier=mult))

            link(pool.memset(ones[:], 1.0))
            pool.memset(ident[:], 0.0)
            pool.memset(negT[:], 0.0)
            pool.memset(mhalf[:], -0.5)
            pool.memset(eps_one[:], EPS)
            link(pool.memset(eps_head[:], P * EPS))
            pool.affine_select(out=ident[:], in_=ident[:], pattern=[[-1, P]], compare_op=ALU.not_equal, fill=1.0,
                               base=0, channel_multiplier=1).then_inc(masks_ready, 1)
            pool.wait_ge(masks_ready, 1)
            keep(triu[:], ones[:], [[1, P]], 0, -1)
            keep(tril[:], ones[:], [[-1, P]], 0, 1)
            keep(negT[:], negT[:], [[1, P]], 0, -1, fill=NEG)
            for l in range(6):
                w = 2 << l
                v = lev[:, l, :].rearrange("p (b j) -> p b j", j=w)
                keep(v, tril[:].rearrange("p (b j) -> p b j", j=w), [[w, P // w], [0, w]], w - 1, -1)
            link(pool.tensor_copy(lev[:, 6, :], tril[:]))
            for l in range(6):
                link(pool.tensor_tensor(lev[:, l, :], lev[:, l + 1, :], lev[:, l, :], ALU.subtract))
            keep(negm1[:].rearrange("p (b j) -> p b j", j=2), triu[:].rearrange("p (b j) -> p b j", j=2),
                 [[-2, P // 2], [0, 2]], 0, 1)
            pool.tensor_tensor(negm1[:], ident[:], negm1[:], ALU.subtract).then_inc(masks_ready, 1)

            def rsqrt(dst, src, tmp, scale):
                link(pool.tensor_scalar(tmp, src, scale, EPS, ALU.mult, ALU.add))
                return pool.tensor_tensor(dst, tmp, mhalf[:, 0:TC], ALU.pow)

            def model_norm(norm):
                pool.wait_ge(xss_ready, norm + 1)
                rsqrt(rr[:, 4, :], ss[:, 0, :], rr[:, 0, :], 1.0 / D).then_inc(xr_ready, 1)

            model_norm(0)

            def rsqrt_sum(dst, src, tmp, guard):
                link(pool.tensor_tensor(tmp, src, guard[:], ALU.add))
                return pool.tensor_tensor(dst, tmp, mhalf[:, 0:TC], ALU.pow)

            def head_a(h):
                pool.wait_ge(ss_ready, 2 * h + 1)
                rsqrt_sum(rr[:, 2, :], ss[:, 0, :], rr[:, 0, :], eps_one).then_inc(r_ready, 1)
                pool.wait_ge(ss_ready, 2 * h + 2)
                rsqrt_sum(rr[:, 3, :], ss[:, 1, :], rr[:, 1, :], eps_one).then_inc(r_ready, 1)
                pool.wait_ge(hc_ready, h + 1)
                pool.wait_ge(dec_ready, h + 1)
                pool.tensor_tensor(LT[:], dec[:], wide(hc[:, C_BETA:C_BETA + TC]), ALU.mult).then_inc(decb_ready, 1)

            def head_b(h):
                pool.wait_ge(oss_ready, h + 1)
                rsqrt_sum(rr[:, 5, :], ss[:, 2, :], rr[:, 6, :], eps_head).then_inc(or_ready, 1)

            head_a(0)
            with pool.Fori(1, HEADS) as h:
                own.enter(h - 1, 3)
                head_b(h - 1)
                head_a(h)
            own.leave(HEADS - 1)
            head_b(HEADS - 1)
            model_norm(1)
            pool.wait_ge(out_read, R_D)
            for i in range(4):
                ins = pool.memset(ikz[i], 0.0)
            link(ins)
            for g in range(2):
                for i in range(2):
                    for what in (i, 2 + i):
                        r = 64 - 64 * i
                        link(pool.memset(ring(g, what)[r:r + 64, :], 0.0))
                        one = r if what < 2 else r + 32
                        link(pool.memset(ring(g, what)[one:one + 1, :], 1.0))
            for g in range(2):
                for i in range(2):
                    rows = slice(64 * i, 64 * i + 64)
                    window = 2 << (2 * g + i)
                    link(pool.memset(small[rows, 32 + g:33 + g], 1.0 / window))
                    for t in range(16):
                        ins = pool.memset(small[rows, 48 + 16 * g + t:49 + 16 * g + t], 1.0 / min(t + 1, window))
                    link(ins)
            pool.wait_ge(xss_ready, 3)
            link(pool.tensor_scalar(rr[:, 0, :], ss[:, 0, :], 1.0 / D, EPS, ALU.mult, ALU.add))
            link(pool.tensor_scalar(rr[:, 2, :], rr[:, 0, :], EPS * D, None, ALU.mult))
            link(pool.tensor_tensor(rr[:, 1, :], rr[:, 2, :], ss[:, 1, :], ALU.add))
            pool.tensor_tensor(rr[:, 4:6, :], rr[:, 0:2, :], mhalf[:].rearrange("p (a c) -> p a c", a=2),
                               ALU.pow).then_inc(xr_ready, 1)
            pool.memset(pw[:], 0.0).then_inc(late_clear, 1)
            link(pool.memset(cbias[:], 0.0))
            keep(cbias[:, T - P:T], cbias[:, T - P:T], [[-1, P]], 0, 1, fill=NEG)
            link(pool.memset(selb[:, 0:P], 0.0))
            pool.memset(selb[0:64, 64:P], NEG).then_inc(pads_ready, 1)
            pool.wait_ge(f_rows, 1)

            def decay_rows(g):
                for i in range(2):
                    r = 64 - 64 * i
                    h = 2 * g + i
                    pool.dma_start(ring(g, i)[r + 32:r + 33, :], frow[h:h + 1, 0, :]).then_inc(f_put[g], 16)
                    pool.dma_start(ring(g, 2 + i)[r:r + 1, :], frow[h:h + 1, 1, :]).then_inc(f_put[g], 16)

            decay_rows(0)
            decay_rows(1)
            pool.wait_ge(xrb_kept, 1)
            for k in range(KD):
                pool.wait_ge(hn_ready, 2 * KD + k + 1)
                link(pool.tensor_scalar(xT[:, k, :], xT[:, k, :], par[:, R_FIN_G + k:R_FIN_G + k + 1], None, ALU.mult))
                pool.tensor_tensor(xT[:, k, :], xT[:, k, :], flat(Vt), ALU.mult).then_inc(xT_norm, 1)
            pool.wait_ge(s_done, TC * 2)
            decay_rows(2)
            for c in range(TC):
                pool.wait_ge(osq, c + 1)
                link(pool.tensor_scalar(small[:, 40 + c:41 + c], small[:, 16 + c:17 + c], 1.0 / D, EPS, ALU.mult, ALU.add))
                pool.tensor_tensor(small[:, 36 + c:37 + c], small[:, 40 + c:41 + c], mhalf[:, 0:1], ALU.pow).then_inc(orr, 1)


_INS = ["x", "norm_mix_g", "w_in", "conv_a_w", "gdn_conv_w", "gdn_A_log", "gdn_dt_bias", "gdn_norm_g", "w_a_out",
        "w_b_out", "w_o", "norm_ffn_g", "w_up", "ffn_conv_w", "w_down", "norm_final_g", "w_in_2", "norm_g_2",
        "pool_w_2", "pool_scale_2", "fox_bf_2", "w_out_2", "final_g_2"]


def kernel(**inputs):
    import numpy as _np
    import concourse.bacc as _bacc
    from concourse import mybir as _mybir
    from concourse.bass_utils import run_bass_kernel_spmd as _run

    nc = _bacc.Bacc("TRN2", target_bir_lowering=False, num_devices=1)
    arrays, args = {}, []
    for name in _INS:
        a = _np.ascontiguousarray(inputs[name])
        arrays[f"in_{name}_dram"] = a
        args.append(nc.dram_tensor(f"in_{name}_dram", a.shape, _mybir.dt.from_np(a.dtype), kind="ExternalInput").ap())
    args.append(nc.dram_tensor("out_0_dram", (1, T, D), F32, kind="ExternalOutput").ap())
    hybrid_block_kernel(nc, *args)
    r = _run(nc, [arrays], core_ids=[0])
    return r.results[0]["out_0_dram"]
```

```python
from contextlib import ExitStack

import concourse.bass as bass
from concourse import mybir

P = 128
F32 = mybir.dt.float32
F32R = mybir.dt.float32r
ALU = mybir.AluOpType
ACT = mybir.ActivationFunctionType
AX_X = mybir.AxisListType.X
ds = bass.ds

T = 512
TC = T // P
D = 1024
KD = D // P
HEADS = 8
FF = 2816
FB = FF // P
EPS = 1e-6
NEG = -1.0e30

A_BG, A_CG, A_XV, A_Q, A_K, A_V, A_Z = (i * D for i in range(7))
A_AB = 7 * D
A_GA = A_AB + 2 * HEADS
A_GB = A_GA + D

H_HI, H_LO = 0, KD
YA_HI, YA_LO = 2 * KD, 3 * KD
YB_HI, YB_LO = 4 * KD, 5 * KD
MIX_HI, MIX_LO = 2 * KD, 3 * KD
FF_CUT = (12, 10)
FF_HI, FF_LO = 2 * KD, 4 * KD
SLOTS_A = 4 * KD

C_G, C_NEGE, C_E, C_BETA, C_BKD, C_EL = (TC * i for i in range(6))
N_COL = 6 * TC
N_TAP = 3 * 4 + 3

R_MIX_G = 0
R_CONV_A = 8
R_CONV_G = 32
R_FFN_G = 128
R_CONV_F = 136
R_FIN_G = R_CONV_F + 3 * 2 * FB
R_G2 = R_FIN_G + 8
R_PSC = R_G2 + 8
R_GDN_G = R_PSC + 2
R_END = R_GDN_G + 1

PAR_DMAS = 13

HX = 6
GROUPS = HX
IDX_HEADS = 8
TOPK = 128
FILL, TAKEN = -3.0e38, -3.3e38
B_PV, B_PG, B_DQ, B_DK, B_DV, B_DG, B_IQ = 0, 256, 512, 896, 1280, 1664, 2048
B_IK, B_IW, B_FQ, B_FK, B_FV, B_FG, B_FF = 2304, 2336, 2344, 2728, 3112, 3496, 3880
B_END = B_FF + HX
SEL_AT = [P * c * (c + 1) // 2 for c in range(TC + 1)]
Z_UNITS = ([("thin", 0, 0), ("iq", 0, B_IQ), ("iq", 1, B_IQ + P)]
           + [(w, g, c + g * P) for g in range(3) for w, c in (("q", B_FQ), ("k", B_FK), ("v", B_FV), ("g", B_FG))]
           + [(w, g + 3, c + g * P) for g in range(2) for w, c in (("q", B_DQ), ("k", B_DK), ("v", B_DV), ("g", B_DG))]
           + [("q", 5, B_DQ + 2 * P), ("k", 5, B_DK + 2 * P)] + [("pv", b, B_PV + b * P) for b in range(2)]
           + [("v", 5, B_DV + 2 * P), ("g", 5, B_DG + 2 * P)] + [("pg", b, B_PG + b * P) for b in range(2)])
W_ORDER = (5, 6, 7, 2, 3, 4, 0, 1)
MASKED = -3.0e38


def readers():
    n = {"act": 0, "dve": 0}
    out = []
    for what, _, _ in Z_UNITS:
        who = "dve" if what == "k" else "act"
        n[who] += 1
        out.append((who, n[who]))
    return out


Z_READER = readers()


def reads_of(what):
    return [count for (name, _, _), (_, count) in zip(Z_UNITS, Z_READER) if name == what]


Q_READ, V_READ, G_READ, PV_READ, PG_READ = (reads_of(w) for w in ("q", "v", "g", "pv", "pg"))


def schedule():
    at = {}
    put = lambda u, m, e: at.setdefault((u, m), []).append(e)
    put(1, 1, ("turn_iw",))
    put(2, 1, ("cum_f",))
    put(3, 1, ("turn_f",))
    todo = [(c, h) for c in range(1, TC) for h in range(IDX_HEADS)]
    for n, (c, h) in enumerate(todo):
        put((14 + n // 2) // 4, (14 + n // 2) % 4, ("score", n, c, h))
    rounds = [(r, c) for c in range(1, TC) for r in range(TOPK // 8)]
    for n, (r, c) in enumerate(rounds):
        put((20 + n) // 4, (20 + n) % 4, ("round", r, c))
    todo = {}
    for t in range(2 * GROUPS):
        start = 4 * 6 + 1 + 8 * t
        for c in range(TC):
            todo.setdefault(start + 2 * c + 2, []).append((5, ("weigh", c, t)))
            todo.setdefault(start + 2 * c + 4, []).append((0, ("t", c, t)))
            todo.setdefault(start + 2 * c, []).append((3, ("s", c, t)))
        todo.setdefault(start + 11, []).append((1, ("pv", 0, t)))
        if t % 2 == 0:
            todo.setdefault(start + (3 if t < 2 * GROUPS - 2 else 9), []).append((2, ("turn_v", t // 2)))
    last = len(Z_UNITS)
    first = [4 * Z_UNITS.index(("pv", b, B_PV + b * P)) + 5 for b in range(2)]
    for b, steps in enumerate((4, 6)):
        for n in range(steps):
            todo.setdefault(first[b] + n, []).append((6, ("window", b)))
    for b in range(2):
        todo.setdefault(4 * last - 4 + b, []).append((4, ("pool", b)))
    for slot in sorted(todo):
        for _, e in sorted(todo[slot], key=lambda x: x[0]):
            put(slot // 4, slot % 4, e)
    assert max(todo) == 4 * last
    return at


class Steps:

    def __init__(self, eng, sem):
        self.eng, self.sem, self.base, self.n = eng, sem, 0, 0

    def link(self, ins):
        ins.then_inc(self.sem, 1)
        self.n += 1
        self.eng.wait_ge(self.sem, self.base + self.n)

    def enter(self, i, per):
        self.at, self.base, self.n, self.per = self.base + self.n, self.base + self.n + i * per, 0, per

    def leave(self, turns):
        assert self.n == self.per, (self.n, self.per)
        self.base, self.n = self.at + turns * self.per, 0


def hybrid_block_kernel(nc, x, norm_mix_g, w_in, conv_a_w, gdn_conv_w, gdn_A_log, gdn_dt_bias, gdn_norm_g,
                        w_a_out, w_b_out, w_o, norm_ffn_g, w_up, ffn_conv_w, w_down, norm_final_g,
                        w_in_2, norm_g_2, pool_w_2, pool_scale_2, fox_bf_2, w_out_2, final_g_2, out):
    with ExitStack() as ctx:
        def sb(name, shape, dt=F32):
            return ctx.enter_context(nc.sbuf_tensor(name, shape, dt))

        def sem(name):
            return ctx.enter_context(nc.semaphore(name))

        raw = sb("raw", [P, 4, KD * P])
        whi = sb("whi", [P, 2, KD * P], F32R)
        wlo = sb("wlo", [P, 2, KD * P], F32R)
        act_a = sb("act_a", [P, SLOTS_A, T], F32R)
        xT = sb("xT", [P, KD, T])
        gate = sb("gate", [P, KD, T])
        qc = sb("qc", [P, T])
        kc = sb("kc", [P, T])
        vc = sb("vc", [P, T])
        cx = sb("cx", [P, T])
        ca = sb("ca", [P, T])
        zs = sb("zs", [P, T])
        Kt = sb("Kt", [P, TC, P])
        Vt = sb("Vt", [P, TC, P])
        KT = sb("KT", [P, TC, P])
        QT = sb("QT", [P, TC, P])
        dec = sb("dec", [P, TC, P])
        LT = sb("LT", [P, TC, P])
        AT = sb("AT", [P, TC, P])
        Ti = sb("Ti", [P, TC, P])
        Ui = sb("Ui", [P, TC, P])
        Yb = sb("Yb", [P, TC, P])
        S = sb("S", [P, P])
        vn = sb("vn", [P, P])
        vd = sb("vd", [P, P])
        Rr = sb("Rr", [P, P])
        ident = sb("ident", [P, P])
        ones = sb("ones", [P, P])
        triu = sb("triu", [P, P])
        tril = vd
        negT = sb("negT", [P, P])
        lev = sb("lev", [P, 6, P])
        negm1 = sb("negm1", [P, P])
        par = sb("par", [P, R_END])
        hcols = sb("hcols", [P, HEADS, N_COL])
        htaps = sb("htaps", [P, HEADS, N_TAP])
        hc = sb("hc", [P, N_COL])
        hw = sb("hw", [P, N_TAP])
        sm = sb("sm", [P, 12, 2 * HEADS * TC])
        rows8 = sb("rows8", [P, 2 * HEADS + 6])
        ss = sb("ss", [P, 4, TC])
        rr = sb("rr", [P, 8, TC])
        mhalf = sb("mhalf", [P, TC])
        eps_one = sb("eps_one", [P, TC])
        eps_head = sb("eps_head", [P, TC])

        small = sb("small", [P, 80])
        ob = sb("ob", [P, TC, P])
        yb = Vt[:].rearrange("p c j -> p (c j)")
        guard = nc.sbuf_tensor("act_b", [P, 2 * KD, T], F32R)
        act_b = guard.__enter__()
        guard.__exit__(None, None, None)
        selb = sb("selb", [P, SEL_AT[TC]])
        pT = sb("pT", [P, TC, T])
        cbias = sb("cbias", [P, T])
        vraw = sb("vraw", [P, T])
        pw = sb("pw", [P, 2, P])
        gfin = sb("gfin", [P, D])
        wk = sb("wk", [P, D])
        frow = sb("frow", [HX, 2, T])

        outs = gate[:].rearrange("p (c a) t -> p c (a t)", c=TC)

        def slot(n):
            return act_a[:, n, :] if n < SLOTS_A else act_b[:, n - SLOTS_A, :]

        def flat(t):
            return t[:].rearrange("p c j -> p (c j)")

        def ring(g, what):
            return gate[:, 4 * (g % 2) + what, :]

        vt = (Kt, Vt)
        iq = (flat(KT), flat(QT))
        ikz = (flat(dec), flat(LT), flat(AT), flat(Ti))
        iwff = Ui
        relu = (flat(Yb), zs[:])
        prob = (qc[:], kc[:], flat(Yb), zs[:])
        sg = (vc, cx)
        ot = ca
        pvb = flat(KT)
        wins = ((flat(QT), flat(dec)), (flat(LT), flat(AT)))

        gb = ctx.enter_context(nc.psum_tensor("gb", [P, 4, T], F32))
        gd = ctx.enter_context(nc.psum_tensor("gd", [P, 4, T], F32))

        xin = gate[:].rearrange("p (c a) t -> p c (a t)", c=TC)
        prow = Kt[:].rearrange("p c j -> p (c j)")

        def wide(ap):
            return ap.unsqueeze(2).to_broadcast([P, TC, P])

        def over(ap):
            return ap.unsqueeze(1).to_broadcast([P, TC, P])

        def halved(ap, l, right=0):
            w = 2 << l
            v = ap.rearrange("p (b j) -> p b j", j=2 * w)
            return v[:, :, right * w:right * w + w]

        def bank(t):
            return t.rearrange("p (c j) -> p c j", c=TC)

        raw_landed = [sem(f"raw_landed{i}") for i in range(4)]
        hi_ready = sem("hi_ready")
        split_ready = sem("split_ready")
        unit_done = sem("unit_done")
        out_read = sem("out_read")
        x_landed = [sem(f"x_landed{i}") for i in range(KD // 2)]
        par_landed = sem("par_landed")
        prow_clear = sem("prow_clear")
        pool_order = sem("pool_order")
        dve_order = sem("dve_order")
        masks_ready = sem("masks_ready")
        x_turned = sem("x_turned")
        xT_ready = sem("xT_ready")
        par_turned = sem("par_turned")
        par_ready = sem("par_ready")
        xsq_ready = sem("xsq_ready")
        xsq_used = sem("xsq_used")
        xss_ready = sem("xss_ready")
        sq_added = sem("sq_added")
        xr_ready = sem("xr_ready")
        xrb_ready = sem("xrb_ready")
        xrb_kept = sem("xrb_kept")
        hn_ready = sem("hn_ready")
        hn_hi = sem("hn_hi")
        h_ready = sem("h_ready")
        ab_ready = sem("ab_ready")
        ab_turned = sem("ab_turned")
        abt_ready = sem("abt_ready")
        ab_exp = sem("ab_exp")
        ab_g = sem("ab_g")
        gcum_done = sem("gcum_done")
        gcum_sb = sem("gcum_sb")
        cols_exp = sem("cols_exp")
        taps_ready = sem("taps_ready")
        tap_first = sem("tap_first")
        conv_done = sem("conv_done")
        conv_silu = sem("conv_silu")
        z_ready = sem("z_ready")
        ga_ready = sem("ga_ready")
        cg_ready = sem("cg_ready")
        cg_copied = sem("cg_copied")
        ya_ready = sem("ya_ready")
        ya_hi = sem("ya_hi")
        ya_lo = sem("ya_lo")
        hc_ready = sem("hc_ready")
        kq_turned = sem("kq_turned")
        sq_ready = sem("sq_ready")
        ss_ready = sem("ss_ready")
        r_ready = sem("r_ready")
        gb_done = sem("gb_done")
        arg_ready = sem("arg_ready")
        dec_ready = sem("dec_ready")
        decb_ready = sem("decb_ready")
        tok_ready = sem("tok_ready")
        back_done = sem("back_done")
        kt_ready = sem("kt_ready")
        kk_done = sem("kk_done")
        lt_ready = sem("lt_ready")
        u_ready = sem("u_ready")
        u_turned = sem("u_turned")
        t_first = sem("t_first")
        t_ready = sem("t_ready")
        v_turned = sem("v_turned")
        vtok_ready = sem("vtok_ready")
        y_done = sem("y_done")
        ym_ready = sem("ym_ready")
        z_done = sem("z_done")
        vn_done = sem("vn_done")
        vn_ready = sem("vn_ready")
        vd_ready = sem("vd_ready")
        av_done = sem("av_done")
        su_done = sem("su_done")
        s_ready = sem("s_ready")
        ks_done = sem("ks_done")
        rhs_ready = sem("rhs_ready")
        qs_ready = sem("qs_ready")
        o_ready = sem("o_ready")
        osq_ready = sem("osq_ready")
        oss_ready = sem("oss_ready")
        or_ready = sem("or_ready")
        on_ready = sem("on_ready")
        o_turned = sem("o_turned")
        yb_ready = sem("yb_ready")
        yb_hi = sem("yb_hi")
        yb_lo = sem("yb_lo")
        gb_tanh = sem("gb_tanh")
        mix_ready = sem("mix_ready")
        mix_hi = sem("mix_hi")
        mix_lo = sem("mix_lo")
        xT_norm = sem("xT_norm")
        up_first = sem("up_first")
        up_conv = sem("up_conv")
        up_silu = sem("up_silu")
        up_ready = sem("up_ready")
        up_hi = sem("up_hi")
        up_lo = sem("up_lo")
        iw_extra = sem("iw_extra")
        late_landed = sem("late_landed")
        late_clear = sem("late_clear")
        pads_ready = sem("pads_ready")
        z_read = sem("z_read")
        z_read_v = sem("z_read_v")
        iw_turned = sem("iw_turned")
        iw_split = sem("iw_split")
        f_exp = sem("f_exp")
        f_ready = sem("f_ready")
        f_cum = sem("f_cum")
        f_tok = sem("f_tok")
        f_turned = sem("f_turned")
        f_rows = sem("f_rows")
        f_put = [sem(f"f_put{g}") for g in range(3)]
        score_done = sem("score_done")
        relu_ready = sem("relu_ready")
        relu_used = sem("relu_used")
        sel_ready = sem("sel_ready")
        v_turn_done = sem("v_turn_done")
        v_ready = sem("v_ready")
        s_done = sem("s_done")
        max_ready = sem("max_ready")
        exp_ready = sem("exp_ready")
        p_ready = sem("p_ready")
        p_turned = sem("p_turned")
        pT_ready = sem("pT_ready")
        pv_done = sem("pv_done")
        ot_ready = sem("ot_ready")
        m_hi = sem("m_hi")
        m_lo = sem("m_lo")
        win_ready = sem("win_ready")
        pool_done = sem("pool_done")
        tile_done = sem("tile_done")
        osq = sem("osq")
        orr = sem("orr")
        outs_ready = sem("outs_ready")
        out_sent = sem("out_sent")

        def blocks(w):
            return w[0].rearrange("(k p) n -> p k n", p=P)

        w_in_v, w_a_v, w_b_v, w_o_v = blocks(w_in), blocks(w_a_out), blocks(w_b_out), blocks(w_o)
        w_up_v, w_dn_v = blocks(w_up), blocks(w_down)

        N_AB = 0
        N_B = 1
        N_C1 = N_B + 8 * HEADS
        N_C2 = N_C1 + KD
        N_D = N_C2 + 2 * KD
        N_UP = [N_D + KD, 0]
        N_DN = [N_UP[0] + 2 * FF_CUT[0], 0]
        N_UP[1] = N_DN[0] + 2 * KD
        N_DN[1] = N_UP[1] + 2 * FF_CUT[1]
        N_Z = N_DN[1] + 2 * KD
        N_W = N_Z + len(Z_UNITS)
        POOL_SPLITS = range(N_Z + 9, N_W)
        plan = schedule()
        R_C2 = KD
        R_D = R_C2 + KD
        R_UP = [R_D + KD, R_D + KD + FF_CUT[0] + KD]
        R_DN = [R_UP[0] + FF_CUT[0], R_UP[1] + FF_CUT[1]]
        B_COLS = (A_Q, A_K, A_V, A_CG, A_XV, A_BG, A_GA, A_Z)

        block = ctx.enter_context(nc.Block())

        @block.sync
        def _(sp):
            def load(n, i, src, k=KD):
                if not isinstance(n, int) or n >= 4:
                    sp.wait_ge(split_ready, n - 3)
                dst = raw[:, i % 4, 0:k * P].rearrange("p (k n) -> p k n", k=k)
                sp.dma_start(dst, src).then_inc(raw_landed[i % 4], 16)

            xv = x[0].rearrange("(c p) d -> p c d", p=P)
            for i in range(KD // 2):
                cols = slice(2 * P * i, 2 * P * (i + 1))
                sp.dma_start(xin[:, :, cols], xv[:, :, cols]).then_inc(x_landed[i], 16)
            sp.wait_ge(prow_clear, 1)
            r = 0
            for src, n in ((norm_mix_g[0], 8), (conv_a_w[0].rearrange("k c -> (k c)"), 24),
                           (gdn_conv_w[0].rearrange("k c -> (k c)"), 96), (norm_ffn_g[0], 8),
                           (ffn_conv_w[0].rearrange("k c -> (k c)"), 3 * 2 * FB), (norm_final_g, 8), (norm_g_2[0], 8),
                           (pool_scale_2[0], 2), (gdn_norm_g[0], 1)):
                v = src.rearrange("(r p) -> r p", p=P)
                done = 0
                while done < n:
                    m = min(n - done, P - r % P)
                    sp.dma_start(prow[r % P:r % P + m, r // P * P:r // P * P + P],
                                 v[done:done + m, :]).then_inc(par_landed, 16)
                    r, done = r + m, done + m
            assert r == R_END
            for src, at, n in ((gdn_A_log, 0, 8), (gdn_dt_bias, 8, 8), (fox_bf_2, 16, 6)):
                sp.dma_start(rows8[:, at:at + n], src.to_broadcast([P, n])).then_inc(par_landed, 16)
            load(N_AB, N_AB, w_in_v[:, :, A_AB:A_AB + P])

            past = sp.alloc_register("column")
            sp.reg_mov(past, 3 * P)

            def column(less):
                return ds(sp.snap(past) + less, P)

            def head_loads(h):
                for s in range(8):
                    load(N_B + 8 * h + s, N_B + s, w_in_v[:, :, column(B_COLS[s] - 3 * P)])
                sp.reg_add(past, past, P)

            head_loads(0)
            with sp.Fori(1, HEADS) as h:
                head_loads(h)
            for j in range(KD):
                load(N_C1 + j, N_C1 + j, w_a_v[:, :, j * P:j * P + P])
            sp.reg_mov(past, 3 * P)
            with sp.Fori(0, KD // 2) as i:
                for q in range(2):
                    for s, w, c in ((0, w_in_v, A_GB), (1, w_b_v, 0)):
                        load(N_C2 + 4 * i + 2 * q + s, N_C2 + 2 * q + s, w[:, :, column(c + q * P - 3 * P)])
                sp.reg_add(past, past, 2 * P)
            with sp.Fori(0, KD // 4) as i:
                for s in range(4):
                    load(N_D + 4 * i + s, N_D + s, w_o_v[:, :, ds(i * (4 * P) + s * P, P)])
            for f in range(2):
                with sp.Fori(0, FF_CUT[f] // 2) as i:
                    for q in range(2):
                        for s in range(2):
                            c = s * FF + (f * FF_CUT[0] + q) * P
                            load(N_UP[f] + 4 * i + 2 * q + s, N_UP[f] + 2 * q + s,
                                 w_up_v[:, :, ds(i * (2 * P) + c, P)])
                kh = FF_CUT[f] // 2
                with sp.Fori(0, KD // 2) as i:
                    for q in range(2):
                        for s in range(2):
                            k0 = f * FF_CUT[0] + s * kh
                            load(N_DN[f] + 4 * i + 2 * q + s, N_DN[f] + 2 * q + s,
                                 w_dn_v[:, k0:k0 + kh, ds(i * (2 * P) + q * P, P)], kh)

            w2 = w_in_2[0].rearrange("(k p) n -> p k n", p=P)
            for u, (what, g, c) in enumerate(Z_UNITS):
                n = N_Z + u
                if what == "thin":
                    sp.wait_ge(split_ready, n - 3)
                    dst = raw[:, n % 4, :].rearrange("p (k n) -> p k n", k=KD)
                    sp.dma_start(dst[:, :, 64:P], w2[:, :, B_END - 64:B_END]).then_inc(iw_extra, 16)
                    sp.wait_ge(iw_extra, 16)
                    sp.dma_start(dst[:, :, 0:64], w2[:, :, B_IK:B_IK + 64]).then_inc(raw_landed[n % 4], 16)
                else:
                    load(n, n, w2[:, :, c:c + P])
                if u == 6:
                    sp.wait_ge(late_clear, 1)
                    for i in range(4):
                        r = 64 * (i % 2)
                        sp.dma_start(pw[r:r + 64, i // 2, r:r + 64], pool_w_2[0, i]).then_inc(late_landed, 16)
                    sp.dma_start(gfin[:], final_g_2.rearrange("(a n) -> a n", a=1).to_broadcast([P, D])).then_inc(
                        late_landed, 16)
            for i, k in enumerate(W_ORDER):
                n = N_W + i
                sp.wait_ge(split_ready, n - 3)
                sp.dma_start(raw[:, n % 4, :], w_out_2[0, k * P:k * P + P, :]).then_inc(raw_landed[n % 4], 16)
            for c in range(TC):
                sp.wait_ge(outs_ready, c + 1)
                sp.dma_start(out[0, c * P:c * P + P, :], outs[:, c, :]).then_inc(out_sent, 16)
            sp.wait_ge(out_sent, 16 * TC)
        @block.tensor
        def _(pe):
            def unit(n, i, b, k0, rhs_hi, rhs_lo, kn=KD, first=True, last=True, parts=1, ready=None, high=None):
                pe.wait_ge(split_ready, n + 1)
                todo = []
                for k in range(kn):
                    hi = whi[:, i % 2, k * P:k * P + P]
                    lo = wlo[:, i % 2, k * P:k * P + P]
                    a, c = slot(rhs_hi + k0 + k), slot(rhs_lo + k0 + k)
                    todo += [(hi, a), (lo, a), (hi, c)]
                each = len(todo) // parts
                for m, (l, r) in enumerate(todo):
                    if high and m % 3 == 0:
                        pe.wait_ge(high[0], high[1] + m // 3 + 1)
                    if ready and m % 3 == (2 if high else 0):
                        pe.wait_ge(ready[0], ready[1] + m // 3 + 1)
                    ins = pe.matmul(gb[:, b, :], l, r, start=(first and m == 0), stop=(last and m == len(todo) - 1))
                    if m == len(todo) - 1:
                        ins.then_inc(unit_done, 1)
                    if (m + 1) % each == 0:
                        yield

            def whole(*a, **k):
                for _ in unit(*a, **k):
                    pass

            def norm_sum(squares, start, stop, b=0):
                return pe.matmul(gd[:, b, :], ones[:], squares, start=start, stop=stop)

            def norm_spread(n, factors=4, b=1):
                pe.wait_ge(xr_ready, n + 1)
                for c in range(TC):
                    ins = pe.matmul(gd[:, b, c * P:c * P + P], rr[:, factors, c:c + 1].to_broadcast([P, P]), ident[:],
                                    start=True, stop=True)
                ins.then_inc(xrb_ready, 1)

            pe.wait_ge(masks_ready, 1)
            for k in range(KD):
                if k % 2 == 0:
                    pe.wait_ge(x_landed[k // 2], 16)
                if k >= 2:
                    pe.wait_ge(xT_ready, k - 1)
                for c in range(TC):
                    ins = pe.transpose(gd[:, 2 + k % 2, c * P:c * P + P], xin[:, c, k * P:k * P + P], ident[:])
                ins.then_inc(x_turned, 1)
                if k == 1:
                    pe.wait_ge(masks_ready, 2)
                if k:
                    pe.wait_ge(xsq_ready, k)
                    norm_sum((cx, ca)[(k - 1) % 2][:], k == 1, False).then_inc(xsq_used, 1)
            pe.wait_ge(par_landed, 16 * PAR_DMAS)
            for r in range((R_END + P - 1) // P):
                m = min(P, R_END - r * P)
                ins = pe.transpose(gd[:, 1, r * P:r * P + m], prow[0:m, r * P:r * P + P], ident[0:m, 0:m])
            ins.then_inc(par_turned, 1)
            pe.wait_ge(xsq_ready, KD)
            norm_sum(ca[:], False, True).then_inc(xsq_used, 1)
            pe.wait_ge(par_ready, 1)
            norm_spread(0)

            whole(N_AB, N_AB, 3, 0, H_HI, H_LO, ready=(h_ready, 0), high=(hn_hi, 0))
            whole(N_B, N_B, 0, 0, H_HI, H_LO)
            pe.wait_ge(ab_ready, 1)
            for c in range(TC):
                ins = pe.transpose(gd[:, 0, c * P:c * P + P], Yb[:, c, :], ident[:])
            ins.then_inc(ab_turned, 1)

            def step(g, h):
                if g == 0:
                    pe.wait_ge(conv_silu, 3 * h + 2)
                    for c in range(TC):
                        ins = pe.transpose(gd[:, 0, c * P:c * P + P], kc[:, c * P:c * P + P], ident[:])
                    ins.then_inc(kq_turned, 1)
                    for c in range(TC):
                        ins = pe.transpose(gd[:, 1, c * P:c * P + P], qc[:, c * P:c * P + P], ident[:])
                    ins.then_inc(kq_turned, 1)
                elif g == 1:
                    pe.wait_ge(hc_ready, h + 1)
                    for c in range(TC):
                        ins = pe.matmul(gd[:, 3, c * P:c * P + P], hc[:, C_G + c:C_G + c + 1].to_broadcast([P, P]),
                                        ident[:], start=True, stop=True)
                    ins.then_inc(gb_done, 1)
                elif g == 3:
                    for i, src in ((0, Kt), (1, Yb)):
                        pe.wait_ge(tok_ready, 2 * h + 1 + i)
                        for c in range(TC):
                            ins = pe.transpose(gd[:, i, c * P:c * P + P], src[:, c, :], ident[:])
                        ins.then_inc(back_done, 1)
                elif g == 4:
                    pe.wait_ge(kt_ready, 2 * h + 1)
                    if not (isinstance(h, int) and h == 0):
                        pe.wait_ge(yb_ready, h)
                    for c in range(TC):
                        ins = pe.matmul(gd[:, 2, c * P:c * P + P], KT[:, c, :], KT[:, c, :], start=True, stop=True)
                    ins.then_inc(kk_done, 1)
                    pe.wait_ge(kt_ready, 2 * h + 2)
                    pe.wait_ge(arg_ready, h + 1)
                    for c in range(TC):
                        ins = pe.matmul(gd[:, 3, c * P:c * P + P], KT[:, c, :], QT[:, c, :], start=True, stop=True)
                    ins.then_inc(kk_done, 1)
                elif g == 33:
                    pe.wait_ge(conv_silu, 3 * h + 3)
                    pe.wait_ge(t_ready, 5 * h + 5)
                    for c in range(TC):
                        ins = pe.transpose(gd[:, 1, c * P:c * P + P], vc[:, c * P:c * P + P], ident[:])
                    ins.then_inc(v_turned, 1)
                elif g == 6:
                    pe.wait_ge(u_ready, 7 * h + 1)
                    pe.wait_ge(lt_ready, 2 * h + 2)
                    for c in range(TC):
                        ins = pe.transpose(gd[:, 3, c * P:c * P + P], Ui[:, c, :], ident[:])
                    ins.then_inc(u_turned, 1)
                elif 7 <= g <= 18 and g % 2:
                    l = (g - 7) // 2
                    if l == 0:
                        pe.wait_ge(t_first, h + 1)
                    else:
                        pe.wait_ge(t_ready, 5 * h + l)
                    for c in range(TC):
                        ins = pe.matmul(halved(gd[:, 0, c * P:c * P + P], l), LT[:, c, :], halved(Ti[:, c, :], l),
                                        start=True, stop=True)
                    ins.then_inc(y_done, 1)
                elif 7 <= g <= 18:
                    l = (g - 8) // 2
                    pe.wait_ge(ym_ready, 6 * h + l + 1)
                    if l < 5:
                        for c in range(TC):
                            pe.matmul(halved(gd[:, 1, c * P:c * P + P], l), Ui[:, c, :], halved(Yb[:, c, :], l),
                                      start=True, stop=True)
                    for c in range(TC):
                        ins = pe.matmul(halved(gd[:, 2, c * P:c * P + P], l, 1), Yb[:, c, :], halved(Ui[:, c, :], l, 1),
                                        start=True, stop=True)
                    ins.then_inc(z_done, 1)
                elif 19 <= g <= 29:
                    c = (g - 18) // 3
                    what = (g - 18) % 3
                    if what == 0:
                        pe.wait_ge(s_ready, 3 * h + c)
                        pe.matmul(gd[:, 0, 0:P], KT[:, c, :], S[:], start=True, stop=True)
                        pe.matmul(gd[:, 0, P:2 * P], QT[:, c, :], S[:], start=True, stop=True).then_inc(ks_done, 1)
                    elif what == 1:
                        if c == 0:
                            pe.wait_ge(u_ready, 7 * h + 7)
                            pe.wait_ge(vtok_ready, h + 1)
                            rhs = Vt[:, 0, :]
                        else:
                            pe.wait_ge(rhs_ready, 3 * h + c)
                            rhs = Rr[:]
                        pe.matmul(gd[:, 3, 0:P], Ui[:, c, :], rhs, start=True, stop=True).then_inc(vn_done, 1)
                    else:
                        if c < TC - 1:
                            pe.wait_ge(vd_ready, 3 * h + c + 1)
                            pe.matmul(gd[:, 2, 0:P], Kt[:, c, :], vd[:], start=True, stop=True).then_inc(su_done, 1)
                        pe.wait_ge(vn_ready, 4 * h + c + 1)
                        if c >= 1:
                            pe.wait_ge(o_ready, 4 * h + c)
                        pe.matmul(gd[:, 1, 0:P], AT[:, c, :], vn[:], start=True, stop=True).then_inc(av_done, 1)
                elif g == 32:
                    pe.wait_ge(on_ready, h + 1)
                    for c in range(TC):
                        ins = pe.transpose(gd[:, 2, c * P:c * P + P], ob[:, c, :], ident[:])
                    ins.then_inc(o_turned, 1)

            def head(h, peeled):
                for s in range(8):
                    if peeled and s == 0:
                        continue
                    if s >= 4:
                        free, count = ((conv_done, 3 * h + 1), (conv_done, 3 * h + 2), (conv_done, 3 * h + 3),
                                       (cg_copied, h + 1))[s - 4]
                        pe.wait_ge(free, count)
                    elif not peeled:
                        pe.wait_ge((cg_ready, ya_ready, ga_ready, z_ready)[s], h)
                    elif s == 3:
                        pe.wait_ge(ab_ready, 1)
                    u = unit(N_B + 8 * h + s, N_B + s, s % 4, 0, H_HI, H_LO, parts=4)
                    for m in range(4):
                        next(u)
                        if peeled and s == 1 and m == 3:
                            pe.wait_ge(ab_g, 1)
                            pe.matmul(gd[:, 0, 0:HEADS * TC], triu[:], sm[:, 0, 0:HEADS * TC], start=True, stop=True)
                            pe.matmul(gd[:, 0, P:P + HEADS * TC], ones[:], sm[:, 0, 0:HEADS * TC],
                                      start=True, stop=True).then_inc(gcum_done, 1)
                        if s == 3 and m == 1 and not peeled:
                            step(32, h - 1)
                        if s >= 3:
                            step((s - 3) * 4 + m, h)
                        elif not peeled:
                            step(20 + s * 4 + m, h - 1)
                        if s == 7 and m == 1:
                            step(33, h)
                    for _ in u:
                        pass

            head(0, True)
            with pe.Fori(1, HEADS) as h:
                head(h, False)

            pe.wait_ge(ya_lo, HEADS)
            for j in range(KD):
                if j < 4:
                    pe.wait_ge((cg_ready, ya_ready, ga_ready, z_ready)[j], HEADS)
                else:
                    pe.wait_ge(out_read, j - 3)
                u = unit(N_C1 + j, N_C1 + j, j % 4, 0, YA_HI, YA_LO, parts=4)
                for m in range(4):
                    next(u)
                    if j < 3:
                        step(20 + j * 4 + m, HEADS - 1)
                    elif j == 3 and m == 2:
                        step(32, HEADS - 1)
                for _ in u:
                    pass
            with pe.Fori(0, KD // 2) as i:
                for q in range(2):
                    pe.wait_ge(out_read, 2 * i + (R_C2 + q - 1))
                    whole(N_C2 + 4 * i + 2 * q, N_C2 + 2 * q, 2 * q, 0, H_HI, H_LO)
                    pe.wait_ge(yb_lo, HEADS)
                    whole(N_C2 + 4 * i + 2 * q + 1, N_C2 + 2 * q + 1, 2 * q + 1, 0, YB_HI, YB_LO)
            for j in range(KD):
                pe.wait_ge(out_read, R_D + (j - 3 if j >= 4 else -1 if j < 2 else 0))
                whole(N_D + j, N_D + j, j % 4, 0, MIX_HI, MIX_LO, ready=(mix_lo, 0) if j == 0 else None)
            pe.wait_ge(sq_added, KD - 2)
            norm_sum(zs[:], True, False)
            pe.wait_ge(xsq_ready, 2 * KD)
            norm_sum(ca[:], False, True).then_inc(xsq_used, 1)
            norm_spread(1)

            def down(f, i):
                kh = FF_CUT[f] // 2
                for q in range(2):
                    pe.wait_ge(out_read, 2 * i + (R_DN[f] + q - 1))
                    for s in range(2):
                        if s == 0:
                            pe.wait_ge(up_lo, f * FF_CUT[0] + kh)
                        whole(N_DN[f] + 4 * i + 2 * q + s, N_DN[f] + 2 * q + s, q,
                              s * kh, FF_HI, FF_LO, kn=kh, first=(s == 0), last=(s == 1),
                              ready=(up_lo, f * FF_CUT[0] + kh) if q == 0 and s == 1 else None)

            for f in range(2):
                with pe.Fori(0, FF_CUT[f] // 2) as i:
                    for q in range(2):
                        pe.wait_ge(out_read, 2 * i + (R_UP[f] + q - 1))
                        for s in range(2):
                            if s:
                                pe.wait_ge(out_read, R_UP[f])
                            whole(N_UP[f] + 4 * i + 2 * q + s, N_UP[f] + 2 * q + s, 2 * q + s, 0, H_HI, H_LO,
                                  ready=(h_ready, KD) if f == q == s == 0 else None,
                                  high=(hn_hi, KD) if f == q == s == 0 else None)
                with pe.Fori(0, KD // 2) as i:
                    down(f, i)
            pe.wait_ge(sq_added, 3 * (KD - 2))
            norm_sum(zs[:], True, False)
            norm_sum(flat(Kt), True, False, 2)
            pe.wait_ge(xsq_ready, 4 * KD - 1)
            norm_sum(ca[:], False, True).then_inc(xsq_used, 1)
            pe.wait_ge(xsq_ready, 4 * KD)
            norm_sum(flat(QT), False, True, 2).then_inc(xsq_used, 1)
            norm_spread(2, 5, 3)
            norm_spread(3)


            def beside(e):
                what = e[0]
                if what == "turn_iw":
                    pe.wait_ge(z_read, 1)
                    for c in range(TC):
                        ins = pe.transpose(gd[:, 2, c * P:c * P + P], flat(iwff)[:, c * P:c * P + P], ident[:])
                    ins.then_inc(iw_turned, 1)
                elif what == "cum_f":
                    pe.wait_ge(f_ready, 1)
                    pe.matmul(gd[:, 3, 0:HX * TC], triu[:], sm[:, 0, 0:HX * TC], start=True, stop=False)
                    pe.matmul(gd[:, 3, 0:HX * TC], ones[:], sm[:, 1, 0:HX * TC], start=False, stop=True).then_inc(f_cum, 1)
                elif what == "turn_f":
                    pe.wait_ge(f_tok, 1)
                    for c in range(TC):
                        ins = pe.transpose(gd[0:HX, 2, c * P:c * P + P], sm[:, 2, c * HX:c * HX + HX], ident[:])
                    ins.then_inc(f_turned, 1)
                elif what == "score":
                    _, n, c, h = e
                    pe.wait_ge(z_read, 3)
                    if n >= 2:
                        pe.wait_ge(relu_ready, n - 1)
                    pe.matmul(gd[:, n % 2, 0:(c + 1) * P], iq[h // 4][:, c * P:c * P + P], ikz[h % 4][:, 0:(c + 1) * P],
                              start=True, stop=True).then_inc(score_done, 1)
                elif what == "turn_v":
                    g = e[1]
                    pe.wait_ge(z_read, V_READ[g])
                    if g == 0:
                        pe.wait_ge(f_rows, 1)
                    else:
                        pe.wait_ge(pT_ready, TC * 2 * g + (TC - 1 if g == GROUPS - 1 else 0))
                    for c in range(TC):
                        ins = pe.transpose(gd[:, 2, c * P:c * P + P], vraw[:, c * P:c * P + P], ident[:])
                    ins.then_inc(v_turn_done, 1)
                elif what == "s":
                    _, c, t = e
                    g, i = t // 2, t % 2
                    if c == 0:
                        pe.wait_ge(z_read, Q_READ[g])
                        pe.wait_ge(z_read_v, g + 1)
                        if g < 3:
                            pe.wait_ge(f_put[g], 64)
                        if t == 0:
                            pe.wait_ge(relu_ready, (TC - 1) * IDX_HEADS)
                    n = TC * t + c
                    if n >= 2:
                        pe.wait_ge(exp_ready, n - 1)
                    q = ring(g, i if g < 3 else 0)
                    pe.matmul(gd[:, c % 2, 0:(c + 1) * P], q[:, c * P:c * P + P], ring(g, 2 + i)[:, 0:(c + 1) * P],
                              start=True, stop=True).then_inc(s_done, 1)
                elif what == "t":
                    _, c, t = e
                    n = TC * t + c
                    pe.wait_ge(p_ready, n + 1)
                    if n >= 1:
                        pe.wait_ge(pT_ready, n)
                    pe.wait_ge(v_ready, t // 2 + (0 if t == 2 * GROUPS - 2 and c < TC - 1 else 1))
                    for j in range(c + 1):
                        ins = pe.transpose(gd[:, 2, j * P:j * P + P], prob[c][:, j * P:j * P + P], ident[:])
                    ins.then_inc(p_turned, 1)
                elif what == "pv":
                    t = e[2]
                    g, i = t // 2, t % 2
                    pe.wait_ge(pT_ready, TC * (t + 1))
                    pe.wait_ge(v_ready, g + 1)
                    if g and i == 0:
                        pe.wait_ge(ot_ready, g)
                    for j in range(TC):
                        ins = pe.matmul(gd[64 * i:64 * i + 64, 3, j * P:T], vt[g % 2][:, j, 64 * i:64 * i + 64],
                                        pT[:, j, j * P:T], start=(j == 0), stop=(j == TC - 1))
                    ins.then_inc(pv_done, 1)
                elif what == "pool":
                    b = e[1]
                    pe.wait_ge(win_ready, b + 1)
                    pe.wait_ge(late_landed, 16 * 5)
                    pe.wait_ge(z_read, (V_READ, G_READ)[b][GROUPS - 1])
                    pe.matmul(gb[:, (len(Z_UNITS) - 4 + b) % 4, :], pw[:, b, :], wins[b][0], start=True, stop=True).then_inc(pool_done, 1)

            for u in range(len(Z_UNITS)):
                if u >= 4:
                    reader, count = Z_READER[u - 4]
                    pe.wait_ge({"act": z_read, "dve": z_read_v}[reader], count)
                if u == 1:
                    pe.wait_ge(pads_ready, 1)
                p = unit(N_Z + u, N_Z + u, u % 4, 0, H_HI, H_LO, parts=4, 
                         ready=(h_ready, 2 * KD) if u == 0 else None, high=(hn_hi, 2 * KD) if u == 0 else None)
                for m in range(4):
                    next(p)
                    for e in plan.get((u, m), ()):
                        beside(e)
                for _ in p:
                    pass
            for e in plan[(len(Z_UNITS), 0)]:
                beside(e)
            def place(c, half):
                b = 2 * c + half
                return gb[:, b, :] if b < 4 else gd[:, b - 4, :]

            pe.wait_ge(xT_norm, KD)
            for c in (2, 3, 1, 0):
                pe.wait_ge(*((ot_ready, GROUPS + 2), (ot_ready, GROUPS + 2), (exp_ready, TC * 2 * GROUPS),
                             (ot_ready, GROUPS))[c])
                for half in range(2):
                    for j in range(4):
                        pe.matmul(place(c, half)[:, j * P:j * P + P], xT[:, 4 * half + j, c * P:c * P + P], ident[:],
                                  start=(j == 0), stop=False, skip_group_check=True)
            for i, k in enumerate(W_ORDER):
                n = N_W + i
                pe.wait_ge(split_ready, n + 1)
                pe.wait_ge(m_lo, i + 1)
                for c in range(TC):
                    hi = act_a[:, MIX_HI + k, c * P:c * P + P]
                    lo = act_a[:, MIX_LO + k, c * P:c * P + P]
                    for half in range(2):
                        wh = whi[:, n % 2, half * T:half * T + T]
                        wl = wlo[:, n % 2, half * T:half * T + T]
                        for m, (l, r) in enumerate(((hi, wh), (lo, wh), (hi, wl))):
                            ins = pe.matmul(place(c, half), l, r, start=False, stop=(i == KD - 1 and m == 2),
                                            skip_group_check=True)
                    if i == KD - 1:
                        ins.then_inc(tile_done, 1)
                    elif c == TC - 1:
                        ins.then_inc(unit_done, 1)

        @block.scalar
        def _(sc):
            def split(n, i, k=KD):
                sc.wait_ge(raw_landed[i % 4], (n + 4 - i % 4) * 4)
                if not isinstance(n, int) or n >= 2:
                    sc.wait_ge(unit_done, n - 1)
                sc.activation(whi[:, i % 2, 0:k * P], raw[:, i % 4, 0:k * P], ACT.Copy).then_inc(hi_ready, 1)

            def norm_square(dst, src, gain=1.0):
                sc.activation(dst, src, ACT.Square, scale=gain).then_inc(xsq_ready, 1)

            def norm_split(norm):
                for k in range(KD):
                    sc.wait_ge(hn_ready, KD * norm + k + 1)
                    sc.activation(act_a[:, H_HI + k, :], (qc, kc, vc)[k % 3][:], ACT.Copy).then_inc(hn_hi, 1)

            for k in range(KD):
                sc.wait_ge(x_turned, k + 1)
                sc.activation(xT[:, k, :], gd[:, 2 + k % 2, :], ACT.Copy).then_inc(xT_ready, 1)
                sc.wait_ge(xT_ready, k + 1)
                if k >= 2:
                    sc.wait_ge(xsq_used, k - 1)
                norm_square((cx, ca)[k % 2][:], xT[:, k, :])
            split(N_AB, N_AB)
            split(N_B, N_B)
            norm_split(0)
            sc.wait_ge(unit_done, 1)
            sc.activation(Yb[:].rearrange("p c j -> p (c j)"), gb[:, 3, :], ACT.Copy).then_inc(ab_ready, 1)
            split(N_B + 1, N_B + 1)
            sc.wait_ge(abt_ready, 1)
            sc.activation(sm[:, 3, 0:32], sm[:, 2, 0:32], ACT.Exp, scale=-1.0)
            sc.activation(sm[:, 3, 32:64], sm[:, 2, 32:64], ACT.Exp, scale=-1.0)
            sc.activation(sm[:, 4, 0:HEADS], rows8[:, 0:HEADS], ACT.Exp).then_inc(ab_exp, 1)
            def decay_exps():
                sc.wait_ge(gcum_sb, 1)
                sc.activation(sm[:, 8, 0:32], sm[:, 5, 0:32], ACT.Exp)
                sc.activation(sm[:, 9, 0:32], sm[:, 6, 0:32], ACT.Exp)
                sc.activation(sm[:, 10, 0:32], sm[:, 7, 0:32], ACT.Exp).then_inc(cols_exp, 1)

            def step(g, h):
                if g == 0:
                    for i, dst in ((0, Ti), (1, Ui)):
                        sc.wait_ge(kq_turned, 2 * h + 1 + i)
                        sc.activation(dst[:], bank(gd[:, i, :]), ACT.Square).then_inc(sq_ready, 1)
                elif g == 2:
                    sc.wait_ge(arg_ready, h + 1)
                    sc.activation(dec[:], dec[:], ACT.Exp).then_inc(dec_ready, 1)
                elif g == 3:
                    for i, dst in ((0, KT), (1, QT)):
                        sc.wait_ge(back_done, 2 * h + 1 + i)
                        sc.activation(dst[:], bank(gd[:, i, :]), ACT.Copy,
                                      scale=(1.0, float(P) ** -0.5)[i]).then_inc(kt_ready, 1)
                elif g == 33:
                    sc.wait_ge(v_turned, h + 1)
                    if not (isinstance(h, int) and h == 0):
                        sc.wait_ge(yb_lo, h)
                    sc.activation(Vt[:], bank(gd[:, 1, :]), ACT.Copy).then_inc(vtok_ready, 1)
                elif g == 6:
                    sc.wait_ge(u_turned, h + 1)
                    sc.activation(Ti[:], bank(gd[:, 3, :]), ACT.Copy).then_inc(t_first, 1)
                elif 19 <= g <= 29:
                    c = (g - 18) // 3
                    what = (g - 18) % 3
                    if what == 0:
                        sc.wait_ge(rhs_ready, 3 * h + c)
                        sc.activation(ob[:, c, :], gd[:, 0, P:2 * P], ACT.Copy, scale=hc[:, C_E + c:C_E + c + 1]).then_inc(qs_ready, 1)
                    elif what == 1:
                        sc.wait_ge(vn_done, 4 * h + c + 1)
                        if c < TC - 1:
                            sc.activation(vd[:], gd[:, 3, 0:P], ACT.Copy,
                                          scale=hc[:, C_BKD + c:C_BKD + c + 1]).then_inc(vd_ready, 1)
                        sc.activation(vn[:], gd[:, 3, 0:P], ACT.Copy, scale=hc[:, C_BETA + c:C_BETA + c + 1]).then_inc(vn_ready, 1)
                elif g == 30:
                    sc.wait_ge(o_ready, 4 * h + 4)
                    sc.activation(yb, flat(ob), ACT.Square).then_inc(osq_ready, 1)
                elif g == 32:
                    sc.wait_ge(yb_ready, h + 1)
                    sc.activation(act_b[:, ds(h + (YB_HI - SLOTS_A), 1), :].rearrange("p a t -> p (a t)"),
                                  yb, ACT.Copy).then_inc(yb_hi, 1)

            def first_half(h, s):
                sc.wait_ge(unit_done, N_B + 8 * h + s + 1)
                if s < 3:
                    if s == 0:
                        sc.wait_ge(taps_ready, h + 1)
                    sc.activation((qc, kc, vc)[s][:], gb[:, s, :], ACT.Copy,
                                  scale=hw[:, 4 * s + 3:4 * s + 4]).then_inc(tap_first, 1)
                elif s == 3:
                    if not (isinstance(h, int) and h == 0):
                        sc.wait_ge(ya_lo, h)
                    sc.activation(cx[:], gb[:, 3, :], ACT.Copy).then_inc(cg_copied, 1)
                elif s == 6:
                    sc.activation(gate[:, ds(h, 1), :].rearrange("p a t -> p (a t)"), gb[:, 2, :], ACT.Tanh,
                                  scale=0.5).then_inc(ga_ready, 1)
                elif s == 7:
                    if not (isinstance(h, int) and h == 0):
                        sc.wait_ge(yb_ready, h)
                    sc.activation(zs[:], gb[:, 3, :], ACT.Silu).then_inc(z_ready, 1)

            def second_half(h, s):
                if s < 3:
                    sc.wait_ge(conv_done, 3 * h + s + 1)
                    dst = (qc, kc, vc)[s]
                    sc.activation(dst[:], dst[:], ACT.Silu).then_inc(conv_silu, 1)
                elif s == 5:
                    sc.wait_ge(ya_ready, h + 1)
                    sc.activation(act_a[:, ds(h + YA_HI, 1), :].rearrange("p a t -> p (a t)"), ca[:],
                                  ACT.Copy).then_inc(ya_hi, 1)

            def head(h, peeled):
                for s in range(8):
                    if not (peeled and s == 0):
                        split(N_B + 8 * h + s + 1, N_B + s + 1)
                    if peeled and s == 2:
                        decay_exps()
                    for m in range(4):
                        if m == 1:
                            if s > 0:
                                first_half(h, s - 1)
                            elif not peeled:
                                first_half(h - 1, 7)
                        if m == 3 and s > 0 and s != 3:
                            second_half(h, s - 1)
                        if s >= 3:
                            step((s - 3) * 4 + m, h)
                        elif not peeled:
                            step(20 + s * 4 + m, h - 1)
                        if s == 3 and m == 2 and not peeled:
                            step(32, h - 1)
                        if s == 4 and m == 3:
                            second_half(h, 2)
                        if s == 7 and m == 2:
                            step(33, h)

            head(0, True)
            with sc.Fori(1, HEADS) as h:
                head(h, False)
            for j in range(KD):
                split(N_C1 + j + 1, N_C1 + j + 1)
                for m in range(4):
                    if j == 0 and m == 1:
                        first_half(HEADS - 1, 7)
                    if j < 3:
                        step(20 + j * 4 + m, HEADS - 1)
                    elif j == 3 and m == 2:
                        step(32, HEADS - 1)
            split(N_C2 + 1, N_C2 + 1)
            with sc.Fori(0, KD // 2) as i:
                for q in range(2):
                    sc.wait_ge(unit_done, N_C2 + 4 * i + 2 * q + 1)
                    sc.activation((qc, kc)[q][:], gb[:, 2 * q, :], ACT.Tanh, scale=0.5).then_inc(gb_tanh, 1)
                    split(N_C2 + 4 * i + 2 * q + 2, N_C2 + 2 * q + 2)
                    sc.wait_ge(mix_ready, 2 * i + q + 1)
                    sc.activation(act_a[:, ds(2 * i + (MIX_HI + q), 1), :].rearrange("p a t -> p (a t)"), (qc, kc)[q][:],
                                  ACT.Copy, scale=0.5).then_inc(mix_hi, 1)
                    split(N_C2 + 4 * i + 2 * q + 3, N_C2 + 2 * q + 3)
            for j in range(KD):
                if j < KD - 1:
                    split(N_D + j + 2, N_D + j + 2)
                sc.wait_ge(out_read, R_D + j + 1)
                if j >= 3:
                    sc.wait_ge(sq_added, j - 2)
                norm_square((cx, ca)[j % 2][:] if j else zs[:], xT[:, j, :])
            split(N_D + KD + 1, N_D + KD + 1)
            norm_split(1)
            for f in range(2):
                with sc.Fori(0, FF_CUT[f] // 2) as i:
                    for q in range(2):
                        for s in range(2):
                            j = 2 * i + (f * FF_CUT[0] + q)
                            sc.wait_ge(unit_done, N_UP[f] + 4 * i + 2 * q + s + 1)
                            dst = ((qc, kc), (vc, cx))[q][s]
                            sc.activation(dst[:], gb[:, 2 * q + s, :], ACT.Copy,
                                          scale=par[:, ds(2 * i + (R_CONV_F + 2 * 2 * FB + s * FB + f * FF_CUT[0] + q), 1)]
                                          ).then_inc(up_first, 1)
                            split(N_UP[f] + 4 * i + 2 * q + s + 2, N_UP[f] + 2 * q + s + 2)
                            if s == 0:
                                sc.wait_ge(up_conv, j + 1)
                                sc.activation(dst[:], dst[:], ACT.Silu).then_inc(up_silu, 1)
                            else:
                                sc.wait_ge(up_ready, j + 1)
                                sc.activation(act_a[:, ds(2 * i + (FF_HI + q), 1), :].rearrange("p a t -> p (a t)"),
                                              (qc, vc)[q][:], ACT.Copy).then_inc(up_hi, 1)
                if f == 0:
                    with sc.Fori(0, KD // 2) as i:
                        for s in range(4):
                            split(N_DN[f] + 4 * i + s + 2, N_DN[f] + s + 2)
                else:
                    for j in range(KD):
                        for s in range(2 if j < KD - 1 else 1):
                            split(N_DN[1] + 2 * j + s + 2, N_DN[1] + 2 * j + s + 2)
                        sc.wait_ge(out_read, R_DN[1] + j + 1)
                        if j >= 3:
                            sc.wait_ge(sq_added, KD - 2 + 2 * (j - 2))
                        norm_square((cx, ca)[j % 2][:] if j else zs[:], xT[:, j, :])
                        norm_square(flat((KT, QT)[j % 2]) if j else flat(Kt), xT[:, j, :],
                                    par[:, R_FIN_G + j:R_FIN_G + j + 1])
                    split(N_DN[1] + 2 * KD + 1, N_DN[1] + 2 * KD + 1)
            sc.wait_ge(xrb_ready, 4)
            sc.activation(flat(Vt), gd[:, 1, :], ACT.Copy).then_inc(xrb_kept, 1)
            norm_split(2)

            sc.wait_ge(pads_ready, 1)

            def z_out(u):
                what, g, _ = Z_UNITS[u]
                src = gb[:, u % 4, :]
                sc.wait_ge(unit_done, N_Z + u + 1)
                if what == "thin":
                    for i in range(4):
                        sc.activation(ikz[i][32 * i:32 * i + 32, :], src[0:32, :], ACT.Copy)
                    sc.activation(flat(iwff), src, ACT.Copy).then_inc(z_read, 1)
                elif what == "iq":
                    sc.activation(iq[g], src, ACT.Copy).then_inc(z_read, 1)
                elif what == "q" and g < 3:
                    if g == 2:
                        sc.wait_ge(s_done, TC * 2)
                    for i in range(2):
                        r = slice(64 * i, 64 * i + 64)
                        ins = sc.activation(ring(g, i)[r, :], src[r, :], ACT.Copy, scale=0.125)
                    ins.then_inc(z_read, 1)
                elif what == "q":
                    sc.wait_ge(s_done, TC * 2 * (g - 1))
                    sc.activation(ring(g, 0), src, ACT.Copy, scale=0.125).then_inc(z_read, 1)
                elif what == "v":
                    if g:
                        sc.wait_ge(v_turn_done, g)
                    sc.activation(vraw[:], src, ACT.Copy).then_inc(z_read, 1)
                elif what == "g":
                    if g >= 2:
                        sc.wait_ge(ot_ready, g - 1)
                    sc.activation(sg[g % 2][:], src, ACT.Silu).then_inc(z_read, 1)
                elif what == "pv":
                    if g:
                        sc.wait_ge(win_ready, 1)
                    sc.activation(pvb, src, ACT.Copy).then_inc(z_read, 1)
                elif what == "pg":
                    if g == 0:
                        sc.wait_ge(ot_ready, GROUPS - 1)
                    else:
                        sc.wait_ge(ot_ready, GROUPS)
                    sc.activation(sg[g][:], src, ACT.Silu).then_inc(z_read, 1)

            def mixed(i, k):
                sc.wait_ge(ot_ready, i + 1)
                sc.activation(act_a[:, MIX_HI + k, :], ot[:], ACT.Copy).then_inc(m_hi, 1)

            def beside(e):
                what = e[0]
                if what == "turn_iw":
                    sc.wait_ge(iw_split, 1)
                    sc.activation(sm[:, 3, 0:HX * TC], sm[:, 2, 0:HX * TC], ACT.Exp, scale=-1.0).then_inc(f_exp, 1)
                elif what == "turn_f":
                    sc.wait_ge(f_turned, 1)
                    sc.activation(frow[:, 0, :], gd[0:HX, 2, :], ACT.Copy)
                    sc.activation(frow[:, 1, :], gd[0:HX, 2, :], ACT.Copy, scale=-1.0).then_inc(f_rows, 1)
                elif what == "score":
                    _, n, c, h = e
                    if n >= 2:
                        sc.wait_ge(relu_used, n - 1)
                    sc.wait_ge(score_done, n + 1)
                    sc.activation(relu[n % 2][:, 0:(c + 1) * P], gd[:, n % 2, 0:(c + 1) * P], ACT.Relu).then_inc(relu_ready, 1)
                elif what == "turn_v":
                    g = e[1]
                    sc.wait_ge(v_turn_done, g + 1)
                    if g == 1:
                        sc.wait_ge(xT_norm, KD)
                    if g >= 2:
                        sc.wait_ge(pv_done, 2 * (g - 1))
                    sc.activation(flat(vt[g % 2]), gd[:, 2, :], ACT.Copy).then_inc(v_ready, 1)
                elif what == "s":
                    _, c, t = e
                    n = TC * t + c
                    sc.wait_ge(max_ready, n + 1)
                    if n >= TC:
                        sc.wait_ge(p_turned, n - TC + 1)
                    elif n == 2:
                        sc.wait_ge(relu_used, (TC - 1) * IDX_HEADS)
                    w = (c + 1) * P
                    sc.activation(prob[c][:, 0:w], gd[:, c % 2, 0:w], ACT.Exp, bias=small[:, 8 + c:9 + c], scale=-1.0,
                                  accum_out=small[:, 12 + c:13 + c]).then_inc(exp_ready, 1)
                elif what == "t":
                    _, c, t = e
                    n = TC * t + c
                    sc.wait_ge(p_turned, n + 1)
                    if t and c == 0:
                        sc.wait_ge(pv_done, t)
                    sc.activation(pT[:, 0:c + 1, c * P:c * P + P],
                                  gd[:, 2, 0:(c + 1) * P].rearrange("p (j q) -> p j q", q=P), ACT.Copy).then_inc(pT_ready, 1)
                elif what == "pv":
                    t = e[2]
                    if t % 2:
                        mixed(t // 2, W_ORDER[t // 2])

            for u in range(len(Z_UNITS)):
                n = N_Z + u + 1
                if u:
                    split(n, n)
                for m in range(4):
                    if m == 1 and u:
                        z_out(u - 1)
                    for e in plan.get((u, m), ()):
                        beside(e)
            z_out(len(Z_UNITS) - 1)
            for e in plan[(len(Z_UNITS), 0)]:
                beside(e)
            for b in range(2):
                mixed(GROUPS + b, b)
            for i in range(1, KD):
                split(N_W + i, N_W + i)
            for c in range(TC):
                sc.wait_ge(tile_done, c + 1)
                if c:
                    sc.wait_ge(osq, c)
                src = gb[:, 2 * c:2 * c + 2, :] if c < 2 else gd[:, 2 * c - 4:2 * c - 2, :]
                sc.activation(wk[:].rearrange("p (a n) -> p a n", a=2), src, ACT.Square,
                              accum_out=small[:, 16 + c:17 + c]).then_inc(osq, 1)

        @block.vector
        def _(dve):
            own = Steps(dve, dve_order)
            link = own.link

            def split(n, i, k=KD):
                if isinstance(n, int) and n in POOL_SPLITS:
                    return
                dve.wait_ge(hi_ready, n + 1)
                if isinstance(n, int) and n - 1 in POOL_SPLITS:
                    dve.wait_ge(split_ready, n)
                dve.tensor_tensor(wlo[:, i % 2, 0:k * P], raw[:, i % 4, 0:k * P],
                                  whi[:, i % 2, 0:k * P].bitcast(F32), ALU.subtract).then_inc(split_ready, 1)

            def log1p(e, s, t, out_):
                link(dve.tensor_scalar(s, e, 2.0, None, ALU.add))
                link(dve.reciprocal(s, s))
                link(dve.tensor_tensor(s, s, e, ALU.mult))
                link(dve.tensor_tensor(t, s, s, ALU.mult))
                link(dve.tensor_scalar(out_, t, 1.0 / 17, None, ALU.mult))
                for c in range(15, 1, -2):
                    link(dve.scalar_tensor_tensor(out_, out_, 1.0 / c, t, ALU.add, ALU.mult))
                link(dve.scalar_tensor_tensor(out_, out_, 1.0, s, ALU.add, ALU.mult))
                link(dve.tensor_scalar(out_, out_, 2.0, None, ALU.mult))

            def sum_positions(b=0, tmp=Yb):
                link(dve.tensor_tensor(tmp[:], bank(gd[:, b, :]), over(ident[:]), ALU.mult))
                link(dve.tensor_reduce(ss[:, b // 2, :], tmp[:], AX_X, ALU.add))

            def mean_square():
                return dve.tensor_scalar(rr[:, 0, :], ss[:, 0, :], 1.0 / D, EPS, ALU.mult, ALU.add)

            def normalise(norm, g0, b=1):
                dve.wait_ge(xrb_ready, norm + 1)

                def low_part(k):
                    dve.wait_ge(hn_hi, KD * norm + k + 1)
                    dve.tensor_tensor(act_a[:, H_LO + k, :], (qc, kc, vc)[k % 3][:], act_a[:, H_HI + k, :].bitcast(F32),
                                      ALU.subtract).then_inc(h_ready, 1)

                for k in range(KD):
                    if k >= 3:
                        dve.wait_ge(h_ready, KD * norm + k - 2)
                    dve.scalar_tensor_tensor((qc, kc, vc)[k % 3][:], xT[:, k, :], par[:, g0 + k:g0 + k + 1], gd[:, b, :],
                                             ALU.mult, ALU.mult).then_inc(hn_ready, 1)
                    if k:
                        low_part(k - 1)
                low_part(KD - 1)

            dve.memset(prow[:, :], 0.0).then_inc(prow_clear, 1)
            dve.wait_ge(par_turned, 1)
            dve.tensor_copy(par[:], gd[:, 1, 0:R_END]).then_inc(par_ready, 1)
            dve.wait_ge(par_ready, 1)
            link(dve.tensor_tensor(par[:, R_G2:R_G2 + KD], par[:, R_G2:R_G2 + KD], par[:, R_FIN_G:R_FIN_G + KD], ALU.mult))
            dve.tensor_scalar(par[:, R_G2:R_G2 + KD], par[:, R_G2:R_G2 + KD], float(D) ** 0.5, None, ALU.mult)
            dve.tensor_scalar(par[:, R_GDN_G:R_GDN_G + 1], par[:, R_GDN_G:R_GDN_G + 1], float(P) ** 0.5, None, ALU.mult)
            for b in range(3):
                dve.tensor_copy(htaps[:, :, 4 * b:4 * b + 4],
                                par[:, R_CONV_G:R_CONV_G + 96].rearrange("p (k b h) -> p h b k", k=4, b=3)[:, :, b, :])
            link(dve.tensor_copy(htaps[:, :, 12:15],
                                 par[:, R_CONV_A:R_CONV_A + 24].rearrange("p (k h) -> p h k", k=3)))
            dve.wait_ge(xsq_used, KD)
            sum_positions()
            mean_square().then_inc(xss_ready, 1)
            split(N_AB, N_AB)
            split(N_B, N_B)
            normalise(0, R_MIX_G)

            split(N_B + 1, N_B + 1)
            dve.wait_ge(ab_turned, 1)
            abt = bank(gd[:, 0, :])
            hct = lambda ap: ap.rearrange("p (h c) -> p h c", c=TC)
            link(dve.tensor_tensor(hct(sm[:, 1, 0:32]), abt[:, :, 0:HEADS].rearrange("p c h -> p h c"),
                                   rows8[:, HEADS:2 * HEADS].unsqueeze(2).to_broadcast([P, HEADS, TC]), ALU.add))
            link(dve.tensor_copy(hct(sm[:, 2, 32:64]), abt[:, :, HEADS:2 * HEADS].rearrange("p c h -> p h c")))
            link(dve.tensor_scalar(sm[:, 2, 0:32], sm[:, 1, 0:32], -1.0, None, ALU.mult))
            dve.tensor_tensor(sm[:, 2, 0:32], sm[:, 2, 0:32], sm[:, 1, 0:32], ALU.max).then_inc(abt_ready, 1)
            dve.wait_ge(ab_exp, 1)
            link(dve.tensor_scalar(sm[:, 3, 32:64], sm[:, 3, 32:64], 1.0, None, ALU.add))
            link(dve.reciprocal(sm[:, 11, 0:32], sm[:, 3, 32:64]))
            log1p(sm[:, 3, 0:32], sm[:, 5, 0:32], sm[:, 6, 0:32], sm[:, 7, 0:32])
            link(dve.tensor_scalar(sm[:, 1, 0:32], sm[:, 1, 0:32], 0.0, None, ALU.max))
            link(dve.tensor_tensor(sm[:, 1, 0:32], sm[:, 1, 0:32], sm[:, 7, 0:32], ALU.add))
            dve.scalar_tensor_tensor(hct(sm[:, 0, 0:32]), hct(sm[:, 1, 0:32]), -1.0,
                                     sm[:, 4, 0:HEADS].unsqueeze(2).to_broadcast([P, HEADS, TC]),
                                     ALU.mult, ALU.mult).then_inc(ab_g, 1)
            def decay_columns():
                dve.wait_ge(gcum_done, 1)
                link(dve.tensor_copy(sm[:, 5, 0:32], gd[:, 0, 0:32]))
                link(dve.tensor_copy(sm[:, 6, 0:32], gd[:, 0, P:P + 32]))
                dve.tensor_tensor(sm[:, 7, 0:32], sm[:, 6, 0:32], sm[:, 5, 0:32], ALU.subtract).then_inc(gcum_sb, 1)
                dve.wait_ge(cols_exp, 1)
                cols = lambda at: hcols[:, :, at:at + TC]
                dve.tensor_copy(cols(C_G), hct(sm[:, 5, 0:32]))
                dve.tensor_scalar(cols(C_NEGE), hct(sm[:, 8, 0:32]), -1.0, None, ALU.mult)
                dve.tensor_copy(cols(C_E), hct(sm[:, 8, 0:32]))
                dve.tensor_copy(cols(C_BETA), hct(sm[:, 11, 0:32]))
                dve.tensor_tensor(cols(C_BKD), hct(sm[:, 11, 0:32]), hct(sm[:, 10, 0:32]), ALU.mult)
                link(dve.tensor_copy(cols(C_EL), hct(sm[:, 9, 0:32])))

            def step(g, h):
                if g == 0:
                    for i, src in ((0, Ti), (1, Ui)):
                        dve.wait_ge(sq_ready, 2 * h + 1 + i)
                        dve.tensor_reduce(ss[:, i, :], src[:], AX_X, ALU.add).then_inc(ss_ready, 1)
                elif g == 1:
                    dve.wait_ge(gb_done, h + 1)
                    link(dve.tensor_tensor(dec[:], bank(gd[:, 3, :]), wide(hc[:, C_G:C_G + TC]), ALU.subtract))
                    dve.tensor_tensor(dec[:], dec[:], over(negT[:]), ALU.add).then_inc(arg_ready, 1)
                elif g == 2:
                    for i, dst in ((0, Kt), (1, Yb)):
                        dve.wait_ge(r_ready, 2 * h + 1 + i)
                        dve.tensor_tensor(dst[:], bank(gd[:, i, :]), wide(rr[:, 2 + i, :]), ALU.mult).then_inc(tok_ready, 1)
                elif g == 4:
                    dve.wait_ge(kk_done, 2 * h + 1)
                    dve.wait_ge(decb_ready, h + 1)
                    dve.tensor_tensor(LT[:], bank(gd[:, 2, :]), LT[:], ALU.mult).then_inc(lt_ready, 1)
                    dve.wait_ge(lt_ready, 2 * h + 1)
                    link(dve.tensor_tensor(Ui[:], LT[:], over(negm1[:]), ALU.mult))
                    dve.tensor_tensor(Ui[:], Ui[:], over(ident[:]), ALU.add).then_inc(u_ready, 1)
                    dve.wait_ge(kk_done, 2 * h + 2)
                    dve.tensor_tensor(AT[:], bank(gd[:, 3, :]), dec[:], ALU.mult).then_inc(lt_ready, 1)
                elif 7 <= g <= 18 and g % 2:
                    l = (g - 7) // 2
                    dve.wait_ge(y_done, 6 * h + l + 1)
                    dve.tensor_tensor(Yb[:], bank(gd[:, 0, :]), over(lev[:, l, :]), ALU.mult).then_inc(ym_ready, 1)
                elif 7 <= g <= 18:
                    l = (g - 8) // 2
                    dve.wait_ge(z_done, 6 * h + l + 1)
                    if l < 5:
                        tl = halved(flat(Ti), l)
                        dve.tensor_tensor(tl, tl, halved(gd[:, 1, :], l), ALU.subtract).then_inc(t_ready, 1)
                    ur = halved(flat(Ui), l, 1)
                    dve.tensor_tensor(ur, ur, halved(gd[:, 2, :], l, 1), ALU.subtract).then_inc(u_ready, 1)
                elif 19 <= g <= 29:
                    c = (g - 18) // 3
                    what = (g - 18) % 3
                    if what == 0:
                        dve.wait_ge(ks_done, 3 * h + c)
                        dve.scalar_tensor_tensor(Rr[:], gd[:, 0, 0:P], hc[:, C_NEGE + c:C_NEGE + c + 1], Vt[:, c, :],
                                                 ALU.mult, ALU.add).then_inc(rhs_ready, 1)
                    elif what == 2:
                        if c < TC - 1:
                            dve.wait_ge(su_done, 3 * h + c + 1)
                        if c == 0:
                            dve.tensor_copy(S[:], gd[:, 2, 0:P]).then_inc(s_ready, 1)
                            dve.wait_ge(av_done, 4 * h + c + 1)
                            dve.tensor_copy(ob[:, 0, :], gd[:, 1, 0:P]).then_inc(o_ready, 1)
                        else:
                            if c < TC - 1:
                                dve.scalar_tensor_tensor(S[:], S[:], hc[:, C_EL + c:C_EL + c + 1], gd[:, 2, 0:P],
                                                         ALU.mult, ALU.add).then_inc(s_ready, 1)
                            dve.wait_ge(av_done, 4 * h + c + 1)
                            dve.wait_ge(qs_ready, 3 * h + c)
                            dve.tensor_tensor(ob[:, c, :], gd[:, 1, 0:P], ob[:, c, :], ALU.add).then_inc(o_ready, 1)
                elif g == 30:
                    dve.wait_ge(osq_ready, h + 1)
                    dve.tensor_reduce(ss[:, 2, :], bank(yb), AX_X, ALU.add).then_inc(oss_ready, 1)
                elif g == 31:
                    dve.wait_ge(or_ready, h + 1)
                    dve.tensor_tensor(ob[:], ob[:], wide(rr[:, 5, :]), ALU.mult).then_inc(on_ready, 1)
                elif g == 32:
                    dve.wait_ge(o_turned, h + 1)
                    dve.wait_ge(z_ready, h + 1)
                    dve.scalar_tensor_tensor(yb, gd[:, 2, :], par[:, R_GDN_G:R_GDN_G + 1], zs[:],
                                             ALU.mult, ALU.mult).then_inc(yb_ready, 1)
                    dve.wait_ge(yb_hi, h + 1)
                    dve.tensor_tensor(act_b[:, ds(h + (YB_LO - SLOTS_A), 1), :].rearrange("p a t -> p (a t)"), yb,
                                      act_b[:, ds(h + (YB_HI - SLOTS_A), 1), :].rearrange("p a t -> p (a t)").bitcast(F32),
                                      ALU.subtract).then_inc(yb_lo, 1)

            def head_columns(h):
                if not (isinstance(h, int) and h == 0):
                    dve.wait_ge(o_ready, 4 * h)
                dve.tensor_copy(hc[:], hcols[:, ds(h, 1), :].rearrange("p a n -> p (a n)")).then_inc(hc_ready, 1)

            def filter_a(h):
                for a in range(1, 3):
                    link(dve.scalar_tensor_tensor(ca[:, a:T], cx[:, 0:T - a], hw[:, 14 - a:15 - a], ca[:, a:T],
                                                  ALU.mult, ALU.add))

            def after(h, s):
                if s < 3:
                    dve.wait_ge(tap_first, 3 * h + s + 1)
                    dst = (qc, kc, vc)[s]
                    for a in range(1, 4):
                        ins = dve.scalar_tensor_tensor(dst[:, a:T], gb[:, s, 0:T - a], hw[:, 4 * s + 3 - a:4 * s + 4 - a],
                                                       dst[:, a:T], ALU.mult, ALU.add)
                        if a < 3:
                            link(ins)
                    ins.then_inc(conv_done, 1)
                elif s == 4:
                    dve.wait_ge(unit_done, N_B + 8 * h + s + 1)
                    dve.wait_ge(cg_copied, h + 1)
                    dve.tensor_tensor(cx[:], gb[:, 0, :], cx[:], ALU.mult).then_inc(cg_ready, 1)
                    dve.wait_ge(cg_ready, h + 1)
                    link(dve.tensor_scalar(ca[:], cx[:], hw[:, 14:15], None, ALU.mult))
                elif s == 5:
                    dve.wait_ge(unit_done, N_B + 8 * h + s + 1)
                    dve.tensor_tensor(ca[:], ca[:], gb[:, 1, :], ALU.mult).then_inc(ya_ready, 1)
                    dve.wait_ge(ya_hi, h + 1)
                    dve.tensor_tensor(act_a[:, ds(h + YA_LO, 1), :].rearrange("p a t -> p (a t)"), ca[:],
                                      act_a[:, ds(h + YA_HI, 1), :].rearrange("p a t -> p (a t)").bitcast(F32),
                                      ALU.subtract).then_inc(ya_lo, 1)

            def head(h, peeled):
                dve.tensor_copy(hw[:], htaps[:, ds(h, 1), :].rearrange("p a n -> p (a n)")).then_inc(taps_ready, 1)
                for s in range(8):
                    late = s in (0, 3, 4) and not (peeled and s == 0)
                    if not late and not (peeled and s == 0):
                        split(N_B + 8 * h + s + 1, N_B + s + 1)
                    if peeled and s == 2:
                        decay_columns()
                    for m in range(4):
                        if late and m == 1:
                            split(N_B + 8 * h + s + 1, N_B + s + 1)
                        if s > 0 and s != 3 and m == (3 if s == 6 else 1):
                            after(h, s - 1)
                        if s == 5 and m == 3:
                            filter_a(h)
                        if s >= 3:
                            step((s - 3) * 4 + m, h)
                        elif not peeled:
                            step(20 + s * 4 + m, h - 1)
                        if s == 2 and m == 3:
                            head_columns(h)
                        if s == 3 and m == 2 and not peeled:
                            step(32, h - 1)
                        if s == 4 and m == 2:
                            after(h, 2)

            head(0, True)
            with dve.Fori(1, HEADS) as h:
                own.enter(h - 1, 11)
                head(h, False)
            own.leave(HEADS - 1)
            for j in range(KD):
                split(N_C1 + j + 1, N_C1 + j + 1)
                if j < 3:
                    for m in range(4):
                        step(20 + j * 4 + m, HEADS - 1)
                elif j == 3:
                    step(32, HEADS - 1)
                dve.wait_ge(ga_ready, HEADS)
                dve.wait_ge(unit_done, N_C1 + j + 1)
                dve.scalar_tensor_tensor(gate[:, j, :], gate[:, j, :], 1.0, gb[:, j % 4, :],
                                         ALU.add, ALU.mult).then_inc(out_read, 1)
            dve.wait_ge(out_read, KD)
            split(N_C2 + 1, N_C2 + 1)
            with dve.Fori(0, KD // 2) as i:
                for q in range(2):
                    split(N_C2 + 4 * i + 2 * q + 2, N_C2 + 2 * q + 2)
                    m = (qc, kc)[q]
                    dve.wait_ge(unit_done, N_C2 + 4 * i + 2 * q + 2)
                    dve.wait_ge(gb_tanh, 2 * i + q + 1)
                    dve.scalar_tensor_tensor(m[:], m[:], 1.0, gb[:, 2 * q + 1, :], ALU.add, ALU.mult).then_inc(out_read, 1)
                    dve.wait_ge(out_read, 2 * i + (R_C2 + q + 1))
                    dve.tensor_tensor(m[:], m[:], gate[:, ds(2 * i + q, 1), :].rearrange("p a t -> p (a t)"),
                                      ALU.add).then_inc(mix_ready, 1)
                    dve.wait_ge(mix_hi, 2 * i + q + 1)
                    dve.scalar_tensor_tensor(act_a[:, ds(2 * i + (MIX_LO + q), 1), :].rearrange("p a t -> p (a t)"), m[:], 0.5,
                                             act_a[:, ds(2 * i + (MIX_HI + q), 1), :].rearrange("p a t -> p (a t)").bitcast(F32),
                                             ALU.mult, ALU.subtract).then_inc(mix_lo, 1)
                    split(N_C2 + 4 * i + 2 * q + 3, N_C2 + 2 * q + 3)
            for j in range(KD):
                dve.wait_ge(unit_done, N_D + j + 1)
                dve.tensor_tensor(xT[:, j, :], xT[:, j, :], gb[:, j % 4, :], ALU.add).then_inc(out_read, 1)
                if j < KD - 1:
                    split(N_D + j + 2, N_D + j + 2)
            dve.wait_ge(xsq_used, KD + 1)
            sum_positions()
            mean_square().then_inc(xss_ready, 1)
            split(N_D + KD + 1, N_D + KD + 1)
            normalise(1, R_FFN_G)
            for f in range(2):
                with dve.Fori(0, FF_CUT[f] // 2) as i:
                    own.enter(i, 4)
                    for q in range(2):
                        for s in range(2):
                            j = 2 * i + (f * FF_CUT[0] + q)
                            dst = ((qc, kc), (vc, cx))[q][s]
                            dve.wait_ge(up_first, 2 * j + s + 1)
                            for a in range(1, 3):
                                at = R_CONV_F + (2 - a) * 2 * FB + s * FB + f * FF_CUT[0] + q
                                ins = dve.scalar_tensor_tensor(dst[:, a:T], gb[:, 2 * q + s, 0:T - a],
                                                               par[:, ds(2 * i + at, 1)],
                                                               dst[:, a:T], ALU.mult, ALU.add)
                                if a == 1:
                                    link(ins)
                            ins.then_inc((up_conv, out_read)[s], 1)
                            split(N_UP[f] + 4 * i + 2 * q + s + 2, N_UP[f] + 2 * q + s + 2)
                            if s == 1:
                                g = (qc, vc)[q]
                                dve.wait_ge(up_silu, j + 1)
                                dve.wait_ge(out_read, 2 * i + (R_UP[f] + q + 1))
                                dve.tensor_tensor(g[:], g[:], dst[:], ALU.mult).then_inc(up_ready, 1)
                                dve.wait_ge(up_hi, j + 1)
                                dve.tensor_tensor(act_b[:, ds(2 * i + (FF_LO - SLOTS_A + q), 1), :].rearrange("p a t -> p (a t)"), g[:],
                                                  act_a[:, ds(2 * i + (FF_HI + q), 1), :].rearrange("p a t -> p (a t)").bitcast(F32),
                                                  ALU.subtract).then_inc(up_lo, 1)
                own.leave(FF_CUT[f] // 2)
                def down(i, q, last=False):
                    split(N_DN[f] + 4 * i + 2 * q + 2, N_DN[f] + 2 * q + 2)
                    dve.wait_ge(unit_done, N_DN[f] + 4 * i + 2 * q + 2)
                    xj = xT[:, ds(2 * i + q, 1), :].rearrange("p a t -> p (a t)")
                    dve.tensor_tensor(xj, xj, gb[:, q, :], ALU.add).then_inc(out_read, 1)
                    if not last:
                        split(N_DN[f] + 4 * i + 2 * q + 3, N_DN[f] + 2 * q + 3)

                with dve.Fori(0, KD // 2 - f) as i:
                    for q in range(2):
                        down(i, q)
                if f:
                    for q in range(2):
                        down(KD // 2 - 1, q, last=q == 1)
            dve.wait_ge(xsq_used, KD + 2)
            sum_positions(0, Yb)
            link(mean_square())
            dve.wait_ge(xsq_used, KD + 3)
            sum_positions(2, Kt)
            dve.scalar_tensor_tensor(rr[:, 1, :], rr[:, 0, :], EPS * D, ss[:, 1, :], ALU.mult, ALU.add).then_inc(xss_ready, 1)
            split(N_Z + 1, N_Z + 1)
            normalise(2, R_G2, 3)

            dve.wait_ge(pads_ready, 1)

            def beside(e):
                what = e[0]
                if what == "turn_iw":
                    dve.wait_ge(iw_turned, 1)
                    t = bank(gd[:, 2, :])
                    col = lambda i, k: sm[:, i, 0:TC * k].rearrange("p (c h) -> p c h", h=k)
                    dve.tensor_scalar(col(8, IDX_HEADS), t[:, :, B_IW - B_IK:B_IW - B_IK + IDX_HEADS], float(IDX_HEADS) ** -0.5, None, ALU.mult)
                    link(dve.tensor_tensor(col(4, HX), t[:, :, P - HX:P],
                                           rows8[:, 16:16 + HX].unsqueeze(1).to_broadcast([P, TC, HX]), ALU.add))
                    n = HX * TC
                    link(dve.tensor_scalar(sm[:, 5, 0:n], sm[:, 4, 0:n], -1.0, None, ALU.mult))
                    dve.tensor_tensor(sm[:, 2, 0:n], sm[:, 4, 0:n], sm[:, 5, 0:n], ALU.max).then_inc(iw_split, 1)
                    dve.wait_ge(f_exp, 1)
                    log1p(sm[:, 3, 0:n], sm[:, 6, 0:n], sm[:, 7, 0:n], sm[:, 9, 0:n])
                    link(dve.tensor_scalar(sm[:, 5, 0:n], sm[:, 5, 0:n], 0.0, None, ALU.max))
                    link(dve.tensor_tensor(sm[:, 5, 0:n], sm[:, 5, 0:n], sm[:, 9, 0:n], ALU.add))
                    link(dve.tensor_scalar(sm[:, 0, 0:n], sm[:, 5, 0:n], -1.0, None, ALU.mult))
                    link(dve.memset(sm[:, 1, 0:HX], 0.0))
                    for c in range(1, TC):
                        ins = dve.tensor_tensor(sm[:, 1, c * HX:c * HX + HX], sm[:, 1, (c - 1) * HX:c * HX],
                                                sm[:, 0, (c - 1) * HX:c * HX], ALU.add)
                        if c < TC - 1:
                            link(ins)
                    ins.then_inc(f_ready, 1)
                elif what == "cum_f":
                    dve.wait_ge(f_cum, 1)
                    dve.tensor_copy(sm[:, 2, 0:HX * TC], gd[:, 3, 0:HX * TC]).then_inc(f_tok, 1)
                elif what == "score":
                    _, n, c, h = e
                    dve.wait_ge(relu_ready, n + 1)
                    w = (c + 1) * P
                    acc = selb[:, SEL_AT[c]:SEL_AT[c] + w]
                    f = sm[:, 8, c * IDX_HEADS + h:c * IDX_HEADS + h + 1]
                    if h == 0:
                        ins = dve.tensor_scalar(acc, relu[n % 2][:, 0:w], f, 0.0, ALU.mult, ALU.add)
                    else:
                        dve.wait_ge(relu_used, n)
                        ins = dve.scalar_tensor_tensor(acc, relu[n % 2][:, 0:w], f, acc, ALU.mult, ALU.add)
                    ins.then_inc(relu_used, 1)
                    if h == IDX_HEADS - 1:
                        dve.wait_ge(relu_used, n + 1)
                        link(dve.memset(selb[0:64, SEL_AT[c] + w - 64:SEL_AT[c] + w], FILL))
                elif what == "round":
                    _, r, c = e
                    v = selb[:, SEL_AT[c]:SEL_AT[c + 1]]
                    link(dve.max(small[:, 0:8], v))
                    link(dve.match_replace(v, small[:, 0:8], v, TAKEN))
                    if r == TOPK // 8 - 1:
                        dve.tensor_scalar(v, v, 0.5 * (FILL + TAKEN), NEG, ALU.is_gt, ALU.mult).then_inc(sel_ready, 1)
                elif what == "s":
                    _, c, t = e
                    n = TC * t + c
                    w = (c + 1) * P
                    if t < HX:
                        bias = cbias[:, T - w:T]
                    else:
                        bias = selb[:, SEL_AT[c]:SEL_AT[c + 1]]
                        if t == HX and c == 0:
                            dve.wait_ge(sel_ready, TC - 1)
                    dve.wait_ge(s_done, n + 1)
                    dve.tensor_tensor_reduce(gd[:, c % 2, 0:w], gd[:, c % 2, 0:w], bias, -1.0, -MASKED, ALU.add,
                                             ALU.min, small[:, 8 + c:9 + c]).then_inc(max_ready, 1)
                elif what == "weigh":
                    _, c, t = e
                    n = TC * t + c
                    dve.wait_ge(exp_ready, n + 1)
                    link(dve.reciprocal(small[:, 24 + c:25 + c], small[:, 12 + c:13 + c]))
                    p = prob[c][:, 0:(c + 1) * P]
                    dve.tensor_scalar(p, p, small[:, 24 + c:25 + c], None, ALU.mult).then_inc(p_ready, 1)
                elif what == "window":
                    next(pool_windows[e[1]])
                elif what == "pv":
                    t = e[2]
                    if t % 2:
                        g = t // 2
                        dve.wait_ge(pv_done, t + 1)
                        dve.wait_ge(z_read, G_READ[g])
                        if g:
                            dve.wait_ge(m_lo, g)
                        dve.tensor_tensor(ot[:], gd[:, 3, :], sg[g % 2][:], ALU.mult).then_inc(ot_ready, 1)
                        low(g, W_ORDER[g])

            def low(i, k):
                dve.wait_ge(m_hi, i + 1)
                dve.tensor_tensor(act_a[:, MIX_LO + k, :], ot[:], act_a[:, MIX_HI + k, :].bitcast(F32),
                                  ALU.subtract).then_inc(m_lo, 1)

            def z_out(u):
                what, g, _ = Z_UNITS[u]
                if what == "k":
                    dve.wait_ge(unit_done, N_Z + u + 1)
                    if g >= 2:
                        dve.wait_ge(s_done, TC * 2 * (g - 1))
                    for i in range(2):
                        r = slice(64 * i, 64 * i + 64)
                        if g in (3, 4):
                            for row in (64 - 64 * i, 96 - 64 * i):
                                dve.memset(ring(g, 2 + i)[row:row + 1, :], 0.0)
                        ins = dve.tensor_copy(ring(g, 2 + i)[r, :], gb[r, u % 4, :])
                    ins.then_inc(z_read_v, 1)

            def windows(g):
                dve.wait_ge(z_read, PV_READ[g])
                src, have = pvb, 1
                for dst in wins[g] * (1 + g):
                    link(dve.tensor_copy(dst[:, 0:have], src[:, 0:have]))
                    link(dve.tensor_tensor(dst[:, have:T], src[:, have:T], src[:, 0:T - have], ALU.add))
                    src, have = dst, 2 * have
                    yield
                res = wins[g][0]
                for rows, win in zip((slice(0, 64), slice(64, P)), wins[g]):
                    link(dve.scalar_tensor_tensor(res[rows, 16:T], win[rows, 16:T], small[rows, 32 + g:33 + g],
                                                  pvb[rows, 16:T], ALU.mult, ALU.subtract))
                    link(dve.tensor_tensor(res[rows, 0:16], win[rows, 0:16], small[rows, 48 + 16 * g:64 + 16 * g], ALU.mult))
                    ins = dve.tensor_tensor(res[rows, 0:16], res[rows, 0:16], pvb[rows, 0:16], ALU.subtract)
                    if rows.start == 0:
                        link(ins)
                        yield
                ins.then_inc(win_ready, 1)
                yield

            pool_windows = [windows(g) for g in range(2)]

            def pool_out(b):
                dve.wait_ge(pool_done, b + 1)
                dve.wait_ge(z_read, PG_READ[b])
                dve.wait_ge(m_lo, GROUPS + b)
                dve.scalar_tensor_tensor(ot[:], gb[:, (len(Z_UNITS) - 4 + b) % 4, :], par[:, R_PSC + b:R_PSC + b + 1], sg[b][:],
                                         ALU.mult, ALU.mult).then_inc(ot_ready, 1)
                low(GROUPS + b, b)

            for u in range(len(Z_UNITS)):
                if u:
                    split(N_Z + u + 1, N_Z + u + 1)
                for m in range(4):
                    if m == 1 and u:
                        z_out(u - 1)
                    for e in plan.get((u, m), ()):
                        beside(e)
            for e in plan[(len(Z_UNITS), 0)]:
                beside(e)
            for b in range(2):
                pool_out(b)
            for i in range(1, KD):
                split(N_W + i, N_W + i)
            dve.wait_ge(late_landed, 16 * 5)
            for c in range(TC):
                dve.wait_ge(orr, c + 1)
                src = gb[:, 2 * c:2 * c + 2, :] if c < 2 else gd[:, 2 * c - 4:2 * c - 2, :]
                dve.scalar_tensor_tensor(outs[:, c, :].rearrange("p (a n) -> p a n", a=2), src, small[:, 36 + c:37 + c],
                                         gfin[:].rearrange("p (a n) -> p a n", a=2), ALU.mult, ALU.mult).then_inc(outs_ready, 1)

        @block.gpsimd
        def _(pool):
            own = Steps(pool, pool_order)
            link = own.link

            def keep(out_, in_, pattern, base, mult, op=ALU.is_ge, fill=0.0):
                link(pool.affine_select(out=out_, in_=in_, pattern=pattern, compare_op=op, fill=fill,
                                        base=base, channel_multiplier=mult))

            link(pool.memset(ident[:], 0.0))
            pool.affine_select(out=ident[:], in_=ident[:], pattern=[[-1, P]], compare_op=ALU.not_equal, fill=1.0,
                               base=0, channel_multiplier=1).then_inc(masks_ready, 1)
            pool.memset(ones[:], 1.0).then_inc(masks_ready, 1)
            pool.wait_ge(masks_ready, 2)
            pool.memset(negT[:], 0.0)
            pool.memset(mhalf[:], -0.5)
            pool.memset(eps_one[:], EPS)
            link(pool.memset(eps_head[:], P * EPS))
            keep(triu[:], ones[:], [[1, P]], 0, -1)
            keep(tril[:], ones[:], [[-1, P]], 0, 1)
            keep(negT[:], negT[:], [[1, P]], 0, -1, fill=NEG)
            for l in range(6):
                w = 2 << l
                v = lev[:, l, :].rearrange("p (b j) -> p b j", j=w)
                keep(v, tril[:].rearrange("p (b j) -> p b j", j=w), [[w, P // w], [0, w]], w - 1, -1)
            for l in range(6):
                link(pool.tensor_tensor(lev[:, l, :], lev[:, l + 1, :] if l < 5 else tril[:], lev[:, l, :], ALU.subtract))
            keep(negm1[:].rearrange("p (b j) -> p b j", j=2), triu[:].rearrange("p (b j) -> p b j", j=2),
                 [[-2, P // 2], [0, 2]], 0, 1)
            pool.tensor_tensor(negm1[:], ident[:], negm1[:], ALU.subtract).then_inc(masks_ready, 1)

            def model_norm(norm):
                pool.wait_ge(xss_ready, norm + 1)
                pool.tensor_tensor(rr[:, 4, :], rr[:, 0, :], mhalf[:], ALU.pow).then_inc(xr_ready, 1)

            model_norm(0)

            def rsqrt_sum(dst, src, tmp, guard):
                link(pool.tensor_tensor(tmp, src, guard[:], ALU.add))
                return pool.tensor_tensor(dst, tmp, mhalf[:], ALU.pow)

            def head_a(h):
                pool.wait_ge(ss_ready, 2 * h + 1)
                rsqrt_sum(rr[:, 2, :], ss[:, 0, :], rr[:, 0, :], eps_one).then_inc(r_ready, 1)
                pool.wait_ge(ss_ready, 2 * h + 2)
                rsqrt_sum(rr[:, 3, :], ss[:, 1, :], rr[:, 1, :], eps_one).then_inc(r_ready, 1)
                pool.wait_ge(hc_ready, h + 1)
                pool.wait_ge(dec_ready, h + 1)
                pool.tensor_tensor(LT[:], dec[:], wide(hc[:, C_BETA:C_BETA + TC]), ALU.mult).then_inc(decb_ready, 1)

            def head_b(h):
                pool.wait_ge(oss_ready, h + 1)
                rsqrt_sum(rr[:, 5, :], ss[:, 2, :], rr[:, 6, :], eps_head).then_inc(or_ready, 1)

            head_a(0)
            with pool.Fori(1, HEADS) as h:
                own.enter(h - 1, 3)
                head_b(h - 1)
                head_a(h)
            own.leave(HEADS - 1)
            head_b(HEADS - 1)
            for j in range(1, KD - 1):
                pool.wait_ge(xsq_ready, KD + j + 1)
                if j >= 2:
                    pool.wait_ge(sq_added, j - 1)
                pool.tensor_tensor(zs[:], zs[:], (cx, ca)[j % 2][:], ALU.add).then_inc(sq_added, 1)
            model_norm(1)
            pool.wait_ge(out_read, R_D)
            for i in range(4):
                ins = pool.memset(ikz[i], 0.0)
            link(ins)
            for g in range(2):
                for i in range(2):
                    for what in (i, 2 + i):
                        r = 64 - 64 * i
                        link(pool.memset(ring(g, what)[r:r + 64, :], 0.0))
                        one = r if what < 2 else r + 32
                        link(pool.memset(ring(g, what)[one:one + 1, :], 1.0))
            for g in range(2):
                for i in range(2):
                    rows = slice(64 * i, 64 * i + 64)
                    window = 2 << (2 * g + i)
                    link(pool.memset(small[rows, 32 + g:33 + g], 1.0 / window))
                    for t in range(16):
                        ins = pool.memset(small[rows, 48 + 16 * g + t:49 + 16 * g + t], 1.0 / min(t + 1, window))
                    link(ins)
            for j in range(1, KD - 1):
                for i, (acc, squares) in enumerate(((zs[:], (cx, ca)[j % 2][:]), (flat(Kt), flat((KT, QT)[j % 2])))):
                    pool.wait_ge(xsq_ready, 2 * (KD + j) + i + 1)
                    if j >= 2:
                        pool.wait_ge(sq_added, KD - 2 + 2 * (j - 2) + i + 1)
                    pool.tensor_tensor(acc, acc, squares, ALU.add).then_inc(sq_added, 1)
            pool.wait_ge(xss_ready, 3)
            pool.tensor_tensor(rr[:, 5, :], rr[:, 1, :], mhalf[:], ALU.pow).then_inc(xr_ready, 1)
            pool.tensor_tensor(rr[:, 4, :], rr[:, 0, :], mhalf[:], ALU.pow).then_inc(xr_ready, 1)
            pool.memset(pw[:], 0.0).then_inc(late_clear, 1)
            link(pool.memset(cbias[:], 0.0))
            keep(cbias[:, T - P:T], cbias[:, T - P:T], [[-1, P]], 0, 1, fill=NEG)
            link(pool.memset(selb[:, 0:P], 0.0))
            pool.memset(selb[0:64, 64:P], NEG).then_inc(pads_ready, 1)
            def decay_rows(g):
                for i in range(2):
                    r = 64 - 64 * i
                    h = 2 * g + i
                    pool.dma_start(ring(g, i)[r + 32:r + 33, :], frow[h:h + 1, 0, :]).then_inc(f_put[g], 16)
                    pool.dma_start(ring(g, 2 + i)[r:r + 1, :], frow[h:h + 1, 1, :]).then_inc(f_put[g], 16)

            pool.wait_ge(f_rows, 1)
            decay_rows(0)
            decay_rows(1)
            pool.wait_ge(xrb_kept, 1)
            for k in range(KD):
                pool.wait_ge(hn_ready, 2 * KD + k + 1)
                link(pool.tensor_scalar(xT[:, k, :], xT[:, k, :], par[:, R_FIN_G + k:R_FIN_G + k + 1], None, ALU.mult))
                pool.tensor_tensor(xT[:, k, :], xT[:, k, :], flat(Vt), ALU.mult).then_inc(xT_norm, 1)
            pool.wait_ge(split_ready, POOL_SPLITS[0])
            for n in POOL_SPLITS:
                if n == POOL_SPLITS[3]:
                    pool.wait_ge(s_done, TC * 2)
                    decay_rows(2)
                pool.wait_ge(hi_ready, n + 1)
                pool.tensor_tensor(wlo[:, n % 2, :], raw[:, n % 4, :], whi[:, n % 2, :].bitcast(F32),
                                   ALU.subtract).then_inc(split_ready, 1)
            for c in range(TC):
                pool.wait_ge(osq, c + 1)
                link(pool.tensor_scalar(small[:, 40 + c:41 + c], small[:, 16 + c:17 + c], 1.0 / D, EPS, ALU.mult, ALU.add))
                pool.tensor_tensor(small[:, 36 + c:37 + c], small[:, 40 + c:41 + c], mhalf[:, 0:1], ALU.pow).then_inc(orr, 1)


_INS = ["x", "norm_mix_g", "w_in", "conv_a_w", "gdn_conv_w", "gdn_A_log", "gdn_dt_bias", "gdn_norm_g", "w_a_out",
        "w_b_out", "w_o", "norm_ffn_g", "w_up", "ffn_conv_w", "w_down", "norm_final_g", "w_in_2", "norm_g_2",
        "pool_w_2", "pool_scale_2", "fox_bf_2", "w_out_2", "final_g_2"]


def kernel(**inputs):
    import numpy as _np
    import concourse.bacc as _bacc
    from concourse import mybir as _mybir
    from concourse.bass_utils import run_bass_kernel_spmd as _run

    nc = _bacc.Bacc("TRN2", target_bir_lowering=False, num_devices=1)
    arrays, args = {}, []
    for name in _INS:
        a = _np.ascontiguousarray(inputs[name])
        arrays[f"in_{name}_dram"] = a
        args.append(nc.dram_tensor(f"in_{name}_dram", a.shape, _mybir.dt.from_np(a.dtype), kind="ExternalInput").ap())
    args.append(nc.dram_tensor("out_0_dram", (1, T, D), F32, kind="ExternalOutput").ap())
    hybrid_block_kernel(nc, *args)
    r = _run(nc, [arrays], core_ids=[0])
    return r.results[0]["out_0_dram"]
```
